# Optimizing a Trainium2 kernel written in Bass

```python
import jax, jax.numpy as jnp
from jax import lax
import numpy as np
import math

D_MODEL = 1024
BATCH = 1
SEQ = 512
DEPTH = 2

CHUNK = 64
N_MIXERS = 2
N_A_LAYERS = (DEPTH + 1) // 2
N_B_LAYERS = DEPTH // 2

SGU_CHUNK = 2 * CHUNK
SGU_HALF = D_MODEL
SGU_GROUPS = 16
SGU_GROUP_DIM = SGU_HALF // SGU_GROUPS

RWKV_HEAD_DIM = 64
RWKV_HEADS = D_MODEL // RWKV_HEAD_DIM
DECAY_LORA = 64
AAA_LORA = 64
GATE_LORA = 160
GN_EPS = 64e-5
N_SHIFT_MIX = 6

FFN_DIM = 2816
CONV_WIDTH = 3
RMS_EPS = 1e-6


def rms_norm(x, g):
    xf = x.astype(jnp.float32)
    y = xf * lax.rsqrt(jnp.mean(xf * xf, axis=-1, keepdims=True) + RMS_EPS)
    return (y * g.astype(jnp.float32)).astype(x.dtype)

def sgu_mixer(h, w_in, b_in, g_v, w_s, b_s, w_out):
    B, S, _ = h.shape
    z = jax.nn.gelu(h @ w_in + b_in, approximate=False)
    u, v = jnp.split(z, 2, axis=-1)
    v = rms_norm(v, g_v)
    n_blk = S // SGU_CHUNK
    v = v.reshape(B, n_blk, SGU_CHUNK, SGU_GROUPS, SGU_GROUP_DIM)
    causal = jnp.tril(jnp.ones((SGU_CHUNK, SGU_CHUNK), dtype=bool))
    w_causal = jnp.where(causal[None], w_s, 0)
    v = jnp.einsum('gts,bnsgc->bntgc', w_causal, v) + b_s.T[None, None, :, :, None]
    y = u * v.reshape(B, S, SGU_HALF)
    return y @ w_out

def token_shift(x):
    return jnp.pad(x, ((0, 0), (1, 0), (0, 0)))[:, :-1]

def wkv7_scan(r, w, k, v, a, b):
    B, S, H, N = r.shape

    def step(state, inp):
        r_t, w_t, k_t, v_t, a_t, b_t = inp
        sa = jnp.einsum('bhvk,bhk->bhv', state, a_t)
        state = (state * w_t[:, :, None, :]
                 + sa[..., None] * b_t[:, :, None, :]
                 + v_t[..., None] * k_t[:, :, None, :])
        y_t = jnp.einsum('bhvk,bhk->bhv', state, r_t)
        return state, y_t

    xs = tuple(jnp.swapaxes(t, 0, 1) for t in (r, w, k, v, a, b))
    s0 = jnp.zeros((B, H, N, N), jnp.float32)
    _, ys = lax.scan(step, s0, xs)
    return jnp.swapaxes(ys, 0, 1)

def rwkv7_mixer(h, mu, w_r, w_k, w_v, w_o, w0, w1, w2, a0, a1, a2,
                g1, g2, k_k, k_a, r_k, ln_w, ln_b):
    B, S, D = h.shape
    H, N = RWKV_HEADS, RWKV_HEAD_DIM
    f32 = jnp.float32
    xx = token_shift(h) - h
    xr = h + xx * mu[0]
    xw = h + xx * mu[1]
    xk = h + xx * mu[2]
    xv = h + xx * mu[3]
    xa = h + xx * mu[4]
    xg = h + xx * mu[5]
    r = xr @ w_r
    k = xk @ w_k
    v = xv @ w_v
    w = -jax.nn.softplus(-(w0 + jnp.tanh(xw @ w1) @ w2)) - 0.5
    a = jax.nn.sigmoid(a0 + (xa @ a1) @ a2)
    g = jax.nn.sigmoid(xg @ g1) @ g2

    def heads(t):
        return t.reshape(B, S, H, N).astype(f32)

    kk = heads(k * k_k)
    kk = kk * lax.rsqrt(jnp.maximum(jnp.sum(kk * kk, -1, keepdims=True), 1e-24))
    k = k * (1 + (a - 1) * k_a)
    r_h, k_h, v_h, a_h = heads(r), heads(k), heads(v), heads(a)
    decay = jnp.exp(-jnp.exp(heads(w)))
    y = wkv7_scan(r_h, decay, k_h, v_h, -kk, kk * a_h)
    mean = jnp.mean(y, -1, keepdims=True)
    var = jnp.mean(jnp.square(y - mean), -1, keepdims=True)
    y = ((y - mean) * lax.rsqrt(var + GN_EPS)).reshape(B, S, D)
    y = y * ln_w.astype(f32) + ln_b.astype(f32)
    bonus = jnp.sum(r_h * k_h * r_k.astype(f32), -1, keepdims=True) * v_h
    y = (y + bonus.reshape(B, S, D)).astype(h.dtype)
    return (y * g) @ w_o

def conv_ffn(h, w_up, conv_w, conv_b, w_down):
    S = h.shape[1]
    z = h @ w_up
    zp = jnp.pad(z, ((0, 0), (CONV_WIDTH - 1, 0), (0, 0)))
    z = sum(zp[:, j:j + S] * conv_w[j] for j in range(CONV_WIDTH)) + conv_b
    gate, val = jnp.split(z, 2, axis=-1)
    return (jax.nn.silu(gate) * val) @ w_down

def first_inputs(seed: int = 0) -> dict:
    key = jax.random.key(seed)
    ks = iter(jax.random.split(key, 40))
    f32 = jnp.float32

    def nrm(shape, scale):
        return jax.random.normal(next(ks), shape, f32) * scale

    def gain(shape):
        return 1.0 + 0.05 * jax.random.normal(next(ks), shape, f32)

    D, NA, NB = D_MODEL, N_A_LAYERS, N_B_LAYERS
    H2, F2 = 2 * SGU_HALF, 2 * FFN_DIM
    return {
        "x": nrm((BATCH, SEQ, D), 1.0),
        "norm_mix_g": gain((DEPTH, D)),
        "norm_ffn_g": gain((DEPTH, D)),
        "norm_final_g": gain((D,)),
        "sgu_w_in": nrm((NA, D, H2), D ** -0.5),
        "sgu_b_in": nrm((NA, H2), 0.02),
        "sgu_g_v": gain((NA, SGU_HALF)),
        "sgu_w_s": nrm((NA, SGU_GROUPS, SGU_CHUNK, SGU_CHUNK), 0.5 * SGU_CHUNK ** -0.5),
        "sgu_b_s": gain((NA, SGU_GROUPS, SGU_CHUNK)),
        "sgu_w_out": nrm((NA, SGU_HALF, D), SGU_HALF ** -0.5),
        "rwkv_mu": jax.random.uniform(next(ks), (NB, N_SHIFT_MIX, D), f32),
        "rwkv_w_r": nrm((NB, D, D), D ** -0.5),
        "rwkv_w_k": nrm((NB, D, D), D ** -0.5),
        "rwkv_w_v": nrm((NB, D, D), D ** -0.5),
        "rwkv_w_o": nrm((NB, D, D), D ** -0.5),
        "rwkv_w0": jax.random.uniform(next(ks), (NB, D), f32, minval=-6.0, maxval=-1.0),
        "rwkv_w1": nrm((NB, D, DECAY_LORA), 0.1 * D ** -0.5),
        "rwkv_w2": nrm((NB, DECAY_LORA, D), 0.1 * DECAY_LORA ** -0.5),
        "rwkv_a0": nrm((NB, D), 0.1),
        "rwkv_a1": nrm((NB, D, AAA_LORA), 0.1 * D ** -0.5),
        "rwkv_a2": nrm((NB, AAA_LORA, D), 0.1 * AAA_LORA ** -0.5),
        "rwkv_g1": nrm((NB, D, GATE_LORA), D ** -0.5),
        "rwkv_g2": nrm((NB, GATE_LORA, D), GATE_LORA ** -0.5),
        "rwkv_k_k": 0.85 + 0.05 * jax.random.normal(next(ks), (NB, D), f32),
        "rwkv_k_a": gain((NB, D)),
        "rwkv_r_k": nrm((NB, RWKV_HEADS, RWKV_HEAD_DIM), 0.1),
        "rwkv_ln_w": gain((NB, D)),
        "rwkv_ln_b": nrm((NB, D), 0.02),
        "ffn_w_up": nrm((DEPTH, D, F2), D ** -0.5),
        "ffn_conv_w": nrm((DEPTH, CONV_WIDTH, F2), CONV_WIDTH ** -0.5),
        "ffn_conv_b": nrm((DEPTH, F2), 0.02),
        "ffn_w_down": nrm((DEPTH, FFN_DIM, D), FFN_DIM ** -0.5),
    }

def first_block(x, norm_mix_g, norm_ffn_g, norm_final_g,
              sgu_w_in, sgu_b_in, sgu_g_v, sgu_w_s, sgu_b_s, sgu_w_out,
              rwkv_mu, rwkv_w_r, rwkv_w_k, rwkv_w_v, rwkv_w_o,
              rwkv_w0, rwkv_w1, rwkv_w2, rwkv_a0, rwkv_a1, rwkv_a2,
              rwkv_g1, rwkv_g2, rwkv_k_k, rwkv_k_a, rwkv_r_k, rwkv_ln_w, rwkv_ln_b,
              ffn_w_up, ffn_conv_w, ffn_conv_b, ffn_w_down):
    h = x
    for i in range(DEPTH):
        hn = rms_norm(h, norm_mix_g[i])
        j = i // N_MIXERS
        if i % N_MIXERS == 0:
            h = h + sgu_mixer(hn, sgu_w_in[j], sgu_b_in[j], sgu_g_v[j],
                              sgu_w_s[j], sgu_b_s[j], sgu_w_out[j])
        else:
            h = h + rwkv7_mixer(hn, rwkv_mu[j], rwkv_w_r[j], rwkv_w_k[j], rwkv_w_v[j], rwkv_w_o[j],
                                rwkv_w0[j], rwkv_w1[j], rwkv_w2[j],
                                rwkv_a0[j], rwkv_a1[j], rwkv_a2[j],
                                rwkv_g1[j], rwkv_g2[j], rwkv_k_k[j], rwkv_k_a[j], rwkv_r_k[j],
                                rwkv_ln_w[j], rwkv_ln_b[j])
        h = h + conv_ffn(rms_norm(h, norm_ffn_g[i]), ffn_w_up[i], ffn_conv_w[i],
                         ffn_conv_b[i], ffn_w_down[i])
    return rms_norm(h, norm_final_g)


GRID_W = 64
NORM_EPS = 1e-6

NA_HEADS = 8
NA_HEAD_DIM = 64
NA_WIDTH = NA_HEADS * NA_HEAD_DIM
NA_KH_MAX = 8
NA_KW = 16

SSD_D_INNER = D_MODEL
SSD_HEAD_DIM = 64
SSD_HEADS = SSD_D_INNER // SSD_HEAD_DIM
SSD_GROUPS = 4
SSD_STATE = 128
SSD_CONV = 4
SSD_CHUNK = 128
SSD_CONV_DIM = SSD_D_INNER + 2 * SSD_GROUPS * SSD_STATE
DT_MIN = 0.001
DT_MAX = 0.1

EVEN_SPLITS = [NA_WIDTH, 2 * NA_WIDTH, 3 * NA_WIDTH,
               3 * NA_WIDTH + SSD_D_INNER,
               3 * NA_WIDTH + SSD_D_INNER + SSD_CONV_DIM]
EVEN_IN_WIDTH = 3 * NA_WIDTH + SSD_D_INNER + SSD_CONV_DIM + 2 * SSD_HEADS
EVEN_MIX_WIDTH = NA_WIDTH + SSD_D_INNER

GQA_HEADS = 16
GQA_KV_HEADS = 4
GQA_HEAD_DIM = 64
GQA_Q_WIDTH = GQA_HEADS * GQA_HEAD_DIM
GQA_KV_WIDTH = GQA_KV_HEADS * GQA_HEAD_DIM
ODD_IN_WIDTH = GQA_Q_WIDTH + 2 * GQA_KV_WIDTH
ROPE_THETA = 10000.0
Q_BLOCK = 128

FFN_HIDDEN = -(-8 * D_MODEL // (3 * 256)) * 256

N_EVEN = (DEPTH + 1) // 2
N_ODD = DEPTH // 2


def rms_norm_2(x, g):
    xf = x.astype(jnp.float32)
    y = xf * lax.rsqrt(jnp.mean(xf * xf, axis=-1, keepdims=True) + NORM_EPS)
    return (y * g.astype(jnp.float32)).astype(x.dtype)

def neighbourhood_attention(q, k, v, rpb):
    B, S, H, Dh = q.shape
    rows = S // GRID_W
    kh = min(NA_KH_MAX, rows)
    qg = q.reshape(B, rows, GRID_W, H, Dh)
    kg = k.reshape(B, rows, GRID_W, H, Dh)
    vg = v.reshape(B, rows, GRID_W, H, Dh)
    r = jnp.arange(rows)
    row_start = jnp.clip(r - kh // 2, 0, rows - kh)
    key_rows = row_start[:, None] + jnp.arange(kh)[None, :]
    k_blk = kg[:, key_rows]
    v_blk = vg[:, key_rows]
    c = jnp.arange(GRID_W)
    col_start = jnp.clip(c - NA_KW // 2, 0, GRID_W - NA_KW)
    in_win = (c[None, :] >= col_start[:, None]) & (c[None, :] < col_start[:, None] + NA_KW)
    dy = key_rows - r[:, None] + (NA_KH_MAX - 1)
    dx = jnp.clip(c[None, :] - c[:, None], -(NA_KW - 1), NA_KW - 1) + (NA_KW - 1)
    bias = rpb.astype(jnp.float32)[:, dy[:, None, :, None], dx[None, :, None, :]]
    scale = Dh ** -0.5
    s = jnp.einsum('brchd,brjkhd->bhrcjk', qg, k_blk).astype(jnp.float32) * scale + bias[None]
    s = jnp.where(in_win[:, None, :], s, -jnp.inf)
    p = jax.nn.softmax(s.reshape(B, H, rows, GRID_W, kh * GRID_W), axis=-1)
    p = p.reshape(B, H, rows, GRID_W, kh, GRID_W).astype(v.dtype)
    o = jnp.einsum('bhrcjk,brjkhd->brchd', p, v_blk)
    return o.reshape(B, S, H * Dh)

def centred_depthwise_conv(x, w, b):
    K, C = w.shape
    left = K // 2
    xp = jnp.pad(x, ((0, 0), (left, K - 1 - left), (0, 0)))
    y = lax.conv_general_dilated(xp, w[:, None, :].astype(x.dtype), window_strides=(1,), padding='VALID',
                                 dimension_numbers=('NWC', 'WIO', 'NWC'), feature_group_count=C)
    return y + b.astype(x.dtype)

def ssd_scan(x, dt, A, Bm, Cm):
    out_dtype = x.dtype
    Bsz, S, H, P = x.shape
    G, N = Bm.shape[2], Bm.shape[3]
    R = H // G
    L = SSD_CHUNK
    nc = S // L
    f32 = jnp.float32
    x = x.astype(f32); dt = dt.astype(f32)
    xc = (x * dt[..., None]).reshape(Bsz, nc, L, G, R, P)
    Bc = Bm.astype(f32).reshape(Bsz, nc, L, G, N)
    Cc = Cm.astype(f32).reshape(Bsz, nc, L, G, N)
    a = (dt * A.astype(f32)).reshape(Bsz, nc, L, G, R)
    a_cum = jnp.moveaxis(jnp.cumsum(a, axis=2), 2, -1)
    seg = a_cum[..., :, None] - a_cum[..., None, :]
    lower = jnp.tril(jnp.ones((L, L), dtype=bool))
    decay = jnp.exp(jnp.where(lower, seg, -jnp.inf))
    cb = jnp.einsum('bclgn,bcsgn->bcgls', Cc, Bc)
    y_diag = jnp.einsum('bcgls,bcgrls,bcsgrp->bclgrp', cb, decay, xc)
    decay_to_end = jnp.exp(a_cum[..., -1:] - a_cum)
    states = jnp.einsum('bcsgn,bcgrs,bcsgrp->bcgrpn', Bc, decay_to_end, xc)
    chunk_decay = jnp.exp(a_cum[..., -1])

    def step(h, inp):
        s_c, d_c = inp
        return h * d_c[..., None, None] + s_c, h

    h0 = jnp.zeros((Bsz, G, R, P, N), f32)
    _, h_prev = lax.scan(step, h0, (jnp.moveaxis(states, 1, 0), jnp.moveaxis(chunk_decay, 1, 0)))
    h_prev = jnp.moveaxis(h_prev, 0, 1)
    y_off = jnp.einsum('bclgn,bcgrpn,bcgrl->bclgrp', Cc, h_prev, jnp.exp(a_cum))
    return (y_diag + y_off).reshape(Bsz, S, H, P).astype(out_dtype)

def gated_group_rms_norm(y, z, g):
    Bsz, S, Dn = y.shape
    h = (y * jax.nn.silu(z)).astype(jnp.float32).reshape(Bsz, S, SSD_GROUPS, Dn // SSD_GROUPS)
    h = h * lax.rsqrt(jnp.mean(h * h, axis=-1, keepdims=True) + NORM_EPS)
    return (h.reshape(Bsz, S, Dn) * g.astype(jnp.float32)).astype(y.dtype)

def even_mixer(x, mix_norm, w_in, na_q_norm, na_k_norm, na_rel_bias, conv_w, conv_b,
               dt_bias, A_log, D_skip, out_norm, w_out):
    Bsz, S, _ = x.shape
    proj = rms_norm_2(x, mix_norm) @ w_in
    q, k, v, z, xbc, dt_raw = jnp.split(proj, EVEN_SPLITS, axis=-1)
    q = rms_norm_2(q.reshape(Bsz, S, NA_HEADS, NA_HEAD_DIM), na_q_norm)
    k = rms_norm_2(k.reshape(Bsz, S, NA_HEADS, NA_HEAD_DIM), na_k_norm)
    v = v.reshape(Bsz, S, NA_HEADS, NA_HEAD_DIM)
    na_out = neighbourhood_attention(q, k, v, na_rel_bias)
    xbc = jax.nn.silu(centred_depthwise_conv(xbc, conv_w, conv_b))
    xs, bm, cm = jnp.split(xbc, [SSD_D_INNER, SSD_D_INNER + SSD_GROUPS * SSD_STATE], axis=-1)
    xs = xs.reshape(Bsz, S, SSD_HEADS, SSD_HEAD_DIM)
    bm = bm.reshape(Bsz, S, SSD_GROUPS, SSD_STATE)
    cm = cm.reshape(Bsz, S, SSD_GROUPS, SSD_STATE)
    dt = jax.nn.softplus(dt_raw.astype(jnp.float32).reshape(Bsz, S, 2, SSD_HEADS)
                         + dt_bias.astype(jnp.float32))
    A = -jnp.exp(A_log.astype(jnp.float32))
    y_fwd = ssd_scan(xs, dt[:, :, 0], A[0], bm, cm)
    y_bwd = jnp.flip(ssd_scan(jnp.flip(xs, 1), jnp.flip(dt[:, :, 1], 1), A[1],
                              jnp.flip(bm, 1), jnp.flip(cm, 1)), 1)
    y = y_fwd + y_bwd + D_skip.astype(xs.dtype)[:, None] * xs
    ssd_out = gated_group_rms_norm(y.reshape(Bsz, S, SSD_D_INNER), z, out_norm)
    return jnp.concatenate([na_out, ssd_out], axis=-1) @ w_out

def axial_rope_tables(S):
    t = jnp.arange(S)
    row = (t // GRID_W).astype(jnp.float32)
    col = (t % GRID_W).astype(jnp.float32)
    axis_dims = GQA_HEAD_DIM // 2
    freqs = ROPE_THETA ** (-jnp.arange(0, axis_dims, 2, dtype=jnp.float32) / axis_dims)
    ang = jnp.concatenate([row[:, None] * freqs, col[:, None] * freqs], axis=-1)
    return jnp.cos(ang), jnp.sin(ang)

def apply_rope(x, cos, sin):
    xf = x.astype(jnp.float32).reshape(*x.shape[:-1], x.shape[-1] // 2, 2)
    x0, x1 = xf[..., 0], xf[..., 1]
    c = cos[None, :, None, :]
    s = sin[None, :, None, :]
    out = jnp.stack([x0 * c - x1 * s, x0 * s + x1 * c], axis=-1)
    return out.reshape(x.shape).astype(x.dtype)

def gqa_block_attention(q, k, v):
    Bsz, S, H, Dh = q.shape
    KV = k.shape[2]
    rep = H // KV
    nb = S // Q_BLOCK
    qb = jnp.moveaxis(q.reshape(Bsz, nb, Q_BLOCK, KV, rep, Dh), 1, 0)
    scale = Dh ** -0.5

    def one_block(q_blk):
        s = jnp.einsum('bqgrd,bkgd->bgrqk', q_blk, k).astype(jnp.float32) * scale
        p = jax.nn.softmax(s, axis=-1).astype(v.dtype)
        return jnp.einsum('bgrqk,bkgd->bqgrd', p, v)

    o = lax.map(one_block, qb)
    return jnp.moveaxis(o, 0, 1).reshape(Bsz, S, H * Dh)

def odd_mixer(x, mix_norm, w_qkv, q_norm, k_norm, w_out):
    Bsz, S, _ = x.shape
    proj = rms_norm_2(x, mix_norm) @ w_qkv
    q, k, v = jnp.split(proj, [GQA_Q_WIDTH, GQA_Q_WIDTH + GQA_KV_WIDTH], axis=-1)
    q = rms_norm_2(q.reshape(Bsz, S, GQA_HEADS, GQA_HEAD_DIM), q_norm)
    k = rms_norm_2(k.reshape(Bsz, S, GQA_KV_HEADS, GQA_HEAD_DIM), k_norm)
    v = v.reshape(Bsz, S, GQA_KV_HEADS, GQA_HEAD_DIM)
    cos, sin = axial_rope_tables(S)
    q = apply_rope(q, cos, sin)
    k = apply_rope(k, cos, sin)
    return gqa_block_attention(q, k, v) @ w_out

def swiglu_ffn(x, norm_g, w13, w2):
    g, u = jnp.split(rms_norm_2(x, norm_g) @ w13, 2, axis=-1)
    return (jax.nn.silu(g) * u) @ w2

def second_inputs(seed: int = 0) -> dict:
    key = jax.random.key(seed)
    ks = jax.random.split(key, 24)
    f32 = jnp.float32

    def normal(k, shape, scale):
        return jax.random.normal(k, shape, f32) * scale

    def gain(k, shape):
        return 1.0 + 0.02 * jax.random.normal(k, shape, f32)

    dt0 = jnp.exp(jax.random.uniform(ks[10], (N_EVEN, 2, SSD_HEADS), f32)
                  * (math.log(DT_MAX) - math.log(DT_MIN)) + math.log(DT_MIN))
    dt_bias = dt0 + jnp.log(-jnp.expm1(-dt0))
    A_log = jnp.log(jax.random.uniform(ks[11], (N_EVEN, 2, SSD_HEADS), f32, 1.0, 16.0))
    return {
        "x": jax.random.normal(ks[0], (BATCH, SEQ, D_MODEL), f32),
        "even_mix_norm": gain(ks[1], (N_EVEN, D_MODEL)),
        "even_w_in": normal(ks[2], (N_EVEN, D_MODEL, EVEN_IN_WIDTH), D_MODEL ** -0.5),
        "na_q_norm": gain(ks[3], (N_EVEN, NA_HEAD_DIM)),
        "na_k_norm": gain(ks[4], (N_EVEN, NA_HEAD_DIM)),
        "na_rel_bias": normal(ks[5], (N_EVEN, NA_HEADS, 2 * NA_KH_MAX - 1, 2 * NA_KW - 1), 0.05),
        "ssd_conv_w": normal(ks[6], (N_EVEN, SSD_CONV, SSD_CONV_DIM), SSD_CONV ** -0.5),
        "ssd_conv_b": normal(ks[7], (N_EVEN, SSD_CONV_DIM), 0.01),
        "ssd_dt_bias": dt_bias,
        "ssd_A_log": A_log,
        "ssd_D": gain(ks[8], (N_EVEN, SSD_HEADS)),
        "ssd_out_norm": gain(ks[9], (N_EVEN, SSD_D_INNER)),
        "even_w_out": normal(ks[12], (N_EVEN, EVEN_MIX_WIDTH, D_MODEL), EVEN_MIX_WIDTH ** -0.5),
        "odd_mix_norm": gain(ks[13], (N_ODD, D_MODEL)),
        "odd_w_qkv": normal(ks[14], (N_ODD, D_MODEL, ODD_IN_WIDTH), D_MODEL ** -0.5),
        "gqa_q_norm": gain(ks[15], (N_ODD, GQA_HEAD_DIM)),
        "gqa_k_norm": gain(ks[16], (N_ODD, GQA_HEAD_DIM)),
        "odd_w_out": normal(ks[17], (N_ODD, GQA_Q_WIDTH, D_MODEL), GQA_Q_WIDTH ** -0.5),
        "ffn_norm": gain(ks[18], (DEPTH, D_MODEL)),
        "ffn_w13": normal(ks[19], (DEPTH, D_MODEL, 2 * FFN_HIDDEN), D_MODEL ** -0.5),
        "ffn_w2": normal(ks[20], (DEPTH, FFN_HIDDEN, D_MODEL), FFN_HIDDEN ** -0.5),
    }

def second_block(x, even_mix_norm, even_w_in, na_q_norm, na_k_norm, na_rel_bias, ssd_conv_w, ssd_conv_b,
              ssd_dt_bias, ssd_A_log, ssd_D, ssd_out_norm, even_w_out, odd_mix_norm, odd_w_qkv,
              gqa_q_norm, gqa_k_norm, odd_w_out, ffn_norm, ffn_w13, ffn_w2):
    for layer in range(DEPTH):
        i = layer // 2
        if layer % 2 == 0:
            x = x + even_mixer(x, even_mix_norm[i], even_w_in[i], na_q_norm[i], na_k_norm[i],
                               na_rel_bias[i], ssd_conv_w[i], ssd_conv_b[i], ssd_dt_bias[i],
                               ssd_A_log[i], ssd_D[i], ssd_out_norm[i], even_w_out[i])
        else:
            x = x + odd_mixer(x, odd_mix_norm[i], odd_w_qkv[i], gqa_q_norm[i], gqa_k_norm[i], odd_w_out[i])
        x = x + swiglu_ffn(x, ffn_norm[layer], ffn_w13[layer], ffn_w2[layer])
    return x


def setup_inputs(seed=0):
    out = dict(first_inputs(seed))
    for name, value in second_inputs(seed + 1).items():
        if name != "x":
            out[name + "_2"] = value
    return out


def reference(
    x, norm_mix_g, norm_ffn_g, norm_final_g, sgu_w_in, sgu_b_in, sgu_g_v, sgu_w_s, sgu_b_s,
    sgu_w_out, rwkv_mu, rwkv_w_r, rwkv_w_k, rwkv_w_v, rwkv_w_o, rwkv_w0, rwkv_w1, rwkv_w2,
    rwkv_a0, rwkv_a1, rwkv_a2, rwkv_g1, rwkv_g2, rwkv_k_k, rwkv_k_a, rwkv_r_k, rwkv_ln_w,
    rwkv_ln_b, ffn_w_up, ffn_conv_w, ffn_conv_b, ffn_w_down, even_mix_norm_2, even_w_in_2,
    na_q_norm_2, na_k_norm_2, na_rel_bias_2, ssd_conv_w_2, ssd_conv_b_2, ssd_dt_bias_2,
    ssd_A_log_2, ssd_D_2, ssd_out_norm_2, even_w_out_2, odd_mix_norm_2, odd_w_qkv_2,
    gqa_q_norm_2, gqa_k_norm_2, odd_w_out_2, ffn_norm_2, ffn_w13_2, ffn_w2_2,
):
    x = first_block(
        x, norm_mix_g, norm_ffn_g, norm_final_g, sgu_w_in, sgu_b_in, sgu_g_v, sgu_w_s, sgu_b_s,
        sgu_w_out, rwkv_mu, rwkv_w_r, rwkv_w_k, rwkv_w_v, rwkv_w_o, rwkv_w0, rwkv_w1, rwkv_w2,
        rwkv_a0, rwkv_a1, rwkv_a2, rwkv_g1, rwkv_g2, rwkv_k_k, rwkv_k_a, rwkv_r_k, rwkv_ln_w,
        rwkv_ln_b, ffn_w_up, ffn_conv_w, ffn_conv_b, ffn_w_down,
    )
    return second_block(
        x, even_mix_norm_2, even_w_in_2, na_q_norm_2, na_k_norm_2, na_rel_bias_2, ssd_conv_w_2,
        ssd_conv_b_2, ssd_dt_bias_2, ssd_A_log_2, ssd_D_2, ssd_out_norm_2, even_w_out_2,
        odd_mix_norm_2, odd_w_qkv_2, gqa_q_norm_2, gqa_k_norm_2, odd_w_out_2, ffn_norm_2,
        ffn_w13_2, ffn_w2_2,
    )


_drawn_inputs = setup_inputs


def setup_inputs(seed=0):
    import zlib

    import numpy as np

    out = dict(_drawn_inputs(seed))
    spreads = {}
    factors = {'sgu_g_v': 3.076,
     'rwkv_w1': 8.0,
     'rwkv_w2': 8.0,
     'rwkv_a1': 8.0,
     'rwkv_a2': 8.0,
     'rwkv_ln_b': 4.823,
     'na_q_norm_2': 8.0,
     'na_k_norm_2': 8.0,
     'na_rel_bias_2': 8.0,
     'ssd_conv_b_2': 5.096,
     'ssd_D_2': 7.26,
     'ssd_out_norm_2': 3.558,
     'odd_mix_norm_2': 8.0,
     'gqa_q_norm_2': 8.0,
     'gqa_k_norm_2': 8.0,
     'ffn_norm_2': 3.324}
    for name, (base, spread) in spreads.items():
        noise = np.random.default_rng([zlib.crc32(name.encode()), seed]).standard_normal(out[name].shape)
        drawn = base * np.exp(spread * noise) if base else spread * noise
        out[name] = __import__('jax').numpy.asarray(drawn.astype(out[name].dtype))
    for name, factor in factors.items():
        out[name] = (out[name] * factor).astype(out[name].dtype)
    return out
```

```python
from contextlib import ExitStack, contextmanager

import numpy as np

import concourse.bass as bass
from concourse import mybir

F32 = mybir.dt.float32
ACT = mybir.ActivationFunctionType
ALU = mybir.AluOpType
AX = mybir.AxisListType.X

P = 128
T = 512
D = 1024
KD = D // P
CH = 128
NCH = T // CH
FFN = 2816
KF = FFN // P
HD = 64
NH = 16
R = 4
SLOT_BLOCKS = 12
EXP_HALF = float(np.exp(-0.5))

CONST_PARTS = [("ident", P), ("le", P), ("lt", P), ("ge", P), ("levels", 7 * P), ("pair_low", P),
               ("ones", P), ("rot", P), ("window", HD), ("head_rows", 64), ("head_cols", 10 * P), ("halves", 2), ("group_rows", 7)]
VECTOR_PARTS = [("mix_g", 16), ("ffn_g", 16), ("final_g", 8), ("sgu_b", 16), ("sgu_gv", 8), ("sgu_bs", 16),
                ("mu", 48), ("w0", 8), ("a0", 8), ("k_k", 8), ("k_a", 8), ("r_k", 8), ("ln_w", 8), ("ln_b", 8),
                ("conv_w", 264), ("conv_b", 88), ("even_g", 8), ("ssd_cw", 64), ("ssd_cb", 16),
                ("ssd_D", 8), ("ssd_g", 8), ("dt_bias", 32), ("A_log", 32), ("na_qk", 8), ("odd_g", 8),
                ("gqa_qk", 10), ("ffn2_g", 16)]


def places(parts):
    at, out = 0, {}
    for name, n in parts:
        out[name] = at
        at += n
    return out, at


CONST_AT, CONST_COLS = places(CONST_PARTS)
VECTOR_AT, VECTOR_COLS = places(VECTOR_PARTS)


def build(nc, dram, out, first=0, last=9):
    with ExitStack() as whole:
        def sbuf(name, shape):
            return whole.enter_context(nc.sbuf_tensor(name, shape, F32))

        arena = sbuf("arena", [P, 64, T])
        resid = sbuf("resid", [P, KD, T])
        ring = sbuf("ring", [P, R, SLOT_BLOCKS * P])
        const = sbuf("const", [P, CONST_COLS])
        vec = sbuf("vec", [P, VECTOR_COLS])
        work = sbuf("work", [P, 4, T])
        rows = sbuf("rows", [P, 4, T])
        state = sbuf("state", [P, KD, HD])
        small = sbuf("small", [P, 192])
        psum = whole.enter_context(nc.psum_tensor("psum", [P, 8, T], F32))

        slot_filled = [whole.enter_context(nc.semaphore(f"slot_filled{r}")) for r in range(R)]
        unit_done = whole.enter_context(nc.semaphore("unit_done"))

        phases = [0]

        @contextmanager
        def phase(*names):
            sems = [nc.alloc_semaphore(f"{n}_{phases[0]}") for n in names]
            phases[0] += 1
            with nc.Block() as block:
                yield block, *sems
            for s in sems:
                nc.gpsimd.sem_clear(s)
                nc.release_semaphore(s)

        def con(name, width=P, off=0, rows_=P):
            a = CONST_AT[name] + off
            return const[0:rows_, a:a + width]

        def col(name, i=0, n=1, rows_=slice(0, P)):
            a = VECTOR_AT[name] + i
            if isinstance(i, int):
                return vec[rows_, a:a + n]
            return vec[rows_, bass.ds(a, n)]

        def tile_of(x, i):
            if isinstance(i, int):
                return x[:, i, :]
            return x[:, bass.ds(i, 1), :].rearrange("p a t -> p (a t)")

        def flat(x):
            return x.rearrange("p a t -> p (a t)")

        def span(i, n):
            return flat(arena[:, i:i + n, :])

        ORDER = ["sgu_in", "sgu_out", "up0", "down0", "rwkv_r", "rwkv_k", "rwkv_v", "rwkv_o", "up1", "down1",
                 "even_in", "even_out", "up2", "down2", "qkv", "odd_out", "up3", "down3"]
        stage_of = dict(sgu_in=0, sgu_out=0, up0=1, down0=1, rwkv_r=2, rwkv_k=2, rwkv_v=2, rwkv_o=2, up1=3, down1=3, even_in=5, even_out=5, up2=6, down2=6, qkv=7, odd_out=7, up3=8, down3=8)
        ORDER = [n for n in ORDER if first <= stage_of[n] < last]
        first_unit, n_units = {}, 0
        for name in ORDER:
            first_unit[name] = n_units
            n_units += dram[name].shape[0]

        def load_unit(sp, name, unit, slot):
            w = dram[name]
            src = w[unit] if isinstance(unit, int) else w[bass.ds(unit, 1)].rearrange("a p n -> (a p) n")
            sp.dma_start(ring[:, slot, 0:w.shape[2]], src).then_inc(slot_filled[slot], 16)

        def load_stream(sp, name):
            n0, groups = first_unit[name], dram[name].shape[0] // R
            with sp.Fori(1, groups) as g:
                for r in range(R):
                    sp.wait_ge(unit_done, g * R + (n0 - R + r + 1))
                    load_unit(sp, name, g * R + r, r)
            at = ORDER.index(name) + 1
            if at < len(ORDER):
                for r in range(R):
                    sp.wait_ge(unit_done, n0 + (groups - 1) * R + r + 1)
                    load_unit(sp, ORDER[at], r, r)

        def products(pe, name, rhs, taken, parts=1, before=None):
            n0, groups = first_unit[name], dram[name].shape[0] // R
            nk = dram[name].shape[2] // P
            banks = R // parts

            def group(g):
                for r in range(R):
                    m, part = r // parts, r % parts
                    pe.wait_ge(slot_filled[r], 16 * (n0 // R + 1) + (0 if g is None else g * 16))
                    if g is not None and part == 0:
                        pe.wait_ge(taken, g * banks + (m + 1 - banks))
                    for k in range(nk):
                        mm = nc.tensor.matmul(psum[:, m, :], ring[:, r, k * P:(k + 1) * P], rhs(part * nk + k),
                                              start=(part == 0 and k == 0), stop=(part == parts - 1 and k == nk - 1))
                    mm.then_inc(unit_done, 1)

            if before:
                before(pe)
            group(None)
            with pe.Fori(1, groups) as g:
                group(g)

        def bodies(eng, name, body, parts=1, lo=0, hi=None):
            n0, groups = first_unit[name], dram[name].shape[0] // R
            with eng.Fori(lo, groups if hi is None else hi) as g:
                for m in range(R // parts):
                    body(g * (R // parts) + m, m, lambda: eng.wait_ge(unit_done, g * R + (n0 + (m + 1) * parts)))

        def add_projection(name, rhs, parts=1):
            with phase("taken") as (block, taken):
                @block.sync
                def _(sp):
                    load_stream(sp, name)

                @block.tensor
                def _(pe):
                    products(pe, name, rhs, taken, parts)

                @block.vector
                def _(dve):
                    def body(m, bank, products_done):
                        products_done()
                        x = tile_of(resid, m)
                        nc.vector.tensor_tensor(x, psum[:, bank, :], x, ALU.add).then_inc(taken, 1)
                    bodies(dve, name, body, parts)

        def norm(src, dst, n, groups, gather, spread, gain, scale, guard, guard_op):
            with phase("squared", "summed", "guarded", "rooted", "inverted", "spread_done", "scaled") as \
                    (block, squared, summed, guarded, rooted, inverted, spread_done, scaled):
                one = groups == 1

                @block.scalar
                def _(act):
                    for i in range(n):
                        if i >= 4:
                            act.wait_ge(summed, i - 3)
                        nc.scalar.activation(work[:, i % 4, :], src(i), ACT.Square).then_inc(squared, 1)
                    act.wait_ge(guarded, 1)
                    nc.scalar.activation(rows[0:groups, 1, :], rows[0:groups, 0, :], ACT.Sqrt).then_inc(rooted, 1)

                @block.tensor
                def _(pe):
                    for i in range(n):
                        pe.wait_ge(squared, i + 1)
                        nc.tensor.matmul(psum[0:groups, 4, :], gather(i), work[:, i % 4, :],
                                         start=(i == 0), stop=(i == n - 1)).then_inc(summed, 1)
                    pe.wait_ge(inverted, 1)
                    for i in range(1 if one else n):
                        if i >= 2:
                            pe.wait_ge(scaled, i - 1)
                        nc.tensor.matmul(psum[:, 5 + i % 2, :], spread(i), rows[0:groups, 0, :],
                                         start=True, stop=True).then_inc(spread_done, 1)

                @block.vector
                def _(dve):
                    dve.wait_ge(summed, n)
                    nc.vector.tensor_scalar(rows[0:groups, 0, :], psum[0:groups, 4, :], scale, guard,
                                            ALU.mult, guard_op).then_inc(guarded, 1)
                    dve.wait_ge(rooted, 1)
                    nc.vector.reciprocal(rows[0:groups, 0, :], rows[0:groups, 1, :]).then_inc(inverted, 1)
                    for i in range(n):
                        dve.wait_ge(spread_done, 1 if one else i + 1)
                        nc.vector.scalar_tensor_tensor(out=dst(i), in0=src(i), scalar=gain(i),
                                                       in1=psum[:, 5 if one else 5 + i % 2, :],
                                                       op0=ALU.mult, op1=ALU.mult).then_inc(scaled, 1)

        def rms_norm(src, dst, n, gain, eps=1e-6):
            norm(src, dst, n, 1, lambda i: con("ones", 1), lambda i: con("ones", P, 0, 1), gain,
                 1.0 / (n * P), eps, ALU.add)

        def head_sums(i):
            return con("head_rows", 32, 32 - 2 * i - 2)

        def head_spread(i):
            return con("head_cols", P, i * P, 32)

        def transposes(n, src, read, engines=("scalar", "vector"), start_bank=0):
            with phase("turned", "read_act", "read_dve") as (block, turned, read_act, read_dve):
                who = [engines[j % len(engines)] for j in range(n)]
                sem = {"scalar": read_act, "vector": read_dve}
                upto_ = [sum(w == who[j] for w in who[:j + 1]) for j in range(n)]

                @block.tensor
                def _(pe):
                    for j in range(n):
                        if j >= 8:
                            pe.wait_ge(sem[who[j - 8]], upto_[j - 8])
                        for b in range(4):
                            tr = nc.tensor.transpose(psum[:, j % 8, b * P:(b + 1) * P], src(j, b), con("ident"))
                        tr.then_inc(turned, 1)

                def reader(eng, name):
                    for j in range(n):
                        if who[j] == name:
                            eng.wait_ge(turned, j + 1)
                            read(name, j, psum[:, j % 8, :]).then_inc(sem[name], 1)

                @block.scalar
                def _(act):
                    reader(act, "scalar")

                @block.vector
                def _(dve):
                    reader(dve, "vector")

        def copy_on(eng, dst, src):
            if eng == "vector":
                return nc.vector.tensor_copy(dst, src)
            return nc.scalar.activation(dst, src, ACT.Copy)

        def by_chunk(bank):
            return bank.rearrange("p (c f) -> p c f", c=NCH)

        def to_tokens(src_tile, n, dst):
            transposes(n, lambda j, b: src_tile(j)[:, b * P:(b + 1) * P],
                       lambda eng, j, bank: copy_on(eng, dst[:, :, j * P:(j + 1) * P], by_chunk(bank)))

        def conv_ffn(layer):
            hidden, xn = 8, 0
            rms_norm(lambda i: resid[:, i, :], lambda i: arena[:, xn + i, :], KD, lambda i: col("ffn_g", layer * KD + i))
            name = f"up{layer}"
            cw, cb = VECTOR_AT["conv_w"] + layer * 132, VECTOR_AT["conv_b"] + layer * 44

            def v1(a):
                return vec[:, bass.ds(a, 1)]

            with phase("biased", "conv_mid", "conv_done", "gated", "multiplied") as \
                    (block, biased, conv_mid, conv_done, gated, multiplied):
                groups = dram[name].shape[0] // R
                n0 = first_unit[name]

                @block.sync
                def _(sp):
                    load_stream(sp, name)

                @block.tensor
                def _(pe):
                    products(pe, name, lambda k: arena[:, xn + k, :], conv_done)

                def act_group(act, g, first):
                    for pair in range(2):
                        for r in (2 * pair, 2 * pair + 1):
                            act.wait_ge(unit_done, g * R + (n0 + r + 1))
                            if not first:
                                act.wait_ge(multiplied, g * 2 + (pair + 1 - 2))
                            nc.scalar.activation(work[:, r, :], psum[:, r, :], ACT.Identity,
                                                 bias=v1(g * R + (cb + r)), scale=v1(g * R + (cw + 88 + r))).then_inc(biased, 1)
                        act.wait_ge(conv_done, g * R + (2 * pair + 1))
                        nc.scalar.activation(rows[:, pair, :], work[:, 2 * pair, :], ACT.Silu).then_inc(gated, 1)

                @block.scalar
                def _(act):
                    act_group(act, 0, True)
                    with act.Fori(1, groups) as g:
                        act_group(act, g, False)

                @block.vector
                def _(dve):
                    with dve.Fori(0, groups) as g:
                        for pair in range(2):
                            for r in (2 * pair, 2 * pair + 1):
                                dve.wait_ge(biased, g * R + (r + 1))
                                nc.vector.scalar_tensor_tensor(out=work[:, r, 1:T], in0=psum[:, r, 0:T - 1],
                                                               scalar=v1(g * R + (cw + 44 + r)), in1=work[:, r, 1:T],
                                                               op0=ALU.mult, op1=ALU.add).then_inc(conv_mid, 1)
                                dve.wait_ge(conv_mid, g * R + (r + 1))
                                nc.vector.scalar_tensor_tensor(out=work[:, r, 2:T], in0=psum[:, r, 0:T - 2],
                                                               scalar=v1(g * R + (cw + r)), in1=work[:, r, 2:T],
                                                               op0=ALU.mult, op1=ALU.add).then_inc(conv_done, 1)
                            dve.wait_ge(conv_done, g * R + (2 * pair + 2))
                            dve.wait_ge(gated, g * 2 + (pair + 1))
                            nc.vector.tensor_tensor(tile_of(arena, g * 2 + (hidden + pair)), rows[:, pair, :],
                                                    work[:, 2 * pair + 1, :], ALU.mult).then_inc(multiplied, 1)
            add_projection(f"down{layer}", lambda k: arena[:, hidden + k, :], 2)

        def swiglu(layer):
            hidden, xn = 8, 0
            rms_norm(lambda i: resid[:, i, :], lambda i: arena[:, xn + i, :], KD, lambda i: col("ffn2_g", layer * KD + i))
            name = f"up{layer + 2}"
            n0 = first_unit[name]
            with phase("taken", "gated") as (block, taken, gated):
                groups = dram[name].shape[0] // R

                @block.sync
                def _(sp):
                    load_stream(sp, name)

                @block.tensor
                def _(pe):
                    products(pe, name, lambda k: arena[:, xn + k, :], taken)

                @block.scalar
                def _(act):
                    def group(g, first):
                        for pair in range(2):
                            act.wait_ge(unit_done, g * R + (n0 + 2 * pair + 1))
                            if not first:
                                act.wait_ge(taken, g * R + (2 * pair + 2 - R))
                            nc.scalar.activation(rows[:, pair, :], psum[:, 2 * pair, :], ACT.Silu).then_inc(gated, 1)
                    group(0, True)
                    with act.Fori(1, groups) as g:
                        group(g, False)

                @block.vector
                def _(dve):
                    with dve.Fori(0, groups) as g:
                        for pair in range(2):
                            dve.wait_ge(gated, g * 2 + (pair + 1))
                            dve.wait_ge(unit_done, g * R + (n0 + 2 * pair + 2))
                            nc.vector.tensor_tensor(tile_of(arena, g * 2 + (hidden + pair)), rows[:, pair, :],
                                                    psum[:, 2 * pair + 1, :], ALU.mult).then_inc(taken, 2)
            add_projection(f"down{layer + 2}", lambda k: arena[:, hidden + k, :], 2)

        with phase("loaded") as (block, loaded):
            @block.sync
            def _(sp):
                for r in range(R if ORDER else 0):
                    load_unit(sp, ORDER[0], r, r)
                sp.wait_ge(loaded, 48)

            @block.scalar
            def _(act):
                act.dma_start(resid[:, :, :], dram["x"]).then_inc(loaded, 16)
                act.dma_start(const[:, :], dram["const"]).then_inc(loaded, 16)
                act.dma_start(vec[:, :], dram["vec"]).then_inc(loaded, 16)

        def sgu():
            xn, uv, vt, mt, wc = 0, 8, 24, 32, 40
            rms_norm(lambda i: resid[:, i, :], lambda i: arena[:, xn + i, :], KD, lambda i: col("mix_g", i))
            wcv = span(wc, 4).rearrange("p (g t) -> p g t", g=NH)
            with phase("taken", "ws_loaded", "masked") as (block, taken, ws_loaded, masked):
                @block.sync
                def _(sp):
                    sp.dma_start(span(wc, 4), dram["sgu_ws"]).then_inc(ws_loaded, 16)
                    load_stream(sp, "sgu_in")

                @block.tensor
                def _(pe):
                    products(pe, "sgu_in", lambda k: arena[:, xn + k, :], taken)

                @block.vector
                def _(dve):
                    dve.wait_ge(ws_loaded, 16)
                    nc.vector.tensor_tensor(wcv, wcv, con("le").unsqueeze(1).to_broadcast([P, NH, P]),
                                            ALU.mult).then_inc(masked, 1)

                @block.scalar
                def _(act):
                    def body(m, bank, products_done):
                        products_done()
                        nc.scalar.activation(tile_of(arena, m + uv), psum[:, bank, :], ACT.Gelu,
                                             bias=col("sgu_b", m)).then_inc(taken, 1)
                    bodies(act, "sgu_in", body)
            rms_norm(lambda i: arena[:, uv + 8 + i, :], lambda i: arena[:, uv + 8 + i, :], KD, lambda i: col("sgu_gv", i))
            vtv = span(vt, 8).rearrange("p (c f) -> p c f", c=NCH)
            mtv = span(mt, 8).rearrange("p (c f) -> p c f", c=NCH)
            to_tokens(lambda j: arena[:, uv + 8 + j, :], KD, vtv)
            with phase("mixed", "read") as (block, mixed, read):
                @block.tensor
                def _(pe):
                    for g in range(NH):
                        if g >= 8:
                            pe.wait_ge(read, g - 7)
                        nc.tensor.matmul(psum[:, g % 8, 0:256].rearrange("p (c f) -> p c f", c=NCH), wcv[:, g, :],
                                         vtv[:, :, g * HD:(g + 1) * HD], start=True, stop=True).then_inc(mixed, 1)

                @block.vector
                def _(dve):
                    for g in range(NH):
                        dve.wait_ge(mixed, g + 1)
                        nc.vector.tensor_scalar(mtv[:, :, g * HD:(g + 1) * HD],
                                                psum[:, g % 8, 0:256].rearrange("p (c f) -> p c f", c=NCH),
                                                col("sgu_bs", g), None, ALU.add).then_inc(read, 1)
            transposes(KD, lambda j, b: mtv[:, b, j * P:(j + 1) * P],
                       lambda eng, j, bank: nc.vector.tensor_tensor(arena[:, uv + j, :], bank, arena[:, uv + j, :], ALU.mult),
                       engines=("vector",))
            add_projection("sgu_out", lambda k: arena[:, uv + k, :])

        def rwkv():
            XN, XX, MX, RR, KK, VV, WW, AA = (8 * i for i in range(8))

            def whole_of(s):
                return span(s, 8)

            rms_norm(lambda i: resid[:, i, :], lambda i: arena[:, XN + i, :], KD, lambda i: col("mix_g", 8 + i))
            lw1 = span(RR, 5)[:, 0:8 * 288].rearrange("p (k n) -> p k n", k=KD)
            w2 = span(KK, 2)
            a2 = span(KK + 2, 2)
            with phase("loaded", "shifted") as (block, loaded, shifted):
                @block.sync
                def _(sp):
                    sp.dma_start(span(RR, 5)[:, 0:8 * 288], dram["lora1"]).then_inc(loaded, 16)
                    sp.dma_start(w2[0:HD, :], dram["lora_w2"]).then_inc(loaded, 16)
                    sp.dma_start(a2[0:HD, :], dram["lora_a2"]).then_inc(loaded, 16)
                    sp.wait_ge(loaded, 48)

                @block.vector
                def _(dve):
                    a, b = arena[:, XN:XN + 8, :], arena[:, XX:XX + 8, :]
                    nc.vector.tensor_tensor(b[:, :, 1:T], a[:, :, 0:T - 1], a[:, :, 1:T], ALU.subtract).then_inc(shifted, 1)
                    nc.vector.tensor_scalar(b[:, :, 0:1], a[:, :, 0:1], -1.0, None, ALU.mult).then_inc(shifted, 1)
                    dve.wait_ge(shifted, 2)

            def mix(dve, which, mixed):
                for i in range(KD):
                    nc.vector.scalar_tensor_tensor(out=arena[:, MX + i, :], in0=arena[:, XX + i, :],
                                                   scalar=col("mu", which * KD + i), in1=arena[:, XN + i, :],
                                                   op0=ALU.mult, op1=ALU.add).then_inc(mixed, 1)

            for which, parts in ((1, [(0, 64, 0, ACT.Tanh)]), (4, [(64, 64, 1, ACT.Copy)]),
                                 (5, [(128, 128, 2, ACT.Sigmoid), (256, 32, 3, ACT.Sigmoid)])):
                with phase("mixed", "summed", "kept") as (block, mixed, summed, kept):
                    @block.vector
                    def _(dve):
                        mix(dve, which, mixed)

                    @block.tensor
                    def _(pe):
                        for n, (at, m, row, _) in enumerate(parts):
                            for k in range(KD):
                                if n == 0:
                                    pe.wait_ge(mixed, k + 1)
                                mm = nc.tensor.matmul(psum[0:m, n, :], lw1[:, k, at:at + m], arena[:, MX + k, :],
                                                      start=(k == 0), stop=(k == KD - 1))
                            mm.then_inc(summed, 1)

                    @block.scalar
                    def _(act):
                        for n, (at, m, row, func) in enumerate(parts):
                            act.wait_ge(summed, n + 1)
                            nc.scalar.activation(rows[0:m, row, :], psum[0:m, n, :], func).then_inc(kept, 1)

            with phase("summed", "kept") as (block, summed, kept):
                jobs = [(w2, 0, WW, "w0", m) for m in range(KD)] + [(a2, 1, AA, "a0", m) for m in range(KD)]

                @block.tensor
                def _(pe):
                    for n, (w, row, dst, bias, m) in enumerate(jobs):
                        if n >= 4:
                            pe.wait_ge(kept, n - 3)
                        nc.tensor.matmul(psum[:, n % 4, :], w[0:HD, m * P:(m + 1) * P], rows[0:HD, row, :],
                                         start=True, stop=True).then_inc(summed, 1)

                @block.scalar
                def _(act):
                    for n, (w, row, dst, bias, m) in enumerate(jobs):
                        act.wait_ge(summed, n + 1)
                        nc.scalar.activation(arena[:, dst + m, :], psum[:, n % 4, :], ACT.Sigmoid,
                                             bias=col(bias, m)).then_inc(kept, 1)

            for which, name, dst in ((0, "rwkv_r", RR), (2, "rwkv_k", KK), (3, "rwkv_v", VV)):
                with phase("mixed", "taken") as (block, mixed, taken):
                    @block.sync
                    def _(sp):
                        load_stream(sp, name)

                    @block.vector
                    def _(dve):
                        mix(dve, which, mixed)

                    @block.tensor
                    def _(pe):
                        products(pe, name, lambda k: arena[:, MX + k, :], taken,
                                 before=lambda pe: pe.wait_ge(mixed, KD))

                    @block.scalar
                    def _(act):
                        def body(m, bank, products_done):
                            products_done()
                            nc.scalar.activation(tile_of(arena, m + dst), psum[:, bank, :], ACT.Copy).then_inc(taken, 1)
                        bodies(act, name, body)

            with phase("scaled") as (block, scaled):
                @block.vector
                def _(dve):
                    for i in range(KD):
                        nc.vector.tensor_scalar(arena[:, XN + i, :], arena[:, KK + i, :], col("k_k", i), None,
                                                ALU.mult).then_inc(scaled, 1)
            norm(lambda i: arena[:, XN + i, :], lambda i: arena[:, XN + i, :], KD, 32, head_sums, head_spread,
                 lambda i: 1.0, 1.0, 1e-24, ALU.max)

            mid = small[:, 0:32].rearrange("p (i c) -> p i c", c=NCH)
            end = small[:, 32:64].rearrange("p (i c) -> p i c", c=NCH)
            scl = small[:, 64:96].rearrange("p (i c) -> p i c", c=NCH)
            bonus = small[:, 128:192].rearrange("p (c h) -> p c h", c=NCH)
            chunks = "p (j t) -> p j t"

            with phase("tmp_done", "k_done", "rk_done", "summed", "b_done", "scanned", "mid_done", "centred", "less") as \
                    (block, tmp_done, k_done, rk_done, summed, b_done, scanned, mid_done, centred, less):
                @block.vector
                def _(dve):
                    for i in range(KD):
                        if i >= 4:
                            dve.wait_ge(k_done, i - 3)
                        nc.vector.tensor_scalar(work[:, i % 4, :], arena[:, AA + i, :], -1.0, col("k_a", i),
                                                ALU.add, ALU.mult).then_inc(tmp_done, 1)
                        for c in range(NCH):
                            s = slice(c * CH, (c + 1) * CH)
                            nc.vector.tensor_tensor_scan(arena[:, XX + i, s], con("ones"), arena[:, WW + i, s], 0.0,
                                                         ALU.mult, ALU.add).then_inc(scanned, 1)
                        dve.wait_ge(tmp_done, i + 1)
                        nc.vector.scalar_tensor_tensor(out=arena[:, KK + i, :], in0=work[:, i % 4, :], scalar=1.0,
                                                       in1=arena[:, KK + i, :], op0=ALU.add, op1=ALU.mult).then_inc(k_done, 1)
                        dve.wait_ge(k_done, i + 1)
                        nc.vector.scalar_tensor_tensor(out=arena[:, MX + i, :], in0=arena[:, RR + i, :],
                                                       scalar=col("r_k", i), in1=arena[:, KK + i, :],
                                                       op0=ALU.mult, op1=ALU.mult).then_inc(rk_done, 1)
                    dve.wait_ge(scanned, KD * NCH)
                    sums = whole_of(XX).rearrange(chunks, t=CH)
                    nc.vector.tensor_copy(mid, sums[:, :, 63:64].rearrange("p (i c) o -> p i (c o)", c=NCH)).then_inc(mid_done, 1)
                    dve.wait_ge(mid_done, 1)
                    nc.vector.tensor_tensor(sums, sums, small[:, 0:32].unsqueeze(2).to_broadcast([P, 32, CH]),
                                            ALU.subtract).then_inc(centred, 1)
                    dve.wait_ge(centred, 1)
                    nc.vector.tensor_tensor(whole_of(WW), whole_of(XX), whole_of(WW), ALU.subtract).then_inc(less, 1)
                    dve.wait_ge(summed, 1)
                    nc.vector.tensor_copy(small[:, 128:192], psum[:, 0, 0:64]).then_inc(less, 1)

                @block.tensor
                def _(pe):
                    pe.wait_ge(rk_done, KD)
                    for c in range(NCH):
                        for i in range(KD):
                            mm = nc.tensor.matmul(psum[:, 0, c * NH + 2 * i:c * NH + 2 * i + 2],
                                                  arena[:, MX + i, c * CH:(c + 1) * CH], con("halves", 2),
                                                  start=True, stop=True)
                    mm.then_inc(summed, 1)

            with phase("b_done", "e1", "e2", "e3", "mids", "hats", "ends", "bonus_kept") as \
                    (block, b_done, e1, e2, e3, mids, hats, ends, bonus_kept):
                @block.scalar
                def _(act):
                    nc.scalar.activation(whole_of(MX), whole_of(XX), ACT.Exp, scale=-EXP_HALF).then_inc(e1, 1)
                    act.wait_ge(e1, 1)
                    nc.scalar.activation(whole_of(XX), whole_of(XX), ACT.Exp, scale=EXP_HALF).then_inc(e2, 1)
                    nc.scalar.activation(whole_of(WW), whole_of(WW), ACT.Exp, scale=-EXP_HALF).then_inc(e3, 1)
                    nc.scalar.activation(small[:, 96:128], small[:, 0:32], ACT.Exp, scale=-EXP_HALF).then_inc(mids, 1)

                @block.vector
                def _(dve):
                    nc.vector.tensor_tensor(whole_of(AA), whole_of(XN), whole_of(AA), ALU.mult).then_inc(b_done, 1)
                    dve.wait_ge(e1, 1)
                    nc.vector.tensor_tensor(whole_of(RR), whole_of(RR), whole_of(MX), ALU.mult).then_inc(hats, 1)
                    nc.vector.tensor_copy(end, whole_of(MX).rearrange(chunks, t=CH)[:, :, 127:128]
                                          .rearrange("p (i c) o -> p i (c o)", c=NCH)).then_inc(ends, 1)
                    dve.wait_ge(e2, 1)
                    nc.vector.tensor_tensor(whole_of(KK), whole_of(KK), whole_of(XX), ALU.mult).then_inc(hats, 1)
                    dve.wait_ge(b_done, 1)
                    nc.vector.tensor_tensor(whole_of(AA), whole_of(AA), whole_of(XX), ALU.mult).then_inc(hats, 1)
                    dve.wait_ge(e3, 1)
                    nc.vector.scalar_tensor_tensor(out=whole_of(WW), in0=whole_of(WW), scalar=-1.0, in1=whole_of(XN),
                                                   op0=ALU.mult, op1=ALU.mult).then_inc(hats, 1)
                    dve.wait_ge(mids, 1)
                    dve.wait_ge(ends, 1)
                    nc.vector.tensor_tensor(scl[:, :, 0:3], end[:, :, 0:3],
                                            small[:, 96:128].rearrange("p (i c) -> p i c", c=NCH)[:, :, 1:4],
                                            ALU.mult).then_inc(ends, 1)

            vt = whole_of(MX).rearrange("p (c f) -> p c f", c=NCH)
            to_tokens(lambda j: arena[:, VV + j, :], KD, vt)
            yt = whole_of(VV).rearrange("p (c f) -> p c f", c=NCH)
            bufs = []
            for s in (XN, XX):
                w = whole_of(s)
                bufs.append(dict(
                    m=w[:, 0:2048].rearrange("p (k h t) -> p k h t", k=4, h=4),
                    x=w[:, 2048:3072].rearrange("p (k h t) -> p k h t", k=2, h=4),
                    xf=w[:, 2048:3072], lb=w[:, 3072:3584].rearrange("p (h t) -> p h t", h=4),
                    t1=w[:, 3584:4096].rearrange("p (h t) -> p h t", h=4), t1f=w[:, 3584:4096]))
            wf = flat(work[:, :, :])
            btm, ktm = wf[:, 0:512], wf[:, 512:1024]
            z, sa = wf[:, 1024:1536], wf[:, 1536:2048]
            AB, RB, AK, RK = range(4)

            def per_head(ap):
                return ap.unsqueeze(1).to_broadcast([P, 4, P])

            for step in range(2 * NCH):
                c, half = step // 2, step % 2
                cs = slice(c * CH, (c + 1) * CH)

                def fm(slot, h):
                    i, e = h // 2, h % 2
                    return arena[e * HD:(e + 1) * HD, slot + i, cs]

                with phase("scored", "masked", "first_inv", "ones_added", "bk_turned", "bk_kept") as \
                        (block, scored, masked, first_inv, ones_added, bk_turned, bk_kept):
                    jobs = [(a, kind) for a in range(2) for kind in (AB, RB, AK, RK, 4)]

                    @block.tensor
                    def _(pe):
                        for n, (a, kind) in enumerate(jobs):
                            if n >= 6:
                                pe.wait_ge(masked, n - 5)
                            for j in range(4):
                                h = half * 8 + 2 * j + a
                                lhs, rhs = {AB: (AA, WW), RB: (AA, RR), AK: (KK, WW), RK: (KK, RR), 4: (WW, AA)}[kind]
                                mm = nc.tensor.matmul(psum[:, n % 6, j * P:(j + 1) * P], fm(lhs, h), fm(rhs, h),
                                                      start=True, stop=True)
                            mm.then_inc(scored, 1)
                        for which, slot in enumerate((AA, KK)):
                            for j in range(4):
                                tr = nc.tensor.transpose(psum[:, 6 + which, j * P:(j + 1) * P],
                                                         arena[:, slot + half * 4 + j, cs], con("ident"))
                            tr.then_inc(bk_turned, 1)

                    @block.scalar
                    def _(act):
                        for which, dst in enumerate((btm, ktm)):
                            act.wait_ge(bk_turned, which + 1)
                            nc.scalar.activation(dst, psum[:, 6 + which, :], ACT.Copy).then_inc(bk_kept, 1)

                    @block.vector
                    def _(dve):
                        for n, (a, kind) in enumerate(jobs):
                            dve.wait_ge(scored, n + 1)
                            src = psum[:, n % 6, :].rearrange("p (h t) -> p h t", h=4)
                            if kind == 4:
                                nc.vector.tensor_tensor(bufs[a]["x"][:, 0], src, per_head(con("pair_low")),
                                                        ALU.mult).then_inc(masked, 1)
                            else:
                                mask = con("lt") if kind in (AB, AK) else con("le")
                                nc.vector.tensor_tensor(bufs[a]["m"][:, kind], src, per_head(mask),
                                                        ALU.mult).then_inc(masked, 1)

                    @block.gpsimd
                    def _(pool):
                        for a in range(2):
                            pool.wait_ge(masked, 5 * a + 5)
                            nc.gpsimd.tensor_tensor(bufs[a]["x"][:, 1], bufs[a]["m"][:, AB], per_head(con("levels")),
                                                    ALU.mult).then_inc(first_inv, 1)
                            pool.wait_ge(first_inv, a + 1)
                            x8 = bufs[a]["xf"].rearrange("p (h t) -> p h t", h=8)
                            nc.gpsimd.tensor_tensor(x8, x8, con("ident").unsqueeze(1).to_broadcast([P, 8, P]),
                                                    ALU.add).then_inc(ones_added, 1)

                with phase("lb_ready", "t1_done", "t1_kept", "p_done", "x_added") as \
                        (block, lb_ready, t1_done, t1_kept, p_done, x_added):
                    @block.gpsimd
                    def _(pool):
                        for l in range(6):
                            for a in range(2):
                                if l:
                                    pool.wait_ge(t1_done, 2 * (l - 1) + a + 1)
                                nc.gpsimd.tensor_tensor(bufs[a]["lb"], bufs[a]["m"][:, AB],
                                                        per_head(con("levels", P, (l + 1) * P)),
                                                        ALU.mult).then_inc(lb_ready, 1)

                    @block.tensor
                    def _(pe):
                        for l in range(6):
                            for a in range(2):
                                pe.wait_ge(lb_ready, 2 * l + a + 1)
                                if l:
                                    pe.wait_ge(x_added, 2 * (l - 1) + a + 1)
                                for j in range(4):
                                    mm = nc.tensor.matmul(psum[:, a, j * P:(j + 1) * P], bufs[a]["lb"][:, j, :],
                                                          bufs[a]["x"][:, 0, j, :], start=True, stop=True)
                                mm.then_inc(t1_done, 1)
                            for a in range(2):
                                pe.wait_ge(t1_kept, 2 * l + a + 1)
                                for j in range(4):
                                    t1, xt = bufs[a]["t1"][:, j, :], bufs[a]["x"][:, 1, j, :]
                                    if l < 5:
                                        nc.tensor.matmul(psum[:, 2 + 2 * a, j * P:(j + 1) * P], xt, t1, start=True, stop=True)
                                    mm = nc.tensor.matmul(psum[:, 3 + 2 * a, j * P:(j + 1) * P], t1, xt, start=True, stop=True)
                                mm.then_inc(p_done, 1)

                    @block.scalar
                    def _(act):
                        for l in range(6):
                            for a in range(2):
                                act.wait_ge(t1_done, 2 * l + a + 1)
                                nc.scalar.activation(bufs[a]["t1f"], psum[:, a, :], ACT.Copy).then_inc(t1_kept, 1)

                    @block.vector
                    def _(dve):
                        for l in range(6):
                            for a in range(2):
                                dve.wait_ge(p_done, 2 * l + a + 1)
                                if l < 5:
                                    x = bufs[a]["xf"]
                                    nc.vector.tensor_tensor(x, flat(psum[:, 2 + 2 * a:4 + 2 * a, :]), x, ALU.add)\
                                        .then_inc(x_added, 1)
                                else:
                                    x = bufs[a]["xf"][:, 512:1024]
                                    nc.vector.tensor_tensor(x, psum[:, 3 + 2 * a, :], x, ALU.add).then_inc(x_added, 1)

                with phase("z_done", "z_kept", "sa_done", "sa_kept", "y_done", "s_done", "y_kept", "s_added", "s_kept") as \
                        (block, z_done, z_kept, sa_done, sa_kept, y_done, s_done, y_kept, s_added, s_kept):
                    def head(j):
                        h = half * 8 + j
                        b = bufs[j % 2]
                        s0 = state[(h % 2) * HD:(h % 2 + 1) * HD, h // 2, :]
                        return h, b, j // 2, s0, vt[:, c, h * HD:(h + 1) * HD]

                    @block.tensor
                    def _(pe):
                        for j in range(8):
                            h, b, jj, s0, v = head(j)
                            o = psum[:, 4 * (j % 2), (j // 2) * HD:(j // 2 + 1) * HD]
                            if c:
                                nc.tensor.matmul(o, fm(WW, h), s0, start=True, stop=False)
                            mm = nc.tensor.matmul(o, b["m"][:, AK, jj, :], v, start=(c == 0), stop=True)
                        mm.then_inc(z_done, 1)
                        pe.wait_ge(z_kept, 2)
                        for j in range(8):
                            h, b, jj, s0, v = head(j)
                            mm = nc.tensor.matmul(psum[:, 1, j * HD:(j + 1) * HD], b["x"][:, 1, jj, :],
                                                  z[:, (j % 2) * 256 + (j // 2) * HD:(j % 2) * 256 + (j // 2 + 1) * HD],
                                                  start=True, stop=True)
                        mm.then_inc(sa_done, 1)
                        pe.wait_ge(sa_kept, 1)
                        if c < NCH - 1:
                            for i in range(4):
                                o = psum[:, 3, i * P:(i + 1) * P]
                                nc.tensor.matmul(o, btm[:, i * P:(i + 1) * P], sa[:, i * P:(i + 1) * P], start=True, stop=False)
                                mm = nc.tensor.matmul(o, ktm[:, i * P:(i + 1) * P],
                                                      vt[:, c, (half * 4 + i) * P:(half * 4 + i + 1) * P],
                                                      start=False, stop=True)
                            mm.then_inc(s_done, 1)
                        for j in range(8):
                            h, b, jj, s0, v = head(j)
                            o = psum[:, 2 + 3 * (j % 2), (j // 2) * HD:(j // 2 + 1) * HD]
                            if c:
                                nc.tensor.matmul(o, fm(RR, h), s0, start=True, stop=False)
                            nc.tensor.matmul(o, b["m"][:, RB, jj, :], sa[:, j * HD:(j + 1) * HD], start=(c == 0), stop=False)
                            mm = nc.tensor.matmul(o, b["m"][:, RK, jj, :], v, start=False, stop=True)
                        mm.then_inc(y_done, 1)

                    @block.vector
                    def _(dve):
                        dve.wait_ge(z_done, 1)
                        for e in range(2):
                            nc.vector.tensor_copy(z[:, e * 256:(e + 1) * 256], psum[:, 4 * e, 0:256]).then_inc(z_kept, 1)
                        dve.wait_ge(sa_done, 1)
                        nc.vector.tensor_copy(sa, psum[:, 1, :]).then_inc(sa_kept, 1)
                        dve.wait_ge(y_done, 1)
                        yh = yt[:, c, half * 512:(half + 1) * 512].rearrange("p (i e f) -> p i e f", i=4, e=2)
                        for e in range(2):
                            nc.vector.tensor_copy(yh[:, :, e, :], psum[:, 2 + 3 * e, 0:256].rearrange("p (i f) -> p i f", i=4))\
                                .then_inc(y_kept, 1)
                        if c < NCH - 1:
                            dve.wait_ge(s_done, 1)
                            for e in range(2):
                                ps = slice(e * HD, (e + 1) * HD)
                                s0 = state[ps, half * 4:half * 4 + 4, :]
                                new = psum[ps, 3, :].rearrange("p (i f) -> p i f", i=4)[:, :, e * HD:(e + 1) * HD]
                                sc = scl[ps, half * 4:half * 4 + 4, c:c + 1].to_broadcast([HD, 4, HD])
                                if c:
                                    nc.vector.tensor_tensor(s0, new, s0, ALU.add).then_inc(s_added, 1)
                                    dve.wait_ge(s_added, e + 1)
                                    nc.vector.tensor_tensor(s0, s0, sc, ALU.mult).then_inc(s_kept, 1)
                                else:
                                    nc.vector.tensor_tensor(s0, new, sc, ALU.mult).then_inc(s_kept, 1)

            yw = whole_of(VV).rearrange("p (j f) -> p j f", f=HD)
            sq = whole_of(XN).rearrange("p (j f) -> p j f", f=HD)
            g2 = span(XX, 4)
            with phase("g2_loaded", "s1", "s2", "s3", "s4", "s5", "s6", "s7", "s8", "s9") as \
                    (block, g2_loaded, mean_sum, mean_done, less_mean, squared, var_sum, var_done, rooted, inverted, done):
                m1, m2, m3 = small[:, 0:64], small[:, 64:128], state[:, 0, :]

                @block.sync
                def _(sp):
                    sp.dma_start(g2[:, 0:D], dram["lora_g2"][0:P, :]).then_inc(g2_loaded, 16)
                    sp.dma_start(g2[0:32, D:2 * D], dram["lora_g2"][P:160, :]).then_inc(g2_loaded, 16)
                    sp.wait_ge(g2_loaded, 32)

                @block.vector
                def _(dve):
                    nc.vector.reduce_sum(m1, yw, axis=AX).then_inc(mean_sum, 1)
                    dve.wait_ge(mean_sum, 1)
                    nc.vector.tensor_scalar(m2, m1, 1.0 / HD, None, ALU.mult).then_inc(mean_done, 1)
                    dve.wait_ge(mean_done, 1)
                    nc.vector.tensor_tensor(yw, yw, m2.unsqueeze(2).to_broadcast([P, 64, HD]), ALU.subtract).then_inc(less_mean, 1)
                    vw = whole_of(MX).rearrange("p (j f) -> p j f", f=HD)
                    nc.vector.tensor_tensor(vw, vw, small[:, 128:192].unsqueeze(2).to_broadcast([P, 64, HD]), ALU.mult).then_inc(done, 1)
                    dve.wait_ge(squared, 1)
                    nc.vector.reduce_sum(m1, sq, axis=AX).then_inc(var_sum, 1)
                    dve.wait_ge(var_sum, 1)
                    nc.vector.tensor_scalar(m2, m1, 1.0 / HD, 64e-5, ALU.mult, ALU.add).then_inc(var_done, 1)
                    dve.wait_ge(rooted, 1)
                    nc.vector.reciprocal(m1, m3).then_inc(inverted, 1)
                    dve.wait_ge(inverted, 1)
                    nc.vector.tensor_tensor(yw, yw, m1.unsqueeze(2).to_broadcast([P, 64, HD]), ALU.mult).then_inc(done, 1)

                @block.scalar
                def _(act):
                    act.wait_ge(less_mean, 1)
                    nc.scalar.activation(whole_of(XN), whole_of(VV), ACT.Square).then_inc(squared, 1)
                    act.wait_ge(var_done, 1)
                    nc.scalar.activation(m3, m2, ACT.Sqrt).then_inc(rooted, 1)

            def take(eng, j, bank):
                i = j // 2
                if j % 2 == 0:
                    return nc.scalar.activation(arena[:, RR + i, :], bank, ACT.Identity, bias=col("ln_b", i), scale=col("ln_w", i))
                return nc.vector.tensor_copy(arena[:, KK + i, :], bank)
            transposes(2 * KD, lambda j, b: (yt, vt)[j % 2][:, b, (j // 2) * P:(j // 2 + 1) * P], take)
            with phase("summed", "gated_", "added") as (block, summed, gated, added):
                @block.tensor
                def _(pe):
                    for m in range(KD):
                        if m >= 4:
                            pe.wait_ge(gated, m - 3)
                        nc.tensor.matmul(psum[:, m % 4, :], g2[:, m * P:(m + 1) * P], rows[:, 2, :], start=True, stop=False)
                        nc.tensor.matmul(psum[:, m % 4, :], g2[0:32, D + m * P:D + (m + 1) * P], rows[0:32, 3, :],
                                         start=False, stop=True).then_inc(summed, 1)

                @block.vector
                def _(dve):
                    for m in range(KD):
                        y = arena[:, RR + m, :]
                        nc.vector.tensor_tensor(y, y, arena[:, KK + m, :], ALU.add).then_inc(added, 1)
                        dve.wait_ge(added, m + 1)
                        dve.wait_ge(summed, m + 1)
                        nc.vector.tensor_tensor(y, psum[:, m % 4, :], y, ALU.mult).then_inc(gated, 1)
            add_projection("rwkv_o", lambda k: arena[:, RR + k, :])

        def attention(units, sb, pr, pt, bias, before):
            n = len(units)
            scale = HD ** -0.5
            mx, nm, sm, rc = (small[:, 4 * a:4 * a + 4] for a in range(4))
            with phase("scored", "biased", "maxed", "negated", "expd", "turned", "pt_kept", "pv_done", "inverted",
                       "out_done", "bias_ready", "bias_loaded") as \
                    (block, scored, biased, maxed, negated, expd, turned, pt_kept, pv_done, inverted, out_done,
                     bias_ready, bias_loaded):
                if bias:
                    before(block, bias_ready, bias_loaded, biased)

                @block.tensor
                def _(pe):
                    for i in range(n + 2):
                        if i < n:
                            if i >= 2:
                                pe.wait_ge(biased if bias else expd, i - 1)
                            nc.tensor.matmul(psum[:, i % 2, :], units[i][0], units[i][1], start=True, stop=True).then_inc(scored, 1)
                        if 1 <= i <= n:
                            u = i - 1
                            pe.wait_ge(expd, u + 1)
                            if u >= 2:
                                pe.wait_ge(pt_kept, u - 1)
                            for b in range(4):
                                tr = nc.tensor.transpose(psum[:, 2 + u % 2, b * P:(b + 1) * P],
                                                         pr[u % 2][:, b * P:(b + 1) * P], con("ident"))
                            tr.then_inc(turned, 1)
                        if i >= 2:
                            u = i - 2
                            pe.wait_ge(pt_kept, u + 1)
                            if u >= 2:
                                pe.wait_ge(out_done, u - 1)
                            for b in range(4):
                                mm = nc.tensor.matmul(psum[:, 4 + u % 2, 0:HD], pt[u % 2][:, b * P:(b + 1) * P],
                                                      units[u][2](b), start=(b == 0), stop=(b == 3))
                            mm.then_inc(pv_done, 1)

                @block.scalar
                def _(act):
                    for i in range(n + 1):
                        if i < n:
                            act.wait_ge(negated, i + 1)
                            if i >= 2:
                                act.wait_ge(turned, i - 1)
                            if i >= 4:
                                act.wait_ge(inverted, i - 3)
                            src = sb[i % 2] if bias else psum[:, i % 2, :]
                            nc.scalar.activation(pr[i % 2], src, ACT.Exp, bias=nm[:, i % 4:i % 4 + 1],
                                                 scale=1.0 if bias else scale,
                                                 accum_out=sm[:, i % 4:i % 4 + 1]).then_inc(expd, 1)
                        if i >= 1:
                            u = i - 1
                            act.wait_ge(turned, u + 1)
                            if u >= 2:
                                act.wait_ge(pv_done, u - 1)
                            nc.scalar.activation(pt[u % 2], psum[:, 2 + u % 2, :], ACT.Copy).then_inc(pt_kept, 1)

                @block.vector
                def _(dve):
                    for i in range(n + 3):
                        if i < n:
                            dve.wait_ge(scored, i + 1)
                            c4 = i % 4
                            if bias:
                                dve.wait_ge(bias_ready, i // 4 + 1)
                                if i >= 2:
                                    dve.wait_ge(expd, i - 1)
                                nc.vector.scalar_tensor_tensor(out=sb[i % 2], in0=psum[:, i % 2, :], scalar=scale,
                                                               in1=bias(i), op0=ALU.mult, op1=ALU.add).then_inc(biased, 1)
                                dve.wait_ge(biased, i + 1)
                                nc.vector.reduce_max(mx[:, c4:c4 + 1], sb[i % 2], axis=AX).then_inc(maxed, 1)
                            else:
                                nc.vector.reduce_max(mx[:, c4:c4 + 1], psum[:, i % 2, :], axis=AX).then_inc(maxed, 1)
                            dve.wait_ge(maxed, i + 1)
                            if i >= 4:
                                dve.wait_ge(expd, i - 3)
                            nc.vector.tensor_scalar(nm[:, c4:c4 + 1], mx[:, c4:c4 + 1], -1.0 if bias else -scale, None,
                                                    ALU.mult).then_inc(negated, 1)
                        if i >= 3:
                            u = i - 3
                            dve.wait_ge(expd, u + 1)
                            if u >= 4:
                                dve.wait_ge(out_done, u - 3)
                            nc.vector.reciprocal(rc[:, u % 4:u % 4 + 1], sm[:, u % 4:u % 4 + 1]).then_inc(inverted, 1)
                            dve.wait_ge(inverted, u + 1)
                            dve.wait_ge(pv_done, u + 1)
                            nc.vector.tensor_scalar(units[u][3], psum[:, 4 + u % 2, 0:HD], rc[:, u % 4:u % 4 + 1], None,
                                                    ALU.mult).then_inc(out_done, 1)

        def even_in():
            XN, Q, Z, XS = 0, 8, 20, 28
            name = "even_in"
            n0 = first_unit[name]
            rms_norm(lambda i: resid[:, i, :], lambda i: arena[:, XN + i, :], KD, lambda i: col("even_g", i))
            wdt = span(44, 1)[:, 0:8 * 32].rearrange("p (k n) -> p k n", k=KD)
            cw, cb = VECTOR_AT["ssd_cw"], VECTOR_AT["ssd_cb"]
            with phase("taken", "biased", "t0", "t1", "t2", "wdt_loaded", "dt_done", "dt_kept") as \
                    (block, taken, biased, tap0, tap1, tap3, wdt_loaded, dt_done, dt_kept):
                @block.sync
                def _(sp):
                    sp.dma_start(span(44, 1)[:, 0:8 * 32], dram["even_dt"]).then_inc(wdt_loaded, 16)
                    load_stream(sp, name)

                @block.tensor
                def _(pe):
                    products(pe, name, lambda k: arena[:, XN + k, :], taken)
                    pe.wait_ge(wdt_loaded, 16)
                    for c in range(NCH):
                        for k in range(KD):
                            mm = nc.tensor.matmul(psum[:, 4, c * 32:(c + 1) * 32], arena[:, XN + k, c * CH:(c + 1) * CH],
                                                  wdt[:, k, :], start=(k == 0), stop=(k == KD - 1))
                    mm.then_inc(dt_done, 1)

                @block.scalar
                def _(act):
                    def body_copy(m, bank, products_done):
                        products_done()
                        nc.scalar.activation(tile_of(arena, m + Q), psum[:, bank, :], ACT.Copy).then_inc(taken, 1)
                    bodies(act, name, body_copy, lo=0, hi=3)

                    def body_silu(m, bank, products_done):
                        products_done()
                        nc.scalar.activation(tile_of(arena, m + Q), psum[:, bank, :], ACT.Silu).then_inc(taken, 1)
                    bodies(act, name, body_silu, lo=3, hi=5)

                    def body_conv(m, bank, products_done):
                        products_done()
                        nc.scalar.activation(tile_of(arena, m + Q), psum[:, bank, :], ACT.Identity,
                                             bias=vec[:, bass.ds(m + (cb - 20), 1)],
                                             scale=vec[:, bass.ds(m + (cw + 32 - 20), 1)]).then_inc(biased, 1)
                    bodies(act, name, body_conv, lo=5, hi=9)

                @block.vector
                def _(dve):
                    with dve.Fori(5, 9) as g:
                        for r in range(R):
                            m = g * R + r
                            o = arena[:, bass.ds(m + Q, 1), :]
                            i = psum[:, r:r + 1, :]

                            def tap(j, dst, src, sem):
                                return nc.vector.scalar_tensor_tensor(
                                    out=o[:, :, dst].rearrange("p a t -> p (a t)"),
                                    in0=i[:, :, src].rearrange("p a t -> p (a t)"),
                                    scalar=vec[:, bass.ds(m + (cw + 16 * j - 20), 1)],
                                    in1=o[:, :, dst].rearrange("p a t -> p (a t)"),
                                    op0=ALU.mult, op1=ALU.add).then_inc(sem, 1)
                            dve.wait_ge(biased, m + (1 - 20))
                            tap(0, slice(2, T), slice(0, T - 2), tap0)
                            dve.wait_ge(tap0, m + (1 - 20))
                            tap(1, slice(1, T), slice(0, T - 1), tap1)
                            dve.wait_ge(tap1, m + (1 - 20))
                            tap(3, slice(0, T - 1), slice(1, T), taken)
                            dve.wait_ge(taken, m + 1)
                    dve.wait_ge(dt_done, 1)
                    nc.vector.tensor_tensor(rows[:, 3, 0:128].rearrange("p (c h) -> p c h", c=NCH),
                                            psum[:, 4, 0:128].rearrange("p (c h) -> p c h", c=NCH),
                                            col("dt_bias", 0, 32).unsqueeze(1).to_broadcast([P, NCH, 32]),
                                            ALU.add).then_inc(dt_kept, 1)
            U, DT, AC, TM = (rows[:, 3, 128 * a:128 * (a + 1)] for a in range(4))
            with phase("silu_", "abs_", "exp_", "ln_", "relu_", "dt", "expA", "a") as \
                    (block, silu_done, abs_done, exp_done, ln_done, relu_done, dt_ready, ea_done, a_ready):
                @block.scalar
                def _(act):
                    x = span(XS, 16)
                    nc.scalar.activation(x, x, ACT.Silu).then_inc(silu_done, 1)
                    nc.scalar.activation(TM, U, ACT.Abs).then_inc(abs_done, 1)
                    act.wait_ge(abs_done, 1)
                    nc.scalar.activation(DT, TM, ACT.Exp, scale=-1.0).then_inc(exp_done, 1)
                    act.wait_ge(exp_done, 1)
                    nc.scalar.activation(TM, DT, ACT.Ln, bias=con("ones", 1)).then_inc(ln_done, 1)
                    nc.scalar.activation(small[:, 0:32], col("A_log", 0, 32), ACT.Exp).then_inc(ea_done, 1)

                @block.vector
                def _(dve):
                    dve.wait_ge(ln_done, 1)
                    nc.vector.scalar_tensor_tensor(out=DT, in0=U, scalar=0.0, in1=TM, op0=ALU.max, op1=ALU.add).then_inc(dt_ready, 1)
                    dve.wait_ge(dt_ready, 1)
                    dve.wait_ge(ea_done, 1)
                    v = "p (c h) -> p c h"
                    nc.vector.scalar_tensor_tensor(out=U.rearrange(v, c=NCH), in0=DT.rearrange(v, c=NCH), scalar=-1.0,
                                                   in1=small[:, 0:32].unsqueeze(1).to_broadcast([P, NCH, 32]),
                                                   op0=ALU.mult, op1=ALU.mult).then_inc(a_ready, 1)
            with phase("summed", "kept", "turned", "t_kept") as (block, summed, kept, turned, t_kept):
                @block.tensor
                def _(pe):
                    for c in range(NCH):
                        for back in range(2):
                            o = psum[:, 0, c * 32 + back * 16:c * 32 + back * 16 + 16]
                            others = range(c + 1, NCH) if back else range(c)
                            for n, i in enumerate(list(others) + [c]):
                                lhs = con("ones") if i != c else (con("ge") if back else con("le"))
                                mm = nc.tensor.matmul(o, lhs, U[:, i * 32 + back * 16:i * 32 + back * 16 + 16],
                                                      start=(n == 0), stop=(i == c))
                    mm.then_inc(summed, 1)
                    pe.wait_ge(kept, 1)
                    for c in range(NCH):
                        tr = nc.tensor.transpose(psum[0:32, 1, c * P:(c + 1) * P], AC[:, c * 32:(c + 1) * 32], con("ident"))
                    tr.then_inc(turned, 1)

                @block.vector
                def _(dve):
                    dve.wait_ge(summed, 1)
                    nc.vector.tensor_copy(AC, psum[:, 0, 0:128]).then_inc(kept, 1)
                    dve.wait_ge(turned, 1)
                    nc.vector.tensor_copy(rows[0:32, 2, :], psum[0:32, 1, :]).then_inc(t_kept, 1)

        def ssd():
            XN, Z, XS, BT, CT, XT = 0, 20, 28, 36, 40, 44
            DT, AC = rows[:, 3, 128:256], rows[:, 3, 256:384]
            xt = span(XT, 8).rearrange("p (c f) -> p c f", c=NCH)
            yt = span(XN, 8).rearrange("p (c f) -> p c f", c=NCH)
            to_tokens(lambda j: arena[:, XS + j, :], KD, xt)
            W5 = 5 * P
            bcm = span(52, 5).rearrange("p (i f) -> p i f", i=4)
            for grp in range(4):
                with phase("bc_done", "bc_kept") as (block, bc_done, bc_kept):
                    @block.tensor
                    def _(pe):
                        for i in range(4):
                            nc.tensor.matmul(psum[:, i, :], arena[:, BT + grp, i * P:(i + 1) * P], arena[:, CT + grp, :],
                                             start=True, stop=True).then_inc(bc_done, 1)

                    @block.vector
                    def _(dve):
                        for i in range(4):
                            dve.wait_ge(bc_done, i + 1)
                            s = slice(i * P, (i + 1) * P)
                            if i:
                                nc.vector.tensor_copy(bcm[:, i, 0:i * P], psum[:, i, 0:i * P]).then_inc(bc_kept, 1)
                            if i < 3:
                                nc.vector.tensor_copy(bcm[:, i, (i + 2) * P:W5], psum[:, i, (i + 1) * P:T]).then_inc(bc_kept, 1)
                            nc.vector.tensor_tensor(bcm[:, i, i * P:(i + 1) * P], psum[:, i, s], con("ge"), ALU.mult).then_inc(bc_kept, 1)
                            nc.vector.tensor_tensor(bcm[:, i, (i + 1) * P:(i + 2) * P], psum[:, i, s], con("le"), ALU.mult).then_inc(bc_kept, 1)
                with phase("cast", "argued", "expd", "weighted", "y_done", "y_kept") as \
                        (block, spread_done, argued, expd, weighted, y_done, y_kept):
                    gs = span(57, 7)[:, 0:5 * W5].rearrange("p (i f) -> p i f", i=5)

                    def slot(u):
                        return gs[:, u % 5, :]

                    @block.tensor
                    def _(pe):
                        def spread(hh):
                            h = grp * 4 + hh
                            if hh >= 2:
                                pe.wait_ge(argued, 8 * (hh - 1))
                            for back in range(2):
                                mm = nc.tensor.matmul(psum[:, 2 * (hh % 2) + back, :],
                                                      con("ident", 1, h + 16 * back, 32).to_broadcast([32, P]),
                                                      rows[0:32, 2, :], start=True, stop=True)
                            mm.then_inc(spread_done, 1)
                        spread(0)
                        for hh in range(4):
                            h = grp * 4 + hh
                            if hh < 3:
                                spread(hh + 1)
                            if hh >= 1:
                                pe.wait_ge(y_kept, hh)
                            for i in range(4):
                                pe.wait_ge(weighted, 2 * (4 * hh + i) + 2)
                                g = slot(4 * hh + i)
                                x = xt[:, i, h * HD:(h + 1) * HD]
                                for j in range(4):
                                    if j <= i:
                                        mm = nc.tensor.matmul(psum[:, 4 + j, 0:HD], g[:, j * P:(j + 1) * P], x,
                                                              start=(i == 0), stop=(i == 3 and j < 3))
                                    if j >= i:
                                        mm = nc.tensor.matmul(psum[:, 4 + j, 0:HD], g[:, (j + 1) * P:(j + 2) * P], x,
                                                              start=(i == 0 and j > 0), stop=(i == 3))
                                mm.then_inc(y_done, 1)

                    @block.vector
                    def _(dve):
                        def argue(u):
                            hh, i = u // 4, u % 4
                            h = grp * 4 + hh
                            if u >= 5:
                                dve.wait_ge(y_done, u - 4)
                            dve.wait_ge(spread_done, hh + 1)
                            g = slot(u)
                            nc.vector.tensor_scalar(g[:, 0:(i + 1) * P], psum[:, 2 * (hh % 2) + 1, 0:(i + 1) * P],
                                                    AC[:, i * 32 + 16 + h:i * 32 + 17 + h], 0.0, ALU.subtract, ALU.min).then_inc(argued, 1)
                            nc.vector.tensor_scalar(g[:, (i + 1) * P:W5], psum[:, 2 * (hh % 2), i * P:T],
                                                    AC[:, i * 32 + h:i * 32 + 1 + h], 0.0, ALU.subtract, ALU.min).then_inc(argued, 1)

                        def weigh(u):
                            hh, i = u // 4, u % 4
                            h = grp * 4 + hh
                            g = slot(u)
                            dve.wait_ge(expd, u + 1)
                            for lo, hi, d in ((0, (i + 1) * P, 16 + h), ((i + 1) * P, W5, h)):
                                nc.vector.scalar_tensor_tensor(out=g[:, lo:hi], in0=g[:, lo:hi],
                                                               scalar=DT[:, i * 32 + d:i * 32 + d + 1], in1=bcm[:, i, lo:hi],
                                                               op0=ALU.mult, op1=ALU.mult).then_inc(weighted, 1)
                        argue(0)
                        for u in range(16):
                            if u < 15:
                                argue(u + 1)
                            weigh(u)

                    @block.scalar
                    def _(act):
                        def keep(hh):
                            h = grp * 4 + hh
                            act.wait_ge(y_done, 4 * hh + 4)
                            nc.scalar.activation(yt[:, :, h * HD:(h + 1) * HD], psum[:, 4:8, 0:HD], ACT.Copy).then_inc(y_kept, 1)
                        for u in range(16):
                            act.wait_ge(argued, 2 * u + 2)
                            nc.scalar.activation(slot(u), slot(u), ACT.Exp).then_inc(expd, 1)
                            if u % 4 == 1 and u > 4:
                                keep(u // 4 - 1)
                        keep(3)
            def take(eng, j, bank):
                x = arena[:, XS + j, :]
                return nc.vector.scalar_tensor_tensor(out=x, in0=x, scalar=col("ssd_D", j), in1=bank, op0=ALU.mult, op1=ALU.add)
            transposes(KD, lambda j, b: yt[:, b, j * P:(j + 1) * P], take, engines=("vector",))
            with phase("gated_") as (block, gated):
                @block.vector
                def _(dve):
                    nc.vector.tensor_tensor(span(XS, 8), span(XS, 8), span(Z, 8), ALU.mult).then_inc(gated, 1)
            norm(lambda i: arena[:, XS + i, :], lambda i: arena[:, XS + i, :], KD, 4,
                 lambda i: con("group_rows", 4, 3 - i // 2), lambda i: con("ident", 1, i // 2, 4).to_broadcast([4, P]),
                 lambda i: col("ssd_g", i), 1.0 / 256, 1e-6, ALU.add)

        def neighbourhood():
            Q, K, V, VT, OT = 8, 12, 16, 48, 44
            norm(lambda i: arena[:, Q + i, :], lambda i: arena[:, Q + i, :], 8, 32, head_sums, head_spread,
                 lambda i: col("na_qk", i), 1.0 / HD, 1e-6, ALU.add)
            vt = span(VT, 4).rearrange("p (c f) -> p c f", c=NCH)
            to_tokens(lambda j: arena[:, V + j, :], 4, vt)
            ot = span(OT, 4).rearrange("p (c f) -> p c f", c=NCH)
            win = [span(52, 2)[:, 0:14 * 64], span(54, 2)[:, 0:14 * 64]]
            units = []
            for h in range(8):
                i, ps = h // 2, slice((h % 2) * HD, (h % 2 + 1) * HD)
                for qt in range(4):
                    units.append((arena[ps, Q + i, qt * P:(qt + 1) * P], arena[ps, K + i, :],
                                  lambda b, h=h: vt[:, b, h * HD:(h + 1) * HD], ot[:, qt, h * HD:(h + 1) * HD]))

            def bias(u):
                lo = (6 - 2 * (u % 4)) * 64
                return win[(u // 4) % 2][:, lo:lo + T]

            def before(block, bias_ready, bias_loaded, biased):
                @block.sync
                def _(sp):
                    for h in range(8):
                        if h >= 2:
                            sp.wait_ge(biased, 4 * (h - 1))
                        if h >= 1:
                            sp.wait_ge(bias_loaded, 32 * h)
                        w = win[h % 2].rearrange("p (d k) -> p d k", k=64)
                        for rr in range(2):
                            sp.dma_start(w[rr * 64:(rr + 1) * 64, :, :],
                                         dram["na_bias"][h, 1 - rr:15 - rr, :, :].rearrange("d c k -> c d k"))\
                                .then_inc(bias_loaded, 16)

                @block.gpsimd
                def _(pool):
                    for h in range(8):
                        pool.wait_ge(bias_loaded, 32 * (h + 1))
                        w = win[h % 2].rearrange("p (d k) -> p d k", k=64)
                        nc.gpsimd.tensor_tensor(w, w, con("window", 64).unsqueeze(1).to_broadcast([P, 14, 64]),
                                                ALU.add).then_inc(bias_ready, 1)
            attention(units, [arena[:, 56, :], arena[:, 57, :]], [arena[:, 58, :], arena[:, 59, :]],
                      [arena[:, 60, :], arena[:, 61, :]], bias, before)
            transposes(4, lambda j, b: ot[:, b, j * P:(j + 1) * P],
                       lambda eng, j, bank: copy_on(eng, arena[:, Q + j, :], bank))

        def gqa():
            XN, Q, K, V, COS, SIN, VT, OT = 0, 8, 16, 18, 20, 21, 22, 24
            rms_norm(lambda i: resid[:, i, :], lambda i: arena[:, XN + i, :], KD, lambda i: col("odd_g", i))
            with phase("taken", "rope_loaded") as (block, taken, rope_loaded):
                @block.sync
                def _(sp):
                    sp.dma_start(span(COS, 2), dram["rope"]).then_inc(rope_loaded, 16)
                    load_stream(sp, "qkv")
                    sp.wait_ge(rope_loaded, 16)

                @block.tensor
                def _(pe):
                    products(pe, "qkv", lambda k: arena[:, XN + k, :], taken)

                @block.scalar
                def _(act):
                    def body(m, bank, products_done):
                        products_done()
                        nc.scalar.activation(tile_of(arena, m + Q), psum[:, bank, :], ACT.Copy).then_inc(taken, 1)
                    bodies(act, "qkv", body)
            norm(lambda i: arena[:, Q + i, :], lambda i: arena[:, Q + i, :], 10, 32, head_sums, head_spread,
                 lambda i: col("gqa_qk", i), 1.0 / HD, 1e-6, ALU.add)
            with phase("rotated", "sin_done", "cos_done", "roped") as (block, rotated, sin_done, cos_done, roped):
                @block.tensor
                def _(pe):
                    for i in range(10):
                        if i >= 4:
                            pe.wait_ge(sin_done, i - 3)
                        nc.tensor.matmul(psum[:, i % 4, :], con("rot"), arena[:, Q + i, :], start=True, stop=True).then_inc(rotated, 1)

                @block.vector
                def _(dve):
                    for i in range(10):
                        dve.wait_ge(rotated, i + 1)
                        if i >= 4:
                            dve.wait_ge(roped, i - 3)
                        x = arena[:, Q + i, :]
                        nc.vector.tensor_tensor(work[:, i % 4, :], psum[:, i % 4, :], arena[:, SIN, :], ALU.mult).then_inc(sin_done, 1)
                        nc.vector.tensor_tensor(x, x, arena[:, COS, :], ALU.mult).then_inc(cos_done, 1)
                        dve.wait_ge(sin_done, i + 1)
                        dve.wait_ge(cos_done, i + 1)
                        nc.vector.tensor_tensor(x, x, work[:, i % 4, :], ALU.add).then_inc(roped, 1)
            vt = span(VT, 2).rearrange("p (c f) -> p c f", c=NCH)
            to_tokens(lambda j: arena[:, V + j, :], 2, vt)
            ot = span(OT, 8).rearrange("p (c f) -> p c f", c=NCH)
            units = []
            for n in range(NH):
                j, e = n // 2, n % 2
                h = (j if j < 4 else j + 4) + 4 * e
                kv, ps = h // 4, slice(e * HD, (e + 1) * HD)
                for qt in range(4):
                    units.append((arena[ps, Q + j, qt * P:(qt + 1) * P], arena[ps, K + kv // 2, :],
                                  lambda b, kv=kv: vt[:, b, kv * HD:(kv + 1) * HD], ot[:, qt, h * HD:(h + 1) * HD]))
            attention(units, None, [arena[:, 32, :], arena[:, 33, :]], [arena[:, 34, :], arena[:, 35, :]], None, None)
            transposes(KD, lambda j, b: ot[:, b, j * P:(j + 1) * P],
                       lambda eng, j, bank: copy_on(eng, arena[:, Q + j, :], bank))
            add_projection("odd_out", lambda k: arena[:, Q + k, :])

        def final_norm():
            rms_norm(lambda i: resid[:, i, :], lambda i: resid[:, i, :], KD, lambda i: col("final_g", i))

        def even():
            even_in()
            ssd()
            neighbourhood()
            add_projection("even_out", lambda k: arena[:, 8 + k, :] if k < 4 else arena[:, 28 + k - 4, :])

        stages = [sgu, lambda: conv_ffn(0), rwkv, lambda: conv_ffn(1), final_norm, even,
                  lambda: swiglu(0), gqa, lambda: swiglu(1)]
        for n, stage in enumerate(stages):
            if first <= n < last:
                stage()
        with phase("stored") as (block, stored):
            @block.sync
            def _(sp):
                sp.dma_start(out, resid[:, :, :]).then_inc(stored, 16)
                sp.wait_ge(stored, 16)


def constants():
    i = np.arange(P)
    p, f = i[:, None], i[None, :]
    levels = []
    for b in (1, 2, 4, 8, 16, 32, 64):
        levels.append(((f // b) % 2 == 1) & (p // b == f // b - 1))
    rot = np.zeros((P, P), np.float32)
    even = np.arange(0, P, 2)
    rot[even + 1, even] = -1.0
    rot[even, even + 1] = 1.0
    c = np.arange(HD)
    start = np.clip(c - 8, 0, HD - 16)
    inside = (c[None, :] >= start[:, None]) & (c[None, :] < start[:, None] + 16)
    window = np.where(np.concatenate([inside, inside]), 0.0, -1e30)
    head_rows = np.zeros((P, 64), np.float32)
    head_rows[i, 30 + i // HD] = 1.0
    head_cols = np.zeros((P, 10, P), np.float32)
    for t in range(10):
        for e in range(2):
            head_cols[2 * t + e, t, e * HD:(e + 1) * HD] = 1.0
    halves = np.zeros((P, 2), np.float32)
    halves[i, i // HD] = 1.0
    group_rows = np.zeros((P, 7), np.float32)
    group_rows[:, 3] = 1.0
    parts = dict(ident=np.eye(P), le=p <= f, lt=p < f, ge=p >= f, levels=np.concatenate(levels, 1),
                 pair_low=levels[0].T, ones=np.ones((P, P)), rot=rot, window=window, head_rows=head_rows,
                 head_cols=head_cols.reshape(P, -1), halves=halves, group_rows=group_rows)
    return np.concatenate([np.asarray(parts[n], np.float32) for n, _ in CONST_PARTS], 1)


def rope_tables():
    t = np.arange(T)
    freqs = (10000.0 ** (-np.arange(0, 32, 2, dtype=np.float32) / np.float32(32))).astype(np.float32)
    ang = np.concatenate([(t // 64).astype(np.float32)[:, None] * freqs, (t % 64).astype(np.float32)[:, None] * freqs], 1)
    def table(x):
        x = np.repeat(x.T, 2, axis=0).astype(np.float32)
        return np.concatenate([x, x], 0)
    return np.concatenate([table(np.cos(ang)), table(np.sin(ang))], 1)


def layouts(a):
    def blocks(w, nk=None, order=None):
        k, m = w.shape
        w = w.reshape(k // P, P, m // P, P).transpose(2, 1, 0, 3)
        if order is not None:
            w = w[order]
        nk = nk or k // P
        w = w.reshape(m // P, P, k // P // nk, nk, P).transpose(0, 2, 1, 3, 4)
        return np.ascontiguousarray(w.reshape(-1, P, nk * P))

    def cols(v):
        return v.reshape(-1, P).T

    def turns(n):
        return np.stack([np.arange(n), np.arange(n) + n], 1).reshape(-1)

    d = {}
    d["x"] = np.ascontiguousarray(a["x"][0].T.reshape(KD, P, T).transpose(1, 0, 2))
    d["const"] = constants()
    d["rope"] = rope_tables()
    pair = turns(KF)
    d["sgu_in"] = blocks(a["sgu_w_in"][0])
    d["sgu_out"] = blocks(a["sgu_w_out"][0])
    d["sgu_ws"] = np.ascontiguousarray(a["sgu_w_s"][0].transpose(2, 0, 1).reshape(P, -1))
    for l in range(2):
        d[f"up{l}"] = blocks(a["ffn_w_up"][l], order=pair)
        d[f"down{l}"] = blocks(a["ffn_w_down"][l], 11)
        d[f"up{l + 2}"] = blocks(a["ffn_w13_2"][l], order=pair)
        d[f"down{l + 2}"] = blocks(a["ffn_w2_2"][l], 11)
    for n in "rkvo":
        d[f"rwkv_{n}"] = blocks(a[f"rwkv_w_{n}"][0])
    lora1 = np.concatenate([a["rwkv_w1"][0], a["rwkv_a1"][0], a["rwkv_g1"][0]], 1)
    d["lora1"] = np.ascontiguousarray(lora1.reshape(KD, P, 288).transpose(1, 0, 2).reshape(P, -1))
    d["lora_w2"] = a["rwkv_w2"][0]
    d["lora_a2"] = a["rwkv_a2"][0]
    d["lora_g2"] = a["rwkv_g2"][0]
    even = a["even_w_in_2"][0]
    d["even_in"] = blocks(np.ascontiguousarray(even[:, :4608]))
    d["even_dt"] = np.ascontiguousarray(even[:, 4608:].reshape(KD, P, 32).transpose(1, 0, 2).reshape(P, -1))
    d["even_out"] = blocks(a["even_w_out_2"][0])
    heads = [(j if j < 4 else j + 4) + 4 * e for j in range(8) for e in range(2)]
    qcols = np.concatenate([np.arange(h * HD, (h + 1) * HD) for h in heads] + [np.arange(1024, 1536)])
    d["qkv"] = blocks(a["odd_w_qkv_2"][0][:, qcols])
    d["odd_out"] = blocks(a["odd_w_out_2"][0])
    rpb = np.pad(a["na_rel_bias_2"][0], ((0, 0), (0, 0), (48, 48)))
    c = np.arange(HD)
    d["na_bias"] = np.ascontiguousarray(rpb[:, :, 63 + c[None, :] - c[:, None]])
    spread = lambda v: np.broadcast_to(v, (P, v.size))
    twice = lambda v: np.concatenate([v, v])[:, None]
    vectors = dict(
        mix_g=cols(a["norm_mix_g"]), ffn_g=cols(a["norm_ffn_g"]), final_g=cols(a["norm_final_g"]),
        sgu_b=cols(a["sgu_b_in"]), sgu_gv=cols(a["sgu_g_v"]), sgu_bs=a["sgu_b_s"][0].T, mu=cols(a["rwkv_mu"]),
        w0=cols(a["rwkv_w0"]), a0=cols(a["rwkv_a0"]), k_k=cols(a["rwkv_k_k"]), k_a=cols(a["rwkv_k_a"]),
        r_k=cols(a["rwkv_r_k"]), ln_w=cols(a["rwkv_ln_w"]), ln_b=cols(a["rwkv_ln_b"]),
        conv_w=np.concatenate([cols(a["ffn_conv_w"][l, j])[:, pair] for l in range(2) for j in range(3)], 1),
        conv_b=np.concatenate([cols(a["ffn_conv_b"][l])[:, pair] for l in range(2)], 1),
        even_g=cols(a["even_mix_norm_2"]), ssd_cw=cols(a["ssd_conv_w_2"]), ssd_cb=cols(a["ssd_conv_b_2"]),
        ssd_D=cols(np.repeat(a["ssd_D_2"][0], HD)), ssd_g=cols(a["ssd_out_norm_2"]),
        dt_bias=spread(a["ssd_dt_bias_2"].reshape(-1)), A_log=spread(a["ssd_A_log_2"].reshape(-1)),
        na_qk=np.concatenate([twice(a["na_q_norm_2"][0])] * 4 + [twice(a["na_k_norm_2"][0])] * 4, 1),
        odd_g=cols(a["odd_mix_norm_2"]),
        gqa_qk=np.concatenate([twice(a["gqa_q_norm_2"][0])] * 8 + [twice(a["gqa_k_norm_2"][0])] * 2, 1),
        ffn2_g=cols(a["ffn_norm_2"]))
    d["vec"] = np.ascontiguousarray(np.concatenate([vectors[n] for n, _ in VECTOR_PARTS], 1))
    return d


def kernel(**inputs):
    import concourse.bacc as bacc
    from concourse.bass_utils import run_bass_kernel_spmd

    arrays = layouts({k: np.asarray(v) for k, v in inputs.items()})
    nc = bacc.Bacc("TRN2", target_bir_lowering=False, num_devices=1)
    dram = {k: nc.dram_tensor(f"in_{k}", v.shape, F32, kind="ExternalInput").ap() for k, v in arrays.items()}
    out = nc.dram_tensor("out", (P, KD, T), F32, kind="ExternalOutput").ap()
    build(nc, dram, out)
    result = run_bass_kernel_spmd(nc, [{f"in_{k}": v for k, v in arrays.items()}], core_ids=[0])
    y = result.results[0]["out"]
    return np.ascontiguousarray(y.transpose(1, 0, 2).reshape(D, T).T)[None]
```

```python
from contextlib import ExitStack, contextmanager

import numpy as np

import concourse.bass as bass
from concourse import mybir

F32 = mybir.dt.float32
F32R = mybir.dt.float32r
ACT = mybir.ActivationFunctionType
ALU = mybir.AluOpType
AX = mybir.AxisListType.X

P = 128
T = 512
D = 1024
KD = D // P
CH = 128
NCH = T // CH
FFN = 2816
KF = FFN // P
HD = 64
NH = 16
R = 4
HIGHS = 2
SLOT_BLOCKS = 8
EXP_HALF = float(np.exp(-0.5))

PARTS = {8: [(0, 8)], 12: [(0, 6), (6, 6)], 22: [(0, 6), (6, 6), (12, 5), (17, 5)]}
CONST_PARTS = [("ident", P), ("le", P), ("lt", P), ("ge", P), ("levels", 7 * P), ("pair_low", P),
               ("ones", P), ("rot", P), ("window", HD), ("head_rows", 64), ("head_cols", 10 * P), ("halves", 2), ("group_rows", 7)]
VECTOR_PARTS = [("mix_g", 16), ("ffn_g", 16), ("final_g", 8), ("sgu_b", 16), ("sgu_gv", 8), ("sgu_bs", 16),
                ("mu", 48), ("w0", 8), ("a0", 8), ("k_k", 8), ("k_a", 8), ("r_k", 8), ("ln_w", 8), ("ln_b", 8),
                ("conv_w", 264), ("conv_b", 88), ("even_g", 8), ("ssd_cw", 64), ("ssd_cb", 16),
                ("ssd_D", 8), ("ssd_g", 8), ("dt_bias", 32), ("A_log", 32), ("na_qk", 8), ("odd_g", 8),
                ("gqa_qk", 10), ("ffn2_g", 16)]


def places(parts):
    at, out = 0, {}
    for name, n in parts:
        out[name] = at
        at += n
    return out, at


CONST_AT, CONST_COLS = places(CONST_PARTS)
VECTOR_AT, VECTOR_COLS = places(VECTOR_PARTS)


def build(nc, dram, out, first=0, last=9):
    with ExitStack() as whole:
        def sbuf(name, shape):
            return whole.enter_context(nc.sbuf_tensor(name, shape, F32))

        def alias(name, at, shape):
            return nc.alloc_sbuf_tensor_at(name, shape, F32R, offset=at)

        arena_at = -(-nc.sbuf_base // 32) * 32
        arena = sbuf("arena", [P, 64, T])
        resid = sbuf("resid", [P, KD, T])
        ring_at = -(-nc.sbuf_base // 32) * 32
        ring = sbuf("ring", [P, R, SLOT_BLOCKS * P])
        ring_low = alias("ring_low", ring_at, [P, R, SLOT_BLOCKS * P])
        high_r = whole.enter_context(nc.sbuf_tensor("high_r", [P, HIGHS, SLOT_BLOCKS * P], F32R))
        const = sbuf("const", [P, CONST_COLS])
        vec = sbuf("vec", [P, VECTOR_COLS])
        work = sbuf("work", [P, 4, T])
        rows = sbuf("rows", [P, 4, T])
        state = sbuf("state", [P, KD, HD])
        small = sbuf("small", [P, 192])
        psum = whole.enter_context(nc.psum_tensor("psum", [P, 8, T], F32))

        slot_filled = [whole.enter_context(nc.semaphore(f"slot_filled{r}")) for r in range(R)]
        unit_done = whole.enter_context(nc.semaphore("unit_done"))
        unit_high = whole.enter_context(nc.semaphore("unit_high"))
        unit_low = whole.enter_context(nc.semaphore("unit_low"))

        phases = [0]

        @contextmanager
        def phase(*names):
            sems = [nc.alloc_semaphore(f"{n}_{phases[0]}") for n in names]
            phases[0] += 1
            with nc.Block() as block:
                yield block, *sems
            for s in sems:
                nc.gpsimd.sem_clear(s)
                nc.release_semaphore(s)

        seen = {}

        def rounded(start, n=8):
            if (start, n) not in seen:
                seen[start, n] = alias(f"rounded_{start}_{n}", arena_at + start * T * 4, [P, n, T])
            return seen[start, n]

        def two_parts(high_at, low_at, n=8):
            return lambda k: (rounded(high_at, n)[:, k, :], rounded(low_at, n)[:, k, :])

        def con(name, width=P, off=0, rows_=P):
            a = CONST_AT[name] + off
            return const[0:rows_, a:a + width]

        def col(name, i=0, n=1, rows_=slice(0, P)):
            a = VECTOR_AT[name] + i
            if isinstance(i, int):
                return vec[rows_, a:a + n]
            return vec[rows_, bass.ds(a, n)]

        def tile_of(x, i):
            if isinstance(i, int):
                return x[:, i, :]
            return x[:, bass.ds(i, 1), :].rearrange("p a t -> p (a t)")

        def flat(x):
            return x.rearrange("p a t -> p (a t)")

        def span(i, n):
            return flat(arena[:, i:i + n, :])

        ORDER = ["sgu_in", "sgu_out", "up0", "down0", "rwkv_r", "rwkv_k", "rwkv_v", "rwkv_o", "up1", "down1",
                 "even_in", "even_out", "up2", "down2", "qkv", "odd_out", "up3", "down3"]
        stage_of = dict(sgu_in=0, sgu_out=0, up0=1, down0=1, rwkv_r=2, rwkv_k=2, rwkv_v=2, rwkv_o=2, up1=3, down1=3, even_in=5, even_out=5, up2=6, down2=6, qkv=7, odd_out=7, up3=8, down3=8)
        ORDER = [n for n in ORDER if first <= stage_of[n] < last]
        first_unit, n_units = {}, 0
        for name in ORDER:
            first_unit[name] = n_units
            n_units += dram[name].shape[0] * len(PARTS[dram[name].shape[2] // P])

        class Stream:
            def __init__(self, name):
                self.name, self.w = name, dram[name]
                self.parts = PARTS[self.w.shape[2] // P]
                self.units = self.w.shape[0] * len(self.parts)
                self.first = first_unit[name]
                self.body = max(R, 2 * len(self.parts))
                self.groups = self.units // self.body
                self.tiles = self.body // len(self.parts)

            def place(self, r):
                m, part = divmod(r, len(self.parts))
                k0, nk = self.parts[part]
                return m, k0, nk, part == len(self.parts) - 1

        def loop(eng, groups, body):
            body(0)
            if groups > 2:
                with eng.Fori(1, groups - 1) as g:
                    body(g)
            if groups > 1:
                body(groups - 1)

        def wait(eng, sem, value):
            if not isinstance(value, int) or value > 0:
                eng.wait_ge(sem, value)

        def load_unit(sp, st, g, r):
            m, k0, nk, _ = st.place(r)
            if isinstance(g, int):
                src = st.w[g * st.tiles + m]
            else:
                src = st.w[bass.ds(g * st.tiles + m, 1)].rearrange("a p n -> (a p) n")
            sp.dma_start(ring[:, r % R, 0:nk * P], src[:, k0 * P:(k0 + nk) * P]).then_inc(slot_filled[r % R], 16)

        def load_stream(sp, name):
            st = Stream(name)

            def body(g):
                for r in range(st.body):
                    if isinstance(g, int) and g == 0 and r < R:
                        continue
                    sp.wait_ge(unit_done, g * st.body + (st.first - R + r + 1))
                    load_unit(sp, st, g, r)
            loop(sp, st.groups, body)
            at = ORDER.index(name) + 1
            if at < len(ORDER):
                for r in range(R):
                    sp.wait_ge(unit_done, st.first + st.units - R + r + 1)
                    load_unit(sp, Stream(ORDER[at]), 0, r)

        def products(pe, name, rhs, taken, before=None):
            st = Stream(name)

            def body(g):
                for r in range(st.body):
                    m, k0, nk, last = st.place(r)
                    wait(pe, unit_low, g * st.body + (st.first + r + 1))
                    if k0 == 0:
                        wait(pe, taken, g * st.tiles + (m + 1 - st.tiles))
                    for k in range(nk):
                        x_high, x_low = rhs(k0 + k)
                        blk = slice(k * P, (k + 1) * P)
                        end = last and k == nk - 1
                        nc.tensor.matmul(psum[:, m, :], high_r[:, r % HIGHS, blk], x_high,
                                         start=(k0 + k == 0), stop=False)
                        nc.tensor.matmul(psum[:, m, :], high_r[:, r % HIGHS, blk], x_low,
                                         start=False, stop=False)
                        mm = nc.tensor.matmul(psum[:, m, :], ring_low[:, r % R, blk], x_high,
                                              start=False, stop=end)
                    mm.then_inc(unit_done, 1)
            if before:
                before(pe)
            loop(pe, st.groups, body)

        def split_high(act, st, g, r):
            nk = st.place(r % st.body)[2]
            n = g * st.body + (st.first + r)
            turn = g * (16 * st.body // R) + 16 * ((st.first + r) // R + 1)
            act.wait_ge(slot_filled[r % R], turn)
            wait(act, unit_done, n + (1 - HIGHS))
            nc.scalar.activation(high_r[:, r % HIGHS, 0:nk * P], ring[:, r % R, 0:nk * P], ACT.Copy).then_inc(unit_high, 1)

        def split_low(dve, st, g, r):
            nk = st.place(r % st.body)[2]
            dve.wait_ge(unit_high, g * st.body + (st.first + r + 1))
            nc.vector.tensor_tensor(ring_low[:, r % R, 0:nk * P], ring[:, r % R, 0:nk * P],
                                    high_r[:, r % HIGHS, 0:nk * P].bitcast(F32), ALU.subtract).then_inc(unit_low, 1)

        def split_and_read(eng, name, split, read=None, groups=None):
            st = Stream(name)

            def body_of(read, last_group):
                def body(g):
                    for r in range(st.body):
                        if not (isinstance(g, int) and g == st.groups - 1 and r == st.body - 1):
                            split(eng, st, g, r + 1)
                        m, _, _, last = st.place(r)
                        if last and read:
                            read(g, m, lambda: eng.wait_ge(unit_done, g * st.body + (st.first + r + 1)))
                return body
            split(eng, st, 0, 0)
            for read_, lo, hi in groups or [(read, 0, st.groups)]:
                body = body_of(read_, None)
                g = lo
                if g == 0 or hi - lo == 1:
                    body(g)
                    g += 1
                end = hi - 1 if hi == st.groups else hi
                if end > g:
                    with eng.Fori(g, end) as i:
                        body(i)
                if end < hi and end >= g:
                    body(end)

        def add_projection(name, rhs):
            with phase("taken") as (block, taken):
                @block.sync
                def _(sp):
                    load_stream(sp, name)

                @block.tensor
                def _(pe):
                    products(pe, name, rhs, taken)

                @block.scalar
                def _(act):
                    split_and_read(act, name, split_high)

                @block.vector
                def _(dve):
                    tiles = Stream(name).tiles

                    def read(g, m, done):
                        done()
                        x = tile_of(resid, g * tiles + m)
                        nc.vector.tensor_tensor(x, psum[:, m, :], x, ALU.add).then_inc(taken, 1)
                    split_and_read(dve, name, split_low, read)

        def split_tiles(n, src, parts):
            with phase("high_done", "low_done") as (block, high_done, low_done):
                @block.scalar
                def _(act):
                    for i in range(n):
                        nc.scalar.activation(parts(i)[0], src(i), ACT.Copy).then_inc(high_done, 1)

                @block.vector
                def _(dve):
                    for i in range(n):
                        dve.wait_ge(high_done, i + 1)
                        nc.vector.tensor_tensor(parts(i)[1], src(i), parts(i)[0].bitcast(F32),
                                                ALU.subtract).then_inc(low_done, 1)

        def norm(src, dst, n, groups, gather, spread, gain, scale, guard, guard_op, parts=None):
            with phase("squared", "summed", "guarded", "rooted", "inverted", "spread_done", "scaled", "high_done",
                       "low_done") as \
                    (block, squared, summed, guarded, rooted, inverted, spread_done, scaled, high_done, low_done):
                one = groups == 1

                @block.scalar
                def _(act):
                    for i in range(n):
                        if i >= 4:
                            act.wait_ge(summed, i - 3)
                        nc.scalar.activation(work[:, i % 4, :], src(i), ACT.Square).then_inc(squared, 1)
                    act.wait_ge(guarded, 1)
                    nc.scalar.activation(rows[0:groups, 1, :], rows[0:groups, 0, :], ACT.Sqrt).then_inc(rooted, 1)
                    for i in range(n if parts else 0):
                        act.wait_ge(scaled, i + 1)
                        nc.scalar.activation(parts(i)[0], rows[:, 2 + i % 2, :], ACT.Copy).then_inc(high_done, 1)

                @block.tensor
                def _(pe):
                    for i in range(n):
                        pe.wait_ge(squared, i + 1)
                        nc.tensor.matmul(psum[0:groups, 4, :], gather(i), work[:, i % 4, :],
                                         start=(i == 0), stop=(i == n - 1)).then_inc(summed, 1)
                    pe.wait_ge(inverted, 1)
                    for i in range(1 if one else n):
                        if i >= 2:
                            pe.wait_ge(scaled, i - 1)
                        nc.tensor.matmul(psum[:, 5 + i % 2, :], spread(i), rows[0:groups, 0, :],
                                         start=True, stop=True).then_inc(spread_done, 1)

                def low(dve, i):
                    dve.wait_ge(high_done, i + 1)
                    nc.vector.tensor_tensor(parts(i)[1], rows[:, 2 + i % 2, :],
                                            parts(i)[0].bitcast(F32), ALU.subtract).then_inc(low_done, 1)

                @block.vector
                def _(dve):
                    dve.wait_ge(summed, n)
                    nc.vector.tensor_scalar(rows[0:groups, 0, :], psum[0:groups, 4, :], scale, guard,
                                            ALU.mult, guard_op).then_inc(guarded, 1)
                    dve.wait_ge(rooted, 1)
                    nc.vector.reciprocal(rows[0:groups, 0, :], rows[0:groups, 1, :]).then_inc(inverted, 1)
                    for i in range(n):
                        dve.wait_ge(spread_done, 1 if one else i + 1)
                        if parts and i >= 2:
                            low(dve, i - 2)
                            dve.wait_ge(low_done, i - 1)
                        nc.vector.scalar_tensor_tensor(out=rows[:, 2 + i % 2, :] if parts else dst(i), in0=src(i),
                                                       scalar=gain(i), in1=psum[:, 5 if one else 5 + i % 2, :],
                                                       op0=ALU.mult, op1=ALU.mult).then_inc(scaled, 1)
                    if parts:
                        low(dve, n - 2)
                        low(dve, n - 1)

        def rms_norm(src, dst, n, gain, eps=1e-6, parts=None):
            norm(src, dst, n, 1, lambda i: con("ones", 1), lambda i: con("ones", P, 0, 1), gain,
                 1.0 / (n * P), eps, ALU.add, parts)

        def head_sums(i):
            return con("head_rows", 32, 32 - 2 * i - 2)

        def head_spread(i):
            return con("head_cols", P, i * P, 32)

        def transposes(n, src, read, engines=("scalar", "vector"), start_bank=0):
            with phase("turned", "read_act", "read_dve") as (block, turned, read_act, read_dve):
                who = [engines[j % len(engines)] for j in range(n)]
                sem = {"scalar": read_act, "vector": read_dve}
                upto_ = [sum(w == who[j] for w in who[:j + 1]) for j in range(n)]

                @block.tensor
                def _(pe):
                    for j in range(n):
                        if j >= 8:
                            pe.wait_ge(sem[who[j - 8]], upto_[j - 8])
                        for b in range(4):
                            tr = nc.tensor.transpose(psum[:, j % 8, b * P:(b + 1) * P], src(j, b), con("ident"))
                        tr.then_inc(turned, 1)

                def reader(eng, name):
                    for j in range(n):
                        if who[j] == name:
                            eng.wait_ge(turned, j + 1)
                            read(name, j, psum[:, j % 8, :]).then_inc(sem[name], 1)

                @block.scalar
                def _(act):
                    reader(act, "scalar")

                @block.vector
                def _(dve):
                    reader(dve, "vector")

        def copy_on(eng, dst, src):
            if eng == "vector":
                return nc.vector.tensor_copy(dst, src)
            return nc.scalar.activation(dst, src, ACT.Copy)

        def by_chunk(bank):
            return bank.rearrange("p (c f) -> p c f", c=NCH)

        def to_tokens(src_tile, n, dst):
            transposes(n, lambda j, b: src_tile(j)[:, b * P:(b + 1) * P],
                       lambda eng, j, bank: copy_on(eng, dst[:, :, j * P:(j + 1) * P], by_chunk(bank)))

        XH, XL, HH, HL = 0, 8, 16, 16 + KF

        def ffn_input(gain):
            rms_norm(lambda i: resid[:, i, :], None, KD, gain, parts=two_parts(XH, XL))

        def split_hidden(pool, st, multiplied, hidden_high, hidden_low):
            def body(g):
                for pair in range(st.tiles // 2):
                    n = g * (st.tiles // 2) + pair
                    pool.wait_ge(multiplied, n + 1)
                    nc.gpsimd.tensor_copy(tile_of(rounded(HH, KF), n), rows[:, 2 + pair, :]).then_inc(hidden_high, 1)
                    pool.wait_ge(hidden_high, n + 1)
                    nc.gpsimd.tensor_tensor(tile_of(rounded(HL, KF), n), rows[:, 2 + pair, :],
                                            tile_of(rounded(HH, KF), n).bitcast(F32), ALU.subtract).then_inc(hidden_low, 1)
            loop(pool, st.groups, body)

        def conv_ffn(layer):
            ffn_input(lambda i: col("ffn_g", layer * KD + i))
            name = f"up{layer}"
            cw, cb = VECTOR_AT["conv_w"] + layer * 132, VECTOR_AT["conv_b"] + layer * 44

            def v1(a):
                return vec[:, a:a + 1] if isinstance(a, int) else vec[:, bass.ds(a, 1)]

            with phase("biased", "conv_mid", "conv_done", "gated", "multiplied", "hidden_high", "hidden_low") as \
                    (block, biased, conv_mid, conv_done, gated, multiplied, hidden_high, hidden_low):
                st = Stream(name)

                @block.sync
                def _(sp):
                    load_stream(sp, name)

                @block.tensor
                def _(pe):
                    products(pe, name, two_parts(XH, XL), conv_done)

                @block.gpsimd
                def _(pool):
                    split_hidden(pool, st, multiplied, hidden_high, hidden_low)

                @block.scalar
                def _(act):
                    def read(g, r, done):
                        done()
                        wait(act, multiplied, g * 2 + (r // 2 + 1 - 2))
                        nc.scalar.activation(work[:, r, :], psum[:, r, :], ACT.Identity,
                                             bias=v1(g * R + (cb + r)), scale=v1(g * R + (cw + 88 + r))).then_inc(biased, 1)
                        if r % 2:
                            act.wait_ge(conv_done, g * R + r)
                            nc.scalar.activation(rows[:, r // 2, :], work[:, r - 1, :], ACT.Silu).then_inc(gated, 1)
                    split_and_read(act, name, split_high, read)

                @block.vector
                def _(dve):
                    def read(g, r, done):
                        dve.wait_ge(biased, g * R + (r + 1))
                        nc.vector.scalar_tensor_tensor(out=work[:, r, 1:T], in0=psum[:, r, 0:T - 1],
                                                       scalar=v1(g * R + (cw + 44 + r)), in1=work[:, r, 1:T],
                                                       op0=ALU.mult, op1=ALU.add).then_inc(conv_mid, 1)
                        dve.wait_ge(conv_mid, g * R + (r + 1))
                        nc.vector.scalar_tensor_tensor(out=work[:, r, 2:T], in0=psum[:, r, 0:T - 2],
                                                       scalar=v1(g * R + (cw + r)), in1=work[:, r, 2:T],
                                                       op0=ALU.mult, op1=ALU.add).then_inc(conv_done, 1)
                        if r % 2:
                            pair = r // 2
                            dve.wait_ge(conv_done, g * R + (r + 1))
                            dve.wait_ge(gated, g * 2 + (pair + 1))
                            wait(dve, hidden_low, g * 2 + (pair + 1 - 2))
                            nc.vector.tensor_tensor(rows[:, 2 + pair, :], rows[:, pair, :], work[:, r, :],
                                                    ALU.mult).then_inc(multiplied, 1)
                    split_and_read(dve, name, split_low, read)
            add_projection(f"down{layer}", two_parts(HH, HL, KF))

        def swiglu(layer):
            ffn_input(lambda i: col("ffn2_g", layer * KD + i))
            name = f"up{layer + 2}"
            with phase("gated", "multiplied", "taken", "hidden_high", "hidden_low") as \
                    (block, gated, multiplied, taken, hidden_high, hidden_low):
                st = Stream(name)

                @block.sync
                def _(sp):
                    load_stream(sp, name)

                @block.tensor
                def _(pe):
                    products(pe, name, two_parts(XH, XL), taken)

                @block.gpsimd
                def _(pool):
                    split_hidden(pool, st, multiplied, hidden_high, hidden_low)

                @block.scalar
                def _(act):
                    def read(g, r, done):
                        done()
                        if r % 2 == 0:
                            wait(act, multiplied, g * 2 + (r // 2 + 1 - 2))
                            nc.scalar.activation(rows[:, r // 2, :], psum[:, r, :], ACT.Silu).then_inc(gated, 1)
                        else:
                            nc.scalar.activation(work[:, r // 2, :], psum[:, r, :], ACT.Copy).then_inc(taken, 2)
                    split_and_read(act, name, split_high, read)

                @block.vector
                def _(dve):
                    def read(g, r, done):
                        if r % 2:
                            pair = r // 2
                            dve.wait_ge(gated, g * 2 + (pair + 1))
                            dve.wait_ge(taken, g * R + (r + 1))
                            wait(dve, hidden_low, g * 2 + (pair + 1 - 2))
                            nc.vector.tensor_tensor(rows[:, 2 + pair, :], rows[:, pair, :],
                                                    work[:, pair, :], ALU.mult).then_inc(multiplied, 1)
                    split_and_read(dve, name, split_low, read)
            add_projection(f"down{layer + 2}", two_parts(HH, HL, KF))

        with phase("loaded") as (block, loaded):
            @block.sync
            def _(sp):
                for r in range(R if ORDER else 0):
                    load_unit(sp, Stream(ORDER[0]), 0, r)
                sp.wait_ge(loaded, 48)

            @block.scalar
            def _(act):
                act.dma_start(resid[:, :, :], dram["x"]).then_inc(loaded, 16)
                act.dma_start(const[:, :], dram["const"]).then_inc(loaded, 16)
                act.dma_start(vec[:, :], dram["vec"]).then_inc(loaded, 16)

        def sgu():
            xn, uv, vt, mt, wc = 0, 8, 24, 32, 40
            xl = vt
            rms_norm(lambda i: resid[:, i, :], None, KD, lambda i: col("mix_g", i), parts=two_parts(xn, xl))
            wcv = span(wc, 4).rearrange("p (g t) -> p g t", g=NH)
            with phase("taken", "ws_loaded", "masked") as (block, taken, ws_loaded, masked):
                @block.sync
                def _(sp):
                    sp.dma_start(span(wc, 4), dram["sgu_ws"]).then_inc(ws_loaded, 16)
                    load_stream(sp, "sgu_in")

                @block.tensor
                def _(pe):
                    products(pe, "sgu_in", two_parts(xn, xl), taken)

                @block.vector
                def _(dve):
                    dve.wait_ge(ws_loaded, 16)
                    nc.vector.tensor_tensor(wcv, wcv, con("le").unsqueeze(1).to_broadcast([P, NH, P]),
                                            ALU.mult).then_inc(masked, 1)
                    split_and_read(dve, "sgu_in", split_low)

                @block.scalar
                def _(act):
                    def read(g, m, done):
                        done()
                        nc.scalar.activation(tile_of(arena, g * R + (m + uv)), psum[:, m, :], ACT.Gelu,
                                             bias=col("sgu_b", g * R + m)).then_inc(taken, 1)
                    split_and_read(act, "sgu_in", split_high, read)
            rms_norm(lambda i: arena[:, uv + 8 + i, :], lambda i: arena[:, uv + 8 + i, :], KD, lambda i: col("sgu_gv", i))
            vtv = span(vt, 8).rearrange("p (c f) -> p c f", c=NCH)
            mtv = span(mt, 8).rearrange("p (c f) -> p c f", c=NCH)
            to_tokens(lambda j: arena[:, uv + 8 + j, :], KD, vtv)
            with phase("mixed", "read") as (block, mixed, read):
                @block.tensor
                def _(pe):
                    for g in range(NH):
                        if g >= 8:
                            pe.wait_ge(read, g - 7)
                        nc.tensor.matmul(psum[:, g % 8, 0:256].rearrange("p (c f) -> p c f", c=NCH), wcv[:, g, :],
                                         vtv[:, :, g * HD:(g + 1) * HD], start=True, stop=True).then_inc(mixed, 1)

                @block.vector
                def _(dve):
                    for g in range(NH):
                        dve.wait_ge(mixed, g + 1)
                        nc.vector.tensor_scalar(mtv[:, :, g * HD:(g + 1) * HD],
                                                psum[:, g % 8, 0:256].rearrange("p (c f) -> p c f", c=NCH),
                                                col("sgu_bs", g), None, ALU.add).then_inc(read, 1)
            transposes(KD, lambda j, b: mtv[:, b, j * P:(j + 1) * P],
                       lambda eng, j, bank: nc.vector.tensor_tensor(arena[:, uv + j, :], bank, arena[:, uv + j, :], ALU.mult),
                       engines=("vector",))
            split_tiles(KD, lambda i: arena[:, uv + i, :], two_parts(xn, uv))
            add_projection("sgu_out", two_parts(xn, uv))

        def rwkv():
            XN, XX, MX, RR, KK, VV, WW, AA = (8 * i for i in range(8))

            def whole_of(s):
                return span(s, 8)

            rms_norm(lambda i: resid[:, i, :], lambda i: arena[:, XN + i, :], KD, lambda i: col("mix_g", 8 + i))
            lw1 = span(RR, 5)[:, 0:8 * 288].rearrange("p (k n) -> p k n", k=KD)
            w2 = span(XN, 2)
            a2 = span(XN + 2, 2)
            with phase("loaded", "shifted") as (block, loaded, shifted):
                @block.sync
                def _(sp):
                    sp.dma_start(span(RR, 5)[:, 0:8 * 288], dram["lora1"]).then_inc(loaded, 16)
                    sp.wait_ge(loaded, 16)

                @block.vector
                def _(dve):
                    a, b = arena[:, XN:XN + 8, :], arena[:, XX:XX + 8, :]
                    nc.vector.tensor_tensor(b[:, :, 1:T], a[:, :, 0:T - 1], a[:, :, 1:T], ALU.subtract).then_inc(shifted, 1)
                    nc.vector.tensor_scalar(b[:, :, 0:1], a[:, :, 0:1], -1.0, None, ALU.mult).then_inc(shifted, 1)
                    dve.wait_ge(shifted, 2)

            def mix(dve, which, mixed):
                for i in range(KD):
                    nc.vector.scalar_tensor_tensor(out=arena[:, MX + i, :], in0=arena[:, XX + i, :],
                                                   scalar=col("mu", which * KD + i), in1=arena[:, XN + i, :],
                                                   op0=ALU.mult, op1=ALU.add).then_inc(mixed, 1)

            for which, parts in ((1, [(0, 64, 0, ACT.Tanh)]), (4, [(64, 64, 1, ACT.Copy)]),
                                 (5, [(128, 128, 2, ACT.Sigmoid), (256, 32, 3, ACT.Sigmoid)])):
                with phase("mixed", "summed", "kept") as (block, mixed, summed, kept):
                    @block.vector
                    def _(dve):
                        mix(dve, which, mixed)

                    @block.tensor
                    def _(pe):
                        for n, (at, m, row, _) in enumerate(parts):
                            for k in range(KD):
                                if n == 0:
                                    pe.wait_ge(mixed, k + 1)
                                mm = nc.tensor.matmul(psum[0:m, n, :], lw1[:, k, at:at + m], arena[:, MX + k, :],
                                                      start=(k == 0), stop=(k == KD - 1))
                            mm.then_inc(summed, 1)

                    @block.scalar
                    def _(act):
                        for n, (at, m, row, func) in enumerate(parts):
                            act.wait_ge(summed, n + 1)
                            nc.scalar.activation(rows[0:m, row, :], psum[0:m, n, :], func).then_inc(kept, 1)

            for which, name, dst in ((0, "rwkv_r", RR), (2, "rwkv_k", KK), (3, "rwkv_v", VV)):
                with phase("mixed", "mixed_high", "mixed_low", "taken") as (block, mixed, mixed_high, mixed_low, taken):
                    @block.sync
                    def _(sp):
                        load_stream(sp, name)

                    @block.vector
                    def _(dve):
                        mix(dve, which, mixed)
                        for i in range(KD):
                            dve.wait_ge(mixed_high, i + 1)
                            nc.vector.tensor_tensor(rounded(MX)[:, i, :], arena[:, MX + i, :], rounded(WW)[:, i, :].bitcast(F32),
                                                    ALU.subtract).then_inc(mixed_low, 1)
                        split_and_read(dve, name, split_low)

                    @block.tensor
                    def _(pe):
                        products(pe, name, two_parts(WW, MX), taken,
                                 before=lambda pe: pe.wait_ge(mixed_low, KD))

                    @block.scalar
                    def _(act):
                        for i in range(KD):
                            act.wait_ge(mixed, i + 1)
                            nc.scalar.activation(rounded(WW)[:, i, :], arena[:, MX + i, :], ACT.Copy).then_inc(mixed_high, 1)

                        def read(g, m, done):
                            done()
                            nc.scalar.activation(tile_of(arena, g * R + (m + dst)), psum[:, m, :], ACT.Copy).then_inc(taken, 1)
                        split_and_read(act, name, split_high, read)

            with phase("loaded_w", "loaded_a", "summed", "kept") as (block, loaded_w, loaded_a, summed, kept):
                @block.sync
                def _(sp):
                    sp.dma_start(w2[0:HD, :], dram["lora_w2"]).then_inc(loaded_w, 16)
                    sp.dma_start(a2[0:HD, :], dram["lora_a2"]).then_inc(loaded_a, 16)

                jobs = [(w2, 0, WW, "w0", m) for m in range(KD)] + [(a2, 1, AA, "a0", m) for m in range(KD)]

                @block.tensor
                def _(pe):
                    for n, (w, row, dst, bias, m) in enumerate(jobs):
                        if m == 0:
                            pe.wait_ge(loaded_a if n else loaded_w, 16)
                        if n >= 4:
                            pe.wait_ge(kept, n - 3)
                        nc.tensor.matmul(psum[:, n % 4, :], w[0:HD, m * P:(m + 1) * P], rows[0:HD, row, :],
                                         start=True, stop=True).then_inc(summed, 1)

                @block.scalar
                def _(act):
                    for n, (w, row, dst, bias, m) in enumerate(jobs):
                        act.wait_ge(summed, n + 1)
                        nc.scalar.activation(arena[:, dst + m, :], psum[:, n % 4, :], ACT.Sigmoid,
                                             bias=col(bias, m)).then_inc(kept, 1)

            with phase("scaled") as (block, scaled):
                @block.vector
                def _(dve):
                    for i in range(KD):
                        nc.vector.tensor_scalar(arena[:, XN + i, :], arena[:, KK + i, :], col("k_k", i), None,
                                                ALU.mult).then_inc(scaled, 1)
            norm(lambda i: arena[:, XN + i, :], lambda i: arena[:, XN + i, :], KD, 32, head_sums, head_spread,
                 lambda i: 1.0, 1.0, 1e-24, ALU.max)

            mid = small[:, 0:32].rearrange("p (i c) -> p i c", c=NCH)
            end = small[:, 32:64].rearrange("p (i c) -> p i c", c=NCH)
            scl = small[:, 64:96].rearrange("p (i c) -> p i c", c=NCH)
            bonus = small[:, 128:192].rearrange("p (c h) -> p c h", c=NCH)
            chunks = "p (j t) -> p j t"

            with phase("tmp_done", "k_done", "rk_done", "summed", "b_done", "scanned", "mid_done", "centred", "less") as \
                    (block, tmp_done, k_done, rk_done, summed, b_done, scanned, mid_done, centred, less):
                @block.vector
                def _(dve):
                    for i in range(KD):
                        if i >= 4:
                            dve.wait_ge(k_done, i - 3)
                        nc.vector.tensor_scalar(work[:, i % 4, :], arena[:, AA + i, :], -1.0, col("k_a", i),
                                                ALU.add, ALU.mult).then_inc(tmp_done, 1)
                        for c in range(NCH):
                            s = slice(c * CH, (c + 1) * CH)
                            nc.vector.tensor_tensor_scan(arena[:, XX + i, s], con("ones"), arena[:, WW + i, s], 0.0,
                                                         ALU.mult, ALU.add).then_inc(scanned, 1)
                        dve.wait_ge(tmp_done, i + 1)
                        nc.vector.scalar_tensor_tensor(out=arena[:, KK + i, :], in0=work[:, i % 4, :], scalar=1.0,
                                                       in1=arena[:, KK + i, :], op0=ALU.add, op1=ALU.mult).then_inc(k_done, 1)
                        dve.wait_ge(k_done, i + 1)
                        nc.vector.scalar_tensor_tensor(out=arena[:, MX + i, :], in0=arena[:, RR + i, :],
                                                       scalar=col("r_k", i), in1=arena[:, KK + i, :],
                                                       op0=ALU.mult, op1=ALU.mult).then_inc(rk_done, 1)
                    dve.wait_ge(scanned, KD * NCH)
                    sums = whole_of(XX).rearrange(chunks, t=CH)
                    nc.vector.tensor_copy(mid, sums[:, :, 63:64].rearrange("p (i c) o -> p i (c o)", c=NCH)).then_inc(mid_done, 1)
                    dve.wait_ge(mid_done, 1)
                    nc.vector.tensor_tensor(sums, sums, small[:, 0:32].unsqueeze(2).to_broadcast([P, 32, CH]),
                                            ALU.subtract).then_inc(centred, 1)
                    dve.wait_ge(centred, 1)
                    nc.vector.tensor_tensor(whole_of(WW), whole_of(XX), whole_of(WW), ALU.subtract).then_inc(less, 1)
                    dve.wait_ge(summed, 1)
                    nc.vector.tensor_copy(small[:, 128:192], psum[:, 0, 0:64]).then_inc(less, 1)

                @block.tensor
                def _(pe):
                    pe.wait_ge(rk_done, KD)
                    for c in range(NCH):
                        for i in range(KD):
                            mm = nc.tensor.matmul(psum[:, 0, c * NH + 2 * i:c * NH + 2 * i + 2],
                                                  arena[:, MX + i, c * CH:(c + 1) * CH], con("halves", 2),
                                                  start=True, stop=True)
                    mm.then_inc(summed, 1)

            with phase("b_done", "e1", "e2", "e3", "mids", "hats", "ends", "bonus_kept") as \
                    (block, b_done, e1, e2, e3, mids, hats, ends, bonus_kept):
                @block.scalar
                def _(act):
                    nc.scalar.activation(whole_of(MX), whole_of(XX), ACT.Exp, scale=-EXP_HALF).then_inc(e1, 1)
                    act.wait_ge(e1, 1)
                    nc.scalar.activation(whole_of(XX), whole_of(XX), ACT.Exp, scale=EXP_HALF).then_inc(e2, 1)
                    nc.scalar.activation(whole_of(WW), whole_of(WW), ACT.Exp, scale=-EXP_HALF).then_inc(e3, 1)
                    nc.scalar.activation(small[:, 96:128], small[:, 0:32], ACT.Exp, scale=-EXP_HALF).then_inc(mids, 1)

                @block.vector
                def _(dve):
                    nc.vector.tensor_tensor(whole_of(AA), whole_of(XN), whole_of(AA), ALU.mult).then_inc(b_done, 1)
                    dve.wait_ge(e1, 1)
                    nc.vector.tensor_tensor(whole_of(RR), whole_of(RR), whole_of(MX), ALU.mult).then_inc(hats, 1)
                    nc.vector.tensor_copy(end, whole_of(MX).rearrange(chunks, t=CH)[:, :, 127:128]
                                          .rearrange("p (i c) o -> p i (c o)", c=NCH)).then_inc(ends, 1)
                    dve.wait_ge(e2, 1)
                    nc.vector.tensor_tensor(whole_of(KK), whole_of(KK), whole_of(XX), ALU.mult).then_inc(hats, 1)
                    dve.wait_ge(b_done, 1)
                    nc.vector.tensor_tensor(whole_of(AA), whole_of(AA), whole_of(XX), ALU.mult).then_inc(hats, 1)
                    dve.wait_ge(e3, 1)
                    nc.vector.scalar_tensor_tensor(out=whole_of(WW), in0=whole_of(WW), scalar=-1.0, in1=whole_of(XN),
                                                   op0=ALU.mult, op1=ALU.mult).then_inc(hats, 1)
                    dve.wait_ge(mids, 1)
                    dve.wait_ge(ends, 1)
                    nc.vector.tensor_tensor(scl[:, :, 0:3], end[:, :, 0:3],
                                            small[:, 96:128].rearrange("p (i c) -> p i c", c=NCH)[:, :, 1:4],
                                            ALU.mult).then_inc(ends, 1)

            vt = whole_of(MX).rearrange("p (c f) -> p c f", c=NCH)
            to_tokens(lambda j: arena[:, VV + j, :], KD, vt)
            yt = whole_of(VV).rearrange("p (c f) -> p c f", c=NCH)
            bufs = []
            for s in (XN, XX):
                w = whole_of(s)
                bufs.append(dict(
                    m=w[:, 0:2048].rearrange("p (k h t) -> p k h t", k=4, h=4),
                    x=w[:, 2048:3072].rearrange("p (k h t) -> p k h t", k=2, h=4),
                    xf=w[:, 2048:3072], lb=w[:, 3072:3584].rearrange("p (h t) -> p h t", h=4),
                    t1=w[:, 3584:4096].rearrange("p (h t) -> p h t", h=4), t1f=w[:, 3584:4096]))
            wf = flat(work[:, :, :])
            btm, ktm = wf[:, 0:512], wf[:, 512:1024]
            z, sa = wf[:, 1024:1536], wf[:, 1536:2048]
            AB, RB, AK, RK = range(4)

            def per_head(ap):
                return ap.unsqueeze(1).to_broadcast([P, 4, P])

            for step in range(2 * NCH):
                c, half = step // 2, step % 2
                cs = slice(c * CH, (c + 1) * CH)

                def fm(slot, h):
                    i, e = h // 2, h % 2
                    return arena[e * HD:(e + 1) * HD, slot + i, cs]

                with phase("scored", "masked", "first_inv", "ones_added", "bk_turned", "bk_kept") as \
                        (block, scored, masked, first_inv, ones_added, bk_turned, bk_kept):
                    jobs = [(a, kind) for a in range(2) for kind in (AB, RB, AK, RK, 4)]

                    @block.tensor
                    def _(pe):
                        for n, (a, kind) in enumerate(jobs):
                            if n >= 6:
                                pe.wait_ge(masked, n - 5)
                            for j in range(4):
                                h = half * 8 + 2 * j + a
                                lhs, rhs = {AB: (AA, WW), RB: (AA, RR), AK: (KK, WW), RK: (KK, RR), 4: (WW, AA)}[kind]
                                mm = nc.tensor.matmul(psum[:, n % 6, j * P:(j + 1) * P], fm(lhs, h), fm(rhs, h),
                                                      start=True, stop=True)
                            mm.then_inc(scored, 1)
                        for which, slot in enumerate((AA, KK)):
                            for j in range(4):
                                tr = nc.tensor.transpose(psum[:, 6 + which, j * P:(j + 1) * P],
                                                         arena[:, slot + half * 4 + j, cs], con("ident"))
                            tr.then_inc(bk_turned, 1)

                    @block.scalar
                    def _(act):
                        for which, dst in enumerate((btm, ktm)):
                            act.wait_ge(bk_turned, which + 1)
                            nc.scalar.activation(dst, psum[:, 6 + which, :], ACT.Copy).then_inc(bk_kept, 1)

                    @block.vector
                    def _(dve):
                        for n, (a, kind) in enumerate(jobs):
                            dve.wait_ge(scored, n + 1)
                            src = psum[:, n % 6, :].rearrange("p (h t) -> p h t", h=4)
                            if kind == 4:
                                nc.vector.tensor_tensor(bufs[a]["x"][:, 0], src, per_head(con("pair_low")),
                                                        ALU.mult).then_inc(masked, 1)
                            else:
                                mask = con("lt") if kind in (AB, AK) else con("le")
                                nc.vector.tensor_tensor(bufs[a]["m"][:, kind], src, per_head(mask),
                                                        ALU.mult).then_inc(masked, 1)

                    @block.gpsimd
                    def _(pool):
                        for a in range(2):
                            pool.wait_ge(masked, 5 * a + 5)
                            nc.gpsimd.tensor_tensor(bufs[a]["x"][:, 1], bufs[a]["m"][:, AB], per_head(con("levels")),
                                                    ALU.mult).then_inc(first_inv, 1)
                            pool.wait_ge(first_inv, a + 1)
                            x8 = bufs[a]["xf"].rearrange("p (h t) -> p h t", h=8)
                            nc.gpsimd.tensor_tensor(x8, x8, con("ident").unsqueeze(1).to_broadcast([P, 8, P]),
                                                    ALU.add).then_inc(ones_added, 1)

                with phase("lb_ready", "t1_done", "t1_kept", "p_done", "x_added") as \
                        (block, lb_ready, t1_done, t1_kept, p_done, x_added):
                    @block.gpsimd
                    def _(pool):
                        for l in range(6):
                            for a in range(2):
                                if l:
                                    pool.wait_ge(t1_done, 2 * (l - 1) + a + 1)
                                nc.gpsimd.tensor_tensor(bufs[a]["lb"], bufs[a]["m"][:, AB],
                                                        per_head(con("levels", P, (l + 1) * P)),
                                                        ALU.mult).then_inc(lb_ready, 1)

                    @block.tensor
                    def _(pe):
                        for l in range(6):
                            for a in range(2):
                                pe.wait_ge(lb_ready, 2 * l + a + 1)
                                if l:
                                    pe.wait_ge(x_added, 2 * (l - 1) + a + 1)
                                for j in range(4):
                                    mm = nc.tensor.matmul(psum[:, a, j * P:(j + 1) * P], bufs[a]["lb"][:, j, :],
                                                          bufs[a]["x"][:, 0, j, :], start=True, stop=True)
                                mm.then_inc(t1_done, 1)
                            for a in range(2):
                                pe.wait_ge(t1_kept, 2 * l + a + 1)
                                for j in range(4):
                                    t1, xt = bufs[a]["t1"][:, j, :], bufs[a]["x"][:, 1, j, :]
                                    if l < 5:
                                        nc.tensor.matmul(psum[:, 2 + 2 * a, j * P:(j + 1) * P], xt, t1, start=True, stop=True)
                                    mm = nc.tensor.matmul(psum[:, 3 + 2 * a, j * P:(j + 1) * P], t1, xt, start=True, stop=True)
                                mm.then_inc(p_done, 1)

                    @block.scalar
                    def _(act):
                        for l in range(6):
                            for a in range(2):
                                act.wait_ge(t1_done, 2 * l + a + 1)
                                nc.scalar.activation(bufs[a]["t1f"], psum[:, a, :], ACT.Copy).then_inc(t1_kept, 1)

                    @block.vector
                    def _(dve):
                        for l in range(6):
                            for a in range(2):
                                dve.wait_ge(p_done, 2 * l + a + 1)
                                if l < 5:
                                    x = bufs[a]["xf"]
                                    nc.vector.tensor_tensor(x, flat(psum[:, 2 + 2 * a:4 + 2 * a, :]), x, ALU.add)\
                                        .then_inc(x_added, 1)
                                else:
                                    x = bufs[a]["xf"][:, 512:1024]
                                    nc.vector.tensor_tensor(x, psum[:, 3 + 2 * a, :], x, ALU.add).then_inc(x_added, 1)

                with phase("z_done", "z_kept", "sa_done", "sa_kept", "y_done", "s_done", "y_kept", "s_added", "s_kept") as \
                        (block, z_done, z_kept, sa_done, sa_kept, y_done, s_done, y_kept, s_added, s_kept):
                    def head(j):
                        h = half * 8 + j
                        b = bufs[j % 2]
                        s0 = state[(h % 2) * HD:(h % 2 + 1) * HD, h // 2, :]
                        return h, b, j // 2, s0, vt[:, c, h * HD:(h + 1) * HD]

                    @block.tensor
                    def _(pe):
                        for j in range(8):
                            h, b, jj, s0, v = head(j)
                            o = psum[:, 4 * (j % 2), (j // 2) * HD:(j // 2 + 1) * HD]
                            if c:
                                nc.tensor.matmul(o, fm(WW, h), s0, start=True, stop=False)
                            mm = nc.tensor.matmul(o, b["m"][:, AK, jj, :], v, start=(c == 0), stop=True)
                        mm.then_inc(z_done, 1)
                        pe.wait_ge(z_kept, 2)
                        for j in range(8):
                            h, b, jj, s0, v = head(j)
                            mm = nc.tensor.matmul(psum[:, 1, j * HD:(j + 1) * HD], b["x"][:, 1, jj, :],
                                                  z[:, (j % 2) * 256 + (j // 2) * HD:(j % 2) * 256 + (j // 2 + 1) * HD],
                                                  start=True, stop=True)
                        mm.then_inc(sa_done, 1)
                        pe.wait_ge(sa_kept, 1)
                        if c < NCH - 1:
                            for i in range(4):
                                o = psum[:, 3, i * P:(i + 1) * P]
                                nc.tensor.matmul(o, btm[:, i * P:(i + 1) * P], sa[:, i * P:(i + 1) * P], start=True, stop=False)
                                mm = nc.tensor.matmul(o, ktm[:, i * P:(i + 1) * P],
                                                      vt[:, c, (half * 4 + i) * P:(half * 4 + i + 1) * P],
                                                      start=False, stop=True)
                            mm.then_inc(s_done, 1)
                        for j in range(8):
                            h, b, jj, s0, v = head(j)
                            o = psum[:, 2 + 3 * (j % 2), (j // 2) * HD:(j // 2 + 1) * HD]
                            if c:
                                nc.tensor.matmul(o, fm(RR, h), s0, start=True, stop=False)
                            nc.tensor.matmul(o, b["m"][:, RB, jj, :], sa[:, j * HD:(j + 1) * HD], start=(c == 0), stop=False)
                            mm = nc.tensor.matmul(o, b["m"][:, RK, jj, :], v, start=False, stop=True)
                        mm.then_inc(y_done, 1)

                    @block.vector
                    def _(dve):
                        dve.wait_ge(z_done, 1)
                        for e in range(2):
                            nc.vector.tensor_copy(z[:, e * 256:(e + 1) * 256], psum[:, 4 * e, 0:256]).then_inc(z_kept, 1)
                        dve.wait_ge(sa_done, 1)
                        nc.vector.tensor_copy(sa, psum[:, 1, :]).then_inc(sa_kept, 1)
                        dve.wait_ge(y_done, 1)
                        yh = yt[:, c, half * 512:(half + 1) * 512].rearrange("p (i e f) -> p i e f", i=4, e=2)
                        for e in range(2):
                            nc.vector.tensor_copy(yh[:, :, e, :], psum[:, 2 + 3 * e, 0:256].rearrange("p (i f) -> p i f", i=4))\
                                .then_inc(y_kept, 1)
                        if c < NCH - 1:
                            dve.wait_ge(s_done, 1)
                            for e in range(2):
                                ps = slice(e * HD, (e + 1) * HD)
                                s0 = state[ps, half * 4:half * 4 + 4, :]
                                new = psum[ps, 3, :].rearrange("p (i f) -> p i f", i=4)[:, :, e * HD:(e + 1) * HD]
                                sc = scl[ps, half * 4:half * 4 + 4, c:c + 1].to_broadcast([HD, 4, HD])
                                if c:
                                    nc.vector.tensor_tensor(s0, new, s0, ALU.add).then_inc(s_added, 1)
                                    dve.wait_ge(s_added, e + 1)
                                    nc.vector.tensor_tensor(s0, s0, sc, ALU.mult).then_inc(s_kept, 1)
                                else:
                                    nc.vector.tensor_tensor(s0, new, sc, ALU.mult).then_inc(s_kept, 1)

            yw = whole_of(VV).rearrange("p (j f) -> p j f", f=HD)
            sq = whole_of(XN).rearrange("p (j f) -> p j f", f=HD)
            g2 = span(XX, 4)
            with phase("g2_loaded", "s1", "s2", "s3", "s4", "s5", "s6", "s7", "s8", "s9") as \
                    (block, g2_loaded, mean_sum, mean_done, less_mean, squared, var_sum, var_done, rooted, inverted, done):
                m1, m2, m3 = small[:, 0:64], small[:, 64:128], state[:, 0, :]

                @block.sync
                def _(sp):
                    sp.dma_start(g2[:, 0:D], dram["lora_g2"][0:P, :]).then_inc(g2_loaded, 16)
                    sp.dma_start(g2[0:32, D:2 * D], dram["lora_g2"][P:160, :]).then_inc(g2_loaded, 16)
                    sp.wait_ge(g2_loaded, 32)

                @block.vector
                def _(dve):
                    nc.vector.reduce_sum(m1, yw, axis=AX).then_inc(mean_sum, 1)
                    dve.wait_ge(mean_sum, 1)
                    nc.vector.tensor_scalar(m2, m1, 1.0 / HD, None, ALU.mult).then_inc(mean_done, 1)
                    dve.wait_ge(mean_done, 1)
                    nc.vector.tensor_tensor(yw, yw, m2.unsqueeze(2).to_broadcast([P, 64, HD]), ALU.subtract).then_inc(less_mean, 1)
                    vw = whole_of(MX).rearrange("p (j f) -> p j f", f=HD)
                    nc.vector.tensor_tensor(vw, vw, small[:, 128:192].unsqueeze(2).to_broadcast([P, 64, HD]), ALU.mult).then_inc(done, 1)
                    dve.wait_ge(squared, 1)
                    nc.vector.reduce_sum(m1, sq, axis=AX).then_inc(var_sum, 1)
                    dve.wait_ge(var_sum, 1)
                    nc.vector.tensor_scalar(m2, m1, 1.0 / HD, 64e-5, ALU.mult, ALU.add).then_inc(var_done, 1)
                    dve.wait_ge(rooted, 1)
                    nc.vector.reciprocal(m1, m3).then_inc(inverted, 1)
                    dve.wait_ge(inverted, 1)
                    nc.vector.tensor_tensor(yw, yw, m1.unsqueeze(2).to_broadcast([P, 64, HD]), ALU.mult).then_inc(done, 1)

                @block.scalar
                def _(act):
                    act.wait_ge(less_mean, 1)
                    nc.scalar.activation(whole_of(XN), whole_of(VV), ACT.Square).then_inc(squared, 1)
                    act.wait_ge(var_done, 1)
                    nc.scalar.activation(m3, m2, ACT.Sqrt).then_inc(rooted, 1)

            def take(eng, j, bank):
                i = j // 2
                if j % 2 == 0:
                    return nc.scalar.activation(arena[:, RR + i, :], bank, ACT.Identity, bias=col("ln_b", i), scale=col("ln_w", i))
                return nc.vector.tensor_copy(arena[:, KK + i, :], bank)
            transposes(2 * KD, lambda j, b: (yt, vt)[j % 2][:, b, (j // 2) * P:(j // 2 + 1) * P], take)
            with phase("summed", "gated_", "added") as (block, summed, gated, added):
                @block.tensor
                def _(pe):
                    for m in range(KD):
                        if m >= 4:
                            pe.wait_ge(gated, m - 3)
                        nc.tensor.matmul(psum[:, m % 4, :], g2[:, m * P:(m + 1) * P], rows[:, 2, :], start=True, stop=False)
                        nc.tensor.matmul(psum[:, m % 4, :], g2[0:32, D + m * P:D + (m + 1) * P], rows[0:32, 3, :],
                                         start=False, stop=True).then_inc(summed, 1)

                @block.vector
                def _(dve):
                    for m in range(KD):
                        y = arena[:, RR + m, :]
                        nc.vector.tensor_tensor(y, y, arena[:, KK + m, :], ALU.add).then_inc(added, 1)
                        dve.wait_ge(added, m + 1)
                        dve.wait_ge(summed, m + 1)
                        nc.vector.tensor_tensor(y, psum[:, m % 4, :], y, ALU.mult).then_inc(gated, 1)
            split_tiles(KD, lambda i: arena[:, RR + i, :], two_parts(WW, RR))
            add_projection("rwkv_o", two_parts(WW, RR))

        def attention(units, sb, pr, pt, bias, before):
            n = len(units)
            scale = HD ** -0.5
            mx, nm, sm, rc = (small[:, 8 * a:8 * a + 8] for a in range(4))
            with phase("scored", "biased", "maxed", "negated", "expd", "turned", "pt_kept", "pv_done", "inverted",
                       "out_done", "bias_ready", "bias_loaded") as \
                    (block, scored, biased, maxed, negated, expd, turned, pt_kept, pv_done, inverted, out_done,
                     bias_ready, bias_loaded):
                if bias:
                    before(block, bias_ready, bias_loaded, biased)

                @block.tensor
                def _(pe):
                    for i in range(n + 3):
                        if i < n:
                            if i >= 4:
                                pe.wait_ge(biased if bias else expd, i - 3)
                            nc.tensor.matmul(psum[:, i % 4, :], units[i][0], units[i][1], start=True, stop=True).then_inc(scored, 1)
                        if 2 <= i < n + 2:
                            u = i - 2
                            pe.wait_ge(expd, u + 1)
                            if u >= 2:
                                pe.wait_ge(pt_kept, u - 1)
                            for b in range(4):
                                tr = nc.tensor.transpose(psum[:, 4 + u % 2, b * P:(b + 1) * P],
                                                         pr[u % 3][:, b * P:(b + 1) * P], con("ident"))
                            tr.then_inc(turned, 1)
                        if i >= 3:
                            u = i - 3
                            pe.wait_ge(pt_kept, u + 1)
                            if u >= 2:
                                pe.wait_ge(out_done, u - 1)
                            for b in range(4):
                                mm = nc.tensor.matmul(psum[:, 6 + u % 2, 0:HD], pt[u % 2][:, b * P:(b + 1) * P],
                                                      units[u][2](b), start=(b == 0), stop=(b == 3))
                            mm.then_inc(pv_done, 1)

                @block.scalar
                def _(act):
                    for i in range(n + 1):
                        if i < n:
                            act.wait_ge(negated, i + 1)
                            if i >= 3:
                                act.wait_ge(turned, i - 2)
                            if i >= 8:
                                act.wait_ge(inverted, i - 7)
                            src = sb[i % 2] if bias else psum[:, i % 4, :]
                            nc.scalar.activation(pr[i % 3], src, ACT.Exp, bias=nm[:, i % 8:i % 8 + 1],
                                                 scale=1.0 if bias else scale,
                                                 accum_out=sm[:, i % 8:i % 8 + 1]).then_inc(expd, 1)
                        if i >= 1:
                            u = i - 1
                            act.wait_ge(turned, u + 1)
                            if u >= 2:
                                act.wait_ge(pv_done, u - 1)
                            nc.scalar.activation(pt[u % 2], psum[:, 4 + u % 2, :], ACT.Copy).then_inc(pt_kept, 1)

                @block.vector
                def _(dve):
                    def maximum(i):
                        dve.wait_ge(scored, i + 1)
                        if i >= 8:
                            dve.wait_ge(negated, i - 7)
                        c8 = i % 8
                        if bias:
                            dve.wait_ge(bias_ready, i // 4 + 1)
                            if i >= 2:
                                dve.wait_ge(expd, i - 1)
                            nc.vector.scalar_tensor_tensor(out=sb[i % 2], in0=psum[:, i % 4, :], scalar=scale,
                                                           in1=bias(i), op0=ALU.mult, op1=ALU.add).then_inc(biased, 1)
                            dve.wait_ge(biased, i + 1)
                            nc.vector.reduce_max(mx[:, c8:c8 + 1], sb[i % 2], axis=AX).then_inc(maxed, 1)
                        else:
                            nc.vector.reduce_max(mx[:, c8:c8 + 1], psum[:, i % 4, :], axis=AX).then_inc(maxed, 1)
                        dve.wait_ge(maxed, i + 1)
                        if i >= 8:
                            dve.wait_ge(expd, i - 7)
                        nc.vector.tensor_scalar(nm[:, c8:c8 + 1], mx[:, c8:c8 + 1], -1.0 if bias else -scale, None,
                                                ALU.mult).then_inc(negated, 1)

                    for i in range(n + 4):
                        if i < n:
                            maximum(i)
                        if i >= 4:
                            u = i - 4
                            dve.wait_ge(expd, u + 1)
                            if u >= 8:
                                dve.wait_ge(out_done, u - 7)
                            nc.vector.reciprocal(rc[:, u % 8:u % 8 + 1], sm[:, u % 8:u % 8 + 1]).then_inc(inverted, 1)
                            dve.wait_ge(inverted, u + 1)
                            dve.wait_ge(pv_done, u + 1)
                            nc.vector.tensor_scalar(units[u][3], psum[:, 6 + u % 2, 0:HD], rc[:, u % 8:u % 8 + 1], None,
                                                    ALU.mult).then_inc(out_done, 1)

        def key_halves(keys, first):
            with phase("zeroed", "copied") as (block, zeroed, copied):
                @block.gpsimd
                def _(pool):
                    for n, (e, t) in enumerate(keys):
                        nc.gpsimd.memset(arena[(1 - e) * HD:(2 - e) * HD, first + n, :], 0.0).then_inc(zeroed, 1)

                @block.vector
                def _(dve):
                    for n, (e, t) in enumerate(keys):
                        ps = slice(e * HD, (e + 1) * HD)
                        nc.vector.tensor_copy(arena[ps, first + n, :], arena[ps, t, :]).then_inc(copied, 1)

        def even_in():
            XN, Q, Z, XS = 0, 8, 20, 28
            name = "even_in"
            n0 = first_unit[name]
            XNL = 44
            rms_norm(lambda i: resid[:, i, :], None, KD, lambda i: col("even_g", i), parts=two_parts(XN, XNL))
            wdt = span(52, 1)[:, 0:8 * 32].rearrange("p (k n) -> p k n", k=KD)
            cw, cb = VECTOR_AT["ssd_cw"], VECTOR_AT["ssd_cb"]

            def v1(a):
                return vec[:, a:a + 1] if isinstance(a, int) else vec[:, bass.ds(a, 1)]

            with phase("taken", "biased", "t0", "t1", "t2", "wdt_loaded", "dt_done", "dt_kept") as \
                    (block, taken, biased, tap0, tap1, tap3, wdt_loaded, dt_done, dt_kept):
                @block.sync
                def _(sp):
                    sp.dma_start(span(52, 1)[:, 0:8 * 32], dram["even_dt"]).then_inc(wdt_loaded, 16)
                    load_stream(sp, name)

                @block.tensor
                def _(pe):
                    products(pe, name, two_parts(XN, XNL), taken)
                    pe.wait_ge(wdt_loaded, 16)
                    for c in range(NCH):
                        for k in range(2 * KD):
                            x = two_parts(XN, XNL)(k % KD)[k // KD]
                            mm = nc.tensor.matmul(psum[:, 4, c * 32:(c + 1) * 32], x[:, c * CH:(c + 1) * CH].bitcast(F32),
                                                  wdt[:, k % KD, :], start=(k == 0), stop=(k == 2 * KD - 1))
                    mm.then_inc(dt_done, 1)

                @block.scalar
                def _(act):
                    def read_copy(g, r, done):
                        done()
                        nc.scalar.activation(tile_of(arena, g * R + (r + Q)), psum[:, r, :], ACT.Copy).then_inc(taken, 1)

                    def read_silu(g, r, done):
                        done()
                        nc.scalar.activation(tile_of(arena, g * R + (r + Q)), psum[:, r, :], ACT.Silu).then_inc(taken, 1)

                    def read_conv(g, r, done):
                        done()
                        nc.scalar.activation(tile_of(arena, g * R + (r + Q)), psum[:, r, :], ACT.Identity,
                                             bias=v1(g * R + (r + cb - 20)), scale=v1(g * R + (r + cw + 32 - 20))).then_inc(biased, 1)
                    split_and_read(act, name, split_high, groups=[(read_copy, 0, 3), (read_silu, 3, 5), (read_conv, 5, 9)])

                @block.vector
                def _(dve):
                    def read_conv(g, r, done):
                        o = tile_of(arena, g * R + (r + Q))

                        def tap(j, dst, src, sem):
                            return nc.vector.scalar_tensor_tensor(
                                out=o[:, dst], in0=psum[:, r, src], scalar=v1(g * R + (r + cw + 16 * j - 20)), in1=o[:, dst],
                                op0=ALU.mult, op1=ALU.add).then_inc(sem, 1)
                        dve.wait_ge(biased, g * R + (r + 1 - 20))
                        tap(0, slice(2, T), slice(0, T - 2), tap0)
                        dve.wait_ge(tap0, g * R + (r + 1 - 20))
                        tap(1, slice(1, T), slice(0, T - 1), tap1)
                        dve.wait_ge(tap1, g * R + (r + 1 - 20))
                        tap(3, slice(0, T - 1), slice(1, T), taken)
                    split_and_read(dve, name, split_low, groups=[(None, 0, 5), (read_conv, 5, 9)])
                    dve.wait_ge(dt_done, 1)
                    nc.vector.tensor_tensor(rows[:, 3, 0:128].rearrange("p (c h) -> p c h", c=NCH),
                                            psum[:, 4, 0:128].rearrange("p (c h) -> p c h", c=NCH),
                                            col("dt_bias", 0, 32).unsqueeze(1).to_broadcast([P, NCH, 32]),
                                            ALU.add).then_inc(dt_kept, 1)
            U, DT, AC, TM = (rows[:, 3, 128 * a:128 * (a + 1)] for a in range(4))
            with phase("silu_", "abs_", "exp_", "ln_", "relu_", "dt", "expA", "a") as \
                    (block, silu_done, abs_done, exp_done, ln_done, relu_done, dt_ready, ea_done, a_ready):
                @block.scalar
                def _(act):
                    x = span(XS, 16)
                    nc.scalar.activation(x, x, ACT.Silu).then_inc(silu_done, 1)
                    nc.scalar.activation(TM, U, ACT.Abs).then_inc(abs_done, 1)
                    act.wait_ge(abs_done, 1)
                    nc.scalar.activation(DT, TM, ACT.Exp, scale=-1.0).then_inc(exp_done, 1)
                    act.wait_ge(exp_done, 1)
                    nc.scalar.activation(TM, DT, ACT.Ln, bias=con("ones", 1)).then_inc(ln_done, 1)
                    nc.scalar.activation(small[:, 0:32], col("A_log", 0, 32), ACT.Exp).then_inc(ea_done, 1)

                @block.vector
                def _(dve):
                    dve.wait_ge(ln_done, 1)
                    nc.vector.scalar_tensor_tensor(out=DT, in0=U, scalar=0.0, in1=TM, op0=ALU.max, op1=ALU.add).then_inc(dt_ready, 1)
                    dve.wait_ge(dt_ready, 1)
                    dve.wait_ge(ea_done, 1)
                    v = "p (c h) -> p c h"
                    nc.vector.scalar_tensor_tensor(out=U.rearrange(v, c=NCH), in0=DT.rearrange(v, c=NCH), scalar=-1.0,
                                                   in1=small[:, 0:32].unsqueeze(1).to_broadcast([P, NCH, 32]),
                                                   op0=ALU.mult, op1=ALU.mult).then_inc(a_ready, 1)
            with phase("summed", "kept", "turned", "t_kept") as (block, summed, kept, turned, t_kept):
                @block.tensor
                def _(pe):
                    for c in range(NCH):
                        for back in range(2):
                            o = psum[:, 0, c * 32 + back * 16:c * 32 + back * 16 + 16]
                            others = range(c + 1, NCH) if back else range(c)
                            for n, i in enumerate(list(others) + [c]):
                                lhs = con("ones") if i != c else (con("ge") if back else con("le"))
                                mm = nc.tensor.matmul(o, lhs, U[:, i * 32 + back * 16:i * 32 + back * 16 + 16],
                                                      start=(n == 0), stop=(i == c))
                    mm.then_inc(summed, 1)
                    pe.wait_ge(kept, 1)
                    for c in range(NCH):
                        tr = nc.tensor.transpose(psum[0:32, 1, c * P:(c + 1) * P], AC[:, c * 32:(c + 1) * 32], con("ident"))
                    tr.then_inc(turned, 1)

                @block.vector
                def _(dve):
                    dve.wait_ge(summed, 1)
                    nc.vector.tensor_copy(AC, psum[:, 0, 0:128]).then_inc(kept, 1)
                    dve.wait_ge(turned, 1)
                    nc.vector.tensor_copy(rows[0:32, 2, :], psum[0:32, 1, :]).then_inc(t_kept, 1)

        def ssd():
            XN, Z, XS, BT, CT, XT = 0, 20, 28, 36, 40, 44
            DT, AC = rows[:, 3, 128:256], rows[:, 3, 256:384]
            xt = span(XT, 8).rearrange("p (c f) -> p c f", c=NCH)
            yt = span(XN, 8).rearrange("p (c f) -> p c f", c=NCH)
            to_tokens(lambda j: arena[:, XS + j, :], KD, xt)
            W5 = 5 * P
            bcm = span(52, 5).rearrange("p (i f) -> p i f", i=4)
            for grp in range(4):
                with phase("bc_done", "bc_kept") as (block, bc_done, bc_kept):
                    @block.tensor
                    def _(pe):
                        for i in range(4):
                            nc.tensor.matmul(psum[:, i, :], arena[:, BT + grp, i * P:(i + 1) * P], arena[:, CT + grp, :],
                                             start=True, stop=True).then_inc(bc_done, 1)

                    @block.vector
                    def _(dve):
                        for i in range(4):
                            dve.wait_ge(bc_done, i + 1)
                            s = slice(i * P, (i + 1) * P)
                            if i:
                                nc.vector.tensor_copy(bcm[:, i, 0:i * P], psum[:, i, 0:i * P]).then_inc(bc_kept, 1)
                            if i < 3:
                                nc.vector.tensor_copy(bcm[:, i, (i + 2) * P:W5], psum[:, i, (i + 1) * P:T]).then_inc(bc_kept, 1)
                            nc.vector.tensor_tensor(bcm[:, i, i * P:(i + 1) * P], psum[:, i, s], con("ge"), ALU.mult).then_inc(bc_kept, 1)
                            nc.vector.tensor_tensor(bcm[:, i, (i + 1) * P:(i + 2) * P], psum[:, i, s], con("le"), ALU.mult).then_inc(bc_kept, 1)
                with phase("cast", "argued", "expd", "weighted", "y_done", "y_kept") as \
                        (block, spread_done, argued, expd, weighted, y_done, y_kept):
                    gs = span(57, 7)[:, 0:5 * W5].rearrange("p (i f) -> p i f", i=5)

                    def slot(u):
                        return gs[:, u % 5, :]

                    @block.tensor
                    def _(pe):
                        def spread(hh):
                            h = grp * 4 + hh
                            if hh >= 2:
                                pe.wait_ge(argued, 8 * (hh - 1))
                            for back in range(2):
                                mm = nc.tensor.matmul(psum[:, 2 * (hh % 2) + back, :],
                                                      con("ident", 1, h + 16 * back, 32).to_broadcast([32, P]),
                                                      rows[0:32, 2, :], start=True, stop=True)
                            mm.then_inc(spread_done, 1)
                        spread(0)
                        for hh in range(4):
                            h = grp * 4 + hh
                            if hh < 3:
                                spread(hh + 1)
                            if hh >= 1:
                                pe.wait_ge(y_kept, hh)
                            for i in range(4):
                                pe.wait_ge(weighted, 2 * (4 * hh + i) + 2)
                                g = slot(4 * hh + i)
                                x = xt[:, i, h * HD:(h + 1) * HD]
                                for j in range(4):
                                    if j <= i:
                                        mm = nc.tensor.matmul(psum[:, 4 + j, 0:HD], g[:, j * P:(j + 1) * P], x,
                                                              start=(i == 0), stop=(i == 3 and j < 3))
                                    if j >= i:
                                        mm = nc.tensor.matmul(psum[:, 4 + j, 0:HD], g[:, (j + 1) * P:(j + 2) * P], x,
                                                              start=(i == 0 and j > 0), stop=(i == 3))
                                mm.then_inc(y_done, 1)

                    @block.vector
                    def _(dve):
                        def argue(u):
                            hh, i = u // 4, u % 4
                            h = grp * 4 + hh
                            if u >= 5:
                                dve.wait_ge(y_done, u - 4)
                            dve.wait_ge(spread_done, hh + 1)
                            g = slot(u)
                            nc.vector.tensor_scalar(g[:, 0:(i + 1) * P], psum[:, 2 * (hh % 2) + 1, 0:(i + 1) * P],
                                                    AC[:, i * 32 + 16 + h:i * 32 + 17 + h], 0.0, ALU.subtract, ALU.min).then_inc(argued, 1)
                            nc.vector.tensor_scalar(g[:, (i + 1) * P:W5], psum[:, 2 * (hh % 2), i * P:T],
                                                    AC[:, i * 32 + h:i * 32 + 1 + h], 0.0, ALU.subtract, ALU.min).then_inc(argued, 1)

                        def weigh(u):
                            hh, i = u // 4, u % 4
                            h = grp * 4 + hh
                            g = slot(u)
                            dve.wait_ge(expd, u + 1)
                            for lo, hi, d in ((0, (i + 1) * P, 16 + h), ((i + 1) * P, W5, h)):
                                nc.vector.scalar_tensor_tensor(out=g[:, lo:hi], in0=g[:, lo:hi],
                                                               scalar=DT[:, i * 32 + d:i * 32 + d + 1], in1=bcm[:, i, lo:hi],
                                                               op0=ALU.mult, op1=ALU.mult).then_inc(weighted, 1)
                        argue(0)
                        argue(1)
                        for u in range(16):
                            if u < 14:
                                argue(u + 2)
                            weigh(u)

                    @block.scalar
                    def _(act):
                        def keep(hh):
                            h = grp * 4 + hh
                            act.wait_ge(y_done, 4 * hh + 4)
                            nc.scalar.activation(yt[:, :, h * HD:(h + 1) * HD], psum[:, 4:8, 0:HD], ACT.Copy).then_inc(y_kept, 1)
                        for u in range(16):
                            act.wait_ge(argued, 2 * u + 2)
                            nc.scalar.activation(slot(u), slot(u), ACT.Exp).then_inc(expd, 1)
                            if u % 4 == 1 and u > 4:
                                keep(u // 4 - 1)
                        keep(3)
            def take(eng, j, bank):
                x = arena[:, XS + j, :]
                return nc.vector.scalar_tensor_tensor(out=x, in0=x, scalar=col("ssd_D", j), in1=bank, op0=ALU.mult, op1=ALU.add)
            transposes(KD, lambda j, b: yt[:, b, j * P:(j + 1) * P], take, engines=("vector",))
            with phase("gated_") as (block, gated):
                @block.vector
                def _(dve):
                    nc.vector.tensor_tensor(span(XS, 8), span(XS, 8), span(Z, 8), ALU.mult).then_inc(gated, 1)
            norm(lambda i: arena[:, XS + i, :], None, KD, 4,
                 lambda i: con("group_rows", 4, 3 - i // 2), lambda i: con("ident", 1, i // 2, 4).to_broadcast([4, P]),
                 lambda i: col("ssd_g", i), 1.0 / 256, 1e-6, ALU.add, parts=two_parts(XN, XS))

        def neighbourhood():
            Q, K, V, KP, VT, OT = 8, 12, 16, 20, 48, 44
            norm(lambda i: arena[:, Q + i, :], lambda i: arena[:, Q + i, :], 8, 32, head_sums, head_spread,
                 lambda i: col("na_qk", i), 1.0 / HD, 1e-6, ALU.add)
            key_halves([(h % 2, K + h // 2) for h in range(8)], KP)
            vt = span(VT, 4).rearrange("p (c f) -> p c f", c=NCH)
            to_tokens(lambda j: arena[:, V + j, :], 4, vt)
            ot = span(OT, 4).rearrange("p (c f) -> p c f", c=NCH)
            win = [span(52, 2)[:, 0:14 * 64], span(54, 2)[:, 0:14 * 64]]
            units = []
            for h in range(8):
                for qt in range(4):
                    units.append((arena[:, Q + h // 2, qt * P:(qt + 1) * P], arena[:, KP + h, :],
                                  lambda b, h=h: vt[:, b, h * HD:(h + 1) * HD], ot[:, qt, h * HD:(h + 1) * HD]))

            def bias(u):
                lo = (6 - 2 * (u % 4)) * 64
                return win[(u // 4) % 2][:, lo:lo + T]

            def before(block, bias_ready, bias_loaded, biased):
                @block.sync
                def _(sp):
                    for h in range(8):
                        if h >= 2:
                            sp.wait_ge(biased, 4 * (h - 1))
                        if h >= 1:
                            sp.wait_ge(bias_loaded, 32 * h)
                        w = win[h % 2].rearrange("p (d k) -> p d k", k=64)
                        for rr in range(2):
                            sp.dma_start(w[rr * 64:(rr + 1) * 64, :, :],
                                         dram["na_bias"][h, 1 - rr:15 - rr, :, :].rearrange("d c k -> c d k"))\
                                .then_inc(bias_loaded, 16)

                @block.gpsimd
                def _(pool):
                    for h in range(8):
                        pool.wait_ge(bias_loaded, 32 * (h + 1))
                        w = win[h % 2].rearrange("p (d k) -> p d k", k=64)
                        nc.gpsimd.tensor_tensor(w, w, con("window", 64).unsqueeze(1).to_broadcast([P, 14, 64]),
                                                ALU.add).then_inc(bias_ready, 1)
            attention(units, [arena[:, 56, :], arena[:, 57, :]], [arena[:, 58 + i, :] for i in range(3)],
                      [arena[:, 61, :], arena[:, 62, :]], bias, before)
            transposes(4, lambda j, b: ot[:, b, j * P:(j + 1) * P],
                       lambda eng, j, bank: copy_on(eng, arena[:, Q + j, :], bank))
            split_tiles(4, lambda i: arena[:, Q + i, :], two_parts(K, Q, 4))

        def gqa():
            XN, Q, K, V, COS, SIN, VT, OT = 0, 8, 16, 18, 20, 21, 22, 24
            rms_norm(lambda i: resid[:, i, :], None, KD, lambda i: col("odd_g", i), parts=two_parts(XN, OT))
            with phase("taken", "rope_loaded") as (block, taken, rope_loaded):
                @block.sync
                def _(sp):
                    sp.dma_start(span(COS, 2), dram["rope"]).then_inc(rope_loaded, 16)
                    load_stream(sp, "qkv")
                    sp.wait_ge(rope_loaded, 16)

                @block.tensor
                def _(pe):
                    products(pe, "qkv", two_parts(XN, OT), taken)

                @block.scalar
                def _(act):
                    def read(g, m, done):
                        done()
                        nc.scalar.activation(tile_of(arena, g * R + (m + Q)), psum[:, m, :], ACT.Copy).then_inc(taken, 1)
                    split_and_read(act, "qkv", split_high, read)

                @block.vector
                def _(dve):
                    split_and_read(dve, "qkv", split_low)
            norm(lambda i: arena[:, Q + i, :], lambda i: arena[:, Q + i, :], 10, 32, head_sums, head_spread,
                 lambda i: col("gqa_qk", i), 1.0 / HD, 1e-6, ALU.add)
            with phase("rotated", "sin_done", "cos_done", "roped") as (block, rotated, sin_done, cos_done, roped):
                @block.tensor
                def _(pe):
                    for i in range(10):
                        if i >= 4:
                            pe.wait_ge(sin_done, i - 3)
                        nc.tensor.matmul(psum[:, i % 4, :], con("rot"), arena[:, Q + i, :], start=True, stop=True).then_inc(rotated, 1)

                @block.vector
                def _(dve):
                    for i in range(10):
                        dve.wait_ge(rotated, i + 1)
                        if i >= 4:
                            dve.wait_ge(roped, i - 3)
                        x = arena[:, Q + i, :]
                        nc.vector.tensor_tensor(work[:, i % 4, :], psum[:, i % 4, :], arena[:, SIN, :], ALU.mult).then_inc(sin_done, 1)
                        nc.vector.tensor_tensor(x, x, arena[:, COS, :], ALU.mult).then_inc(cos_done, 1)
                        dve.wait_ge(sin_done, i + 1)
                        dve.wait_ge(cos_done, i + 1)
                        nc.vector.tensor_tensor(x, x, work[:, i % 4, :], ALU.add).then_inc(roped, 1)
            key_halves([(kv % 2, K + kv // 2) for kv in range(4)], 40)
            vt = span(VT, 2).rearrange("p (c f) -> p c f", c=NCH)
            to_tokens(lambda j: arena[:, V + j, :], 2, vt)
            ot = span(OT, 8).rearrange("p (c f) -> p c f", c=NCH)
            units = []
            for n in range(NH):
                j, e = n // 2, n % 2
                h = (j if j < 4 else j + 4) + 4 * e
                kv = h // 4
                for qt in range(4):
                    units.append((arena[:, Q + j, qt * P:(qt + 1) * P], arena[:, 40 + kv, :],
                                  lambda b, kv=kv: vt[:, b, kv * HD:(kv + 1) * HD], ot[:, qt, h * HD:(h + 1) * HD]))
            attention(units, None, [arena[:, 32 + i, :] for i in range(3)], [arena[:, 35, :], arena[:, 36, :]], None, None)
            transposes(KD, lambda j, b: ot[:, b, j * P:(j + 1) * P],
                       lambda eng, j, bank: copy_on(eng, arena[:, Q + j, :], bank))
            split_tiles(KD, lambda i: arena[:, Q + i, :], two_parts(XN, Q))
            add_projection("odd_out", two_parts(XN, Q))

        def final_norm():
            rms_norm(lambda i: resid[:, i, :], lambda i: resid[:, i, :], KD, lambda i: col("final_g", i))

        def even():
            even_in()
            ssd()
            neighbourhood()
            add_projection("even_out", lambda k: two_parts(12, 8, 4)(k) if k < 4 else two_parts(0, 28)(k - 4))

        stages = [sgu, lambda: conv_ffn(0), rwkv, lambda: conv_ffn(1), final_norm, even,
                  lambda: swiglu(0), gqa, lambda: swiglu(1)]
        for n, stage in enumerate(stages):
            if first <= n < last:
                stage()
        with phase("stored") as (block, stored):
            @block.sync
            def _(sp):
                sp.dma_start(out, resid[:, :, :]).then_inc(stored, 16)
                sp.wait_ge(stored, 16)


def constants():
    i = np.arange(P)
    p, f = i[:, None], i[None, :]
    levels = []
    for b in (1, 2, 4, 8, 16, 32, 64):
        levels.append(((f // b) % 2 == 1) & (p // b == f // b - 1))
    rot = np.zeros((P, P), np.float32)
    even = np.arange(0, P, 2)
    rot[even + 1, even] = -1.0
    rot[even, even + 1] = 1.0
    c = np.arange(HD)
    start = np.clip(c - 8, 0, HD - 16)
    inside = (c[None, :] >= start[:, None]) & (c[None, :] < start[:, None] + 16)
    window = np.where(np.concatenate([inside, inside]), 0.0, -1e30)
    head_rows = np.zeros((P, 64), np.float32)
    head_rows[i, 30 + i // HD] = 1.0
    head_cols = np.zeros((P, 10, P), np.float32)
    for t in range(10):
        for e in range(2):
            head_cols[2 * t + e, t, e * HD:(e + 1) * HD] = 1.0
    halves = np.zeros((P, 2), np.float32)
    halves[i, i // HD] = 1.0
    group_rows = np.zeros((P, 7), np.float32)
    group_rows[:, 3] = 1.0
    parts = dict(ident=np.eye(P), le=p <= f, lt=p < f, ge=p >= f, levels=np.concatenate(levels, 1),
                 pair_low=levels[0].T, ones=np.ones((P, P)), rot=rot, window=window, head_rows=head_rows,
                 head_cols=head_cols.reshape(P, -1), halves=halves, group_rows=group_rows)
    return np.concatenate([np.asarray(parts[n], np.float32) for n, _ in CONST_PARTS], 1)


def rope_tables():
    t = np.arange(T)
    freqs = (10000.0 ** (-np.arange(0, 32, 2, dtype=np.float32) / np.float32(32))).astype(np.float32)
    ang = np.concatenate([(t // 64).astype(np.float32)[:, None] * freqs, (t % 64).astype(np.float32)[:, None] * freqs], 1)
    def table(x):
        x = np.repeat(x.T, 2, axis=0).astype(np.float32)
        return np.concatenate([x, x], 0)
    return np.concatenate([table(np.cos(ang)), table(np.sin(ang))], 1)


def layouts(a):
    def blocks(w, order=None):
        k, m = w.shape
        w = w.reshape(k // P, P, m // P, P).transpose(2, 1, 0, 3)
        if order is not None:
            w = w[order]
        return np.ascontiguousarray(w.reshape(m // P, P, k))

    def cols(v):
        return v.reshape(-1, P).T

    def turns(n):
        return np.stack([np.arange(n), np.arange(n) + n], 1).reshape(-1)

    d = {}
    d["x"] = np.ascontiguousarray(a["x"][0].T.reshape(KD, P, T).transpose(1, 0, 2))
    d["const"] = constants()
    d["rope"] = rope_tables()
    pair = turns(KF)
    d["sgu_in"] = blocks(a["sgu_w_in"][0])
    d["sgu_out"] = blocks(a["sgu_w_out"][0])
    d["sgu_ws"] = np.ascontiguousarray(a["sgu_w_s"][0].transpose(2, 0, 1).reshape(P, -1))
    for l in range(2):
        d[f"up{l}"] = blocks(a["ffn_w_up"][l], order=pair)
        d[f"down{l}"] = blocks(a["ffn_w_down"][l])
        d[f"up{l + 2}"] = blocks(a["ffn_w13_2"][l], order=pair)
        d[f"down{l + 2}"] = blocks(a["ffn_w2_2"][l])
    for n in "rkvo":
        d[f"rwkv_{n}"] = blocks(a[f"rwkv_w_{n}"][0])
    lora1 = np.concatenate([a["rwkv_w1"][0], a["rwkv_a1"][0], a["rwkv_g1"][0]], 1)
    d["lora1"] = np.ascontiguousarray(lora1.reshape(KD, P, 288).transpose(1, 0, 2).reshape(P, -1))
    d["lora_w2"] = a["rwkv_w2"][0]
    d["lora_a2"] = a["rwkv_a2"][0]
    d["lora_g2"] = a["rwkv_g2"][0]
    even = a["even_w_in_2"][0]
    d["even_in"] = blocks(np.ascontiguousarray(even[:, :4608]))
    d["even_dt"] = np.ascontiguousarray(even[:, 4608:].reshape(KD, P, 32).transpose(1, 0, 2).reshape(P, -1))
    d["even_out"] = blocks(a["even_w_out_2"][0])
    heads = [(j if j < 4 else j + 4) + 4 * e for j in range(8) for e in range(2)]
    qcols = np.concatenate([np.arange(h * HD, (h + 1) * HD) for h in heads] + [np.arange(1024, 1536)])
    d["qkv"] = blocks(a["odd_w_qkv_2"][0][:, qcols])
    d["odd_out"] = blocks(a["odd_w_out_2"][0])
    rpb = np.pad(a["na_rel_bias_2"][0], ((0, 0), (0, 0), (48, 48)))
    c = np.arange(HD)
    d["na_bias"] = np.ascontiguousarray(rpb[:, :, 63 + c[None, :] - c[:, None]])
    spread = lambda v: np.broadcast_to(v, (P, v.size))
    twice = lambda v: np.concatenate([v, v])[:, None]
    vectors = dict(
        mix_g=cols(a["norm_mix_g"]), ffn_g=cols(a["norm_ffn_g"]), final_g=cols(a["norm_final_g"]),
        sgu_b=cols(a["sgu_b_in"]), sgu_gv=cols(a["sgu_g_v"]), sgu_bs=a["sgu_b_s"][0].T, mu=cols(a["rwkv_mu"]),
        w0=cols(a["rwkv_w0"]), a0=cols(a["rwkv_a0"]), k_k=cols(a["rwkv_k_k"]), k_a=cols(a["rwkv_k_a"]),
        r_k=cols(a["rwkv_r_k"]), ln_w=cols(a["rwkv_ln_w"]), ln_b=cols(a["rwkv_ln_b"]),
        conv_w=np.concatenate([cols(a["ffn_conv_w"][l, j])[:, pair] for l in range(2) for j in range(3)], 1),
        conv_b=np.concatenate([cols(a["ffn_conv_b"][l])[:, pair] for l in range(2)], 1),
        even_g=cols(a["even_mix_norm_2"]), ssd_cw=cols(a["ssd_conv_w_2"]), ssd_cb=cols(a["ssd_conv_b_2"]),
        ssd_D=cols(np.repeat(a["ssd_D_2"][0], HD)), ssd_g=cols(a["ssd_out_norm_2"]),
        dt_bias=spread(a["ssd_dt_bias_2"].reshape(-1)), A_log=spread(a["ssd_A_log_2"].reshape(-1)),
        na_qk=np.concatenate([twice(a["na_q_norm_2"][0])] * 4 + [twice(a["na_k_norm_2"][0])] * 4, 1),
        odd_g=cols(a["odd_mix_norm_2"]),
        gqa_qk=np.concatenate([twice(a["gqa_q_norm_2"][0])] * 8 + [twice(a["gqa_k_norm_2"][0])] * 2, 1),
        ffn2_g=cols(a["ffn_norm_2"]))
    d["vec"] = np.ascontiguousarray(np.concatenate([vectors[n] for n, _ in VECTOR_PARTS], 1))
    return d


def kernel(**inputs):
    import concourse.bacc as bacc
    from concourse.bass_utils import run_bass_kernel_spmd

    arrays = layouts({k: np.asarray(v) for k, v in inputs.items()})
    nc = bacc.Bacc("TRN2", target_bir_lowering=False, num_devices=1)
    dram = {k: nc.dram_tensor(f"in_{k}", v.shape, F32, kind="ExternalInput").ap() for k, v in arrays.items()}
    out = nc.dram_tensor("out", (P, KD, T), F32, kind="ExternalOutput").ap()
    build(nc, dram, out)
    result = run_bass_kernel_spmd(nc, [{f"in_{k}": v for k, v in arrays.items()}], core_ids=[0])
    y = result.results[0]["out"]
    return np.ascontiguousarray(y.transpose(1, 0, 2).reshape(D, T).T)[None]
```

```python
from contextlib import ExitStack, contextmanager

import numpy as np

import concourse.bass as bass
from concourse import mybir

F32 = mybir.dt.float32
F32R = mybir.dt.float32r
ACT = mybir.ActivationFunctionType
ALU = mybir.AluOpType
AX = mybir.AxisListType.X

P = 128
T = 512
D = 1024
KD = D // P
CH = 128
NCH = T // CH
FFN = 2816
KF = FFN // P
HD = 64
NH = 16
R = 4
HIGHS = 2
SLOT_BLOCKS = 8
EXP_HALF = float(np.exp(-0.5))

PARTS = {8: [(0, 8)], 12: [(0, 6), (6, 6)], 22: [(0, 6), (6, 6), (12, 5), (17, 5)]}
CONST_PARTS = [("ident", P), ("le", P), ("lt", P), ("ge", P), ("levels", 7 * P), ("pair_low", P),
               ("ones", P), ("rot", P), ("window", HD), ("head_rows", 160), ("head_cols", 10 * P), ("halves", 2), ("group_rows", 132)]
VECTOR_PARTS = [("mix_g", 16), ("ffn_g", 16), ("final_g", 8), ("sgu_b", 16), ("sgu_gv", 8), ("sgu_bs", 16),
                ("mu", 48), ("w0", 8), ("a0", 8), ("k_k", 8), ("k_a", 8), ("r_k", 8), ("ln_w", 8), ("ln_b", 8),
                ("conv_w", 264), ("conv_b", 88), ("even_g", 8), ("ssd_cw", 64), ("ssd_cb", 16),
                ("ssd_D", 8), ("ssd_g", 8), ("dt_bias", 32), ("A_log", 32), ("na_qk", 8), ("odd_g", 8),
                ("gqa_qk", 10), ("ffn2_g", 16)]


def places(parts):
    at, out = 0, {}
    for name, n in parts:
        out[name] = at
        at += n
    return out, at


CONST_AT, CONST_COLS = places(CONST_PARTS)
VECTOR_AT, VECTOR_COLS = places(VECTOR_PARTS)


def build(nc, dram, out):
    with ExitStack() as whole:
        def sbuf(name, shape):
            return whole.enter_context(nc.sbuf_tensor(name, shape, F32))

        def alias(name, at, shape):
            return nc.alloc_sbuf_tensor_at(name, shape, F32R, offset=at)

        arena_at = -(-nc.sbuf_base // 32) * 32
        arena = sbuf("arena", [P, 64, T])
        resid = sbuf("resid", [P, KD, T])
        ring_at = -(-nc.sbuf_base // 32) * 32
        ring = sbuf("ring", [P, R, SLOT_BLOCKS * P])
        ring_low = alias("ring_low", ring_at, [P, R, SLOT_BLOCKS * P])
        high_at = -(-nc.sbuf_base // 32) * 32
        high_r = whole.enter_context(nc.sbuf_tensor("high_r", [P, HIGHS, SLOT_BLOCKS * P], F32R))
        spare = nc.alloc_sbuf_tensor_at("spare", [P, 4, T], F32, offset=high_at)
        const = sbuf("const", [P, CONST_COLS])
        vec = sbuf("vec", [P, VECTOR_COLS])
        work = sbuf("work", [P, 4, T])
        rows = sbuf("rows", [P, 4, T])
        roots = sbuf("roots", [P, NCH * NH])
        small = sbuf("small", [P, 192])
        psum = whole.enter_context(nc.psum_tensor("psum", [P, 8, T], F32))

        slot_filled = [whole.enter_context(nc.semaphore(f"slot_filled{r}")) for r in range(R)]
        unit_done = whole.enter_context(nc.semaphore("unit_done"))
        unit_high = whole.enter_context(nc.semaphore("unit_high"))
        unit_low = whole.enter_context(nc.semaphore("unit_low"))

        input_scaled, input_high, input_low = (whole.enter_context(nc.semaphore(f"input_{n}")) for n in ("scaled", "high", "low"))

        phases = [0]

        @contextmanager
        def phase(*names):
            sems = [nc.alloc_semaphore(f"{n}_{phases[0]}") for n in names]
            phases[0] += 1
            with nc.Block() as block:
                yield block, *sems
            for s in sems:
                nc.gpsimd.sem_clear(s)
                nc.release_semaphore(s)

        seen = {}

        def rounded(start, n=8):
            if (start, n) not in seen:
                seen[start, n] = alias(f"rounded_{start}_{n}", arena_at + start * T * 4, [P, n, T])
            return seen[start, n]

        def two_parts(high_at, low_at, n=8):
            return lambda k: (rounded(high_at, n)[:, k, :], rounded(low_at, n)[:, k, :])

        def con(name, width=P, off=0, rows_=P):
            a = CONST_AT[name] + off
            return const[0:rows_, a:a + width]

        def col(name, i=0, n=1, rows_=slice(0, P)):
            a = VECTOR_AT[name] + i
            if isinstance(i, int):
                return vec[rows_, a:a + n]
            return vec[rows_, bass.ds(a, n)]

        def tile_of(x, i):
            if isinstance(i, int):
                return x[:, i, :]
            return x[:, bass.ds(i, 1), :].rearrange("p a t -> p (a t)")

        def flat(x):
            return x.rearrange("p a t -> p (a t)")

        def span(i, n):
            return flat(arena[:, i:i + n, :])

        ORDER = ["sgu_in", "sgu_out", "up0", "down0", "rwkv_r", "rwkv_k", "rwkv_v", "rwkv_o", "up1", "down1",
                 "even_in", "even_out", "up2", "down2", "qkv", "odd_out", "up3", "down3"]
        SPLIT_LATE = ("sgu_in", "rwkv_o", "even_out")
        first_unit, n_units = {}, 0
        for name in ORDER:
            first_unit[name] = n_units
            n_units += dram[name].shape[0] * len(PARTS[dram[name].shape[2] // P])

        class Stream:
            def __init__(self, name):
                self.name, self.w = name, dram[name]
                self.parts = PARTS[self.w.shape[2] // P]
                self.units = self.w.shape[0] * len(self.parts)
                self.first = first_unit[name]
                self.body = max(R, 2 * len(self.parts))
                self.groups = self.units // self.body
                self.tiles = self.body // len(self.parts)

            def place(self, r):
                m, part = divmod(r, len(self.parts))
                k0, nk = self.parts[part]
                return m, k0, nk, part == len(self.parts) - 1

        def loop(eng, groups, body):
            body(0)
            if groups > 2:
                with eng.Fori(1, groups - 1) as g:
                    body(g)
            if groups > 1:
                body(groups - 1)

        def wait(eng, sem, value):
            if not isinstance(value, int) or value > 0:
                eng.wait_ge(sem, value)

        def load_unit(sp, st, g, r):
            m, k0, nk, _ = st.place(r)
            if isinstance(g, int):
                src = st.w[g * st.tiles + m]
            else:
                src = st.w[bass.ds(g * st.tiles + m, 1)].rearrange("a p n -> (a p) n")
            sp.dma_start(ring[:, r % R, 0:nk * P], src[:, k0 * P:(k0 + nk) * P]).then_inc(slot_filled[r % R], 16)

        def load_stream(sp, name):
            st = Stream(name)

            def body(g):
                for r in range(st.body):
                    if isinstance(g, int) and g == 0 and r < R:
                        continue
                    sp.wait_ge(unit_done, g * st.body + (st.first - R + r + 1))
                    load_unit(sp, st, g, r)
            loop(sp, st.groups, body)
            at = ORDER.index(name) + 1
            if at < len(ORDER):
                for r in range(R):
                    sp.wait_ge(unit_done, st.first + st.units - R + r + 1)
                    load_unit(sp, Stream(ORDER[at]), 0, r)

        class Inputs:
            tiles_before = [0, 0]

            def __init__(self, n, src, parts, gain=None):
                self.n, self.src, self.parts, self.gain = n, src, parts, gain
                self.scaled_before, self.before = self.tiles_before
                self.tiles_before[0] += n if gain else 0
                self.tiles_before[1] += n

            def whole_tile(self, i):
                return rows[:, 2 + i % 2, :] if self.gain else self.src(i)

            def high(self, act):
                for i in range(self.n):
                    if self.gain:
                        act.wait_ge(input_scaled, self.scaled_before + i + 1)
                    nc.scalar.activation(self.parts(i)[0], self.whole_tile(i), ACT.Copy).then_inc(input_high, 1)

            def low(self, dve):
                def rest(i):
                    dve.wait_ge(input_high, self.before + i + 1)
                    nc.vector.tensor_tensor(self.parts(i)[1], self.whole_tile(i), self.parts(i)[0].bitcast(F32),
                                            ALU.subtract).then_inc(input_low, 1)
                for i in range(self.n):
                    if self.gain:
                        if i >= 2:
                            dve.wait_ge(input_low, self.before + i - 1)
                        nc.vector.scalar_tensor_tensor(out=self.whole_tile(i), in0=self.src(i), scalar=self.gain(i), in1=rows[:, 0, :],
                                                       op0=ALU.mult, op1=ALU.mult).then_inc(input_scaled, 1)
                        if i:
                            rest(i - 1)
                    else:
                        rest(i)
                if self.gain:
                    rest(self.n - 1)

        def products(pe, name, rhs, taken, inputs=None):
            st = Stream(name)

            def body(g):
                for r in range(st.body):
                    m, k0, nk, last = st.place(r)
                    wait(pe, unit_low, g * st.body + (st.first + r + 1))
                    if k0 == 0:
                        wait(pe, taken, g * st.tiles + (m + 1 - st.tiles))
                    for k in range(nk):
                        if inputs and isinstance(g, int) and g == 0 and m == 0:
                            pe.wait_ge(input_low, inputs.before + k0 + k + 1)
                        x_high, x_low = rhs(k0 + k)
                        blk = slice(k * P, (k + 1) * P)
                        end = last and k == nk - 1
                        nc.tensor.matmul(psum[:, m, :], high_r[:, r % HIGHS, blk], x_high,
                                         start=(k0 + k == 0), stop=False)
                        nc.tensor.matmul(psum[:, m, :], high_r[:, r % HIGHS, blk], x_low,
                                         start=False, stop=False)
                        mm = nc.tensor.matmul(psum[:, m, :], ring_low[:, r % R, blk], x_high,
                                              start=False, stop=end)
                    mm.then_inc(unit_done, 1)
            loop(pe, st.groups, body)

        def split_high(act, st, g, r):
            nk = st.place(r % st.body)[2]
            n = g * st.body + (st.first + r)
            turn = g * (16 * st.body // R) + 16 * ((st.first + r) // R + 1)
            act.wait_ge(slot_filled[r % R], turn)
            wait(act, unit_done, n + (1 - HIGHS))
            nc.scalar.activation(high_r[:, r % HIGHS, 0:nk * P], ring[:, r % R, 0:nk * P], ACT.Copy).then_inc(unit_high, 1)

        def split_low(dve, st, g, r):
            nk = st.place(r % st.body)[2]
            dve.wait_ge(unit_high, g * st.body + (st.first + r + 1))
            nc.vector.tensor_tensor(ring_low[:, r % R, 0:nk * P], ring[:, r % R, 0:nk * P],
                                    high_r[:, r % HIGHS, 0:nk * P].bitcast(F32), ALU.subtract).then_inc(unit_low, 1)

        def split_and_read(eng, name, split, read=None, groups=None, inputs=None):
            st = Stream(name)

            def body_of(read):
                def body(g):
                    for r in range(st.body):
                        if not (isinstance(g, int) and g == st.groups - 1 and r == st.body - 1):
                            split(eng, st, g, r + 1)
                        elif following and following not in SPLIT_LATE:
                            split(eng, Stream(following), 0, 0)
                        m, _, _, last = st.place(r)
                        if last and read:
                            read(g, m, lambda: eng.wait_ge(unit_done, g * st.body + (st.first + r + 1)))
                return body
            following = (ORDER + [None])[ORDER.index(name) + 1]
            if name in SPLIT_LATE:
                split(eng, st, 0, 0)
            if inputs:
                (inputs.high if split is split_high else inputs.low)(eng)
            for read_, lo, hi in groups or [(read, 0, st.groups)]:
                body = body_of(read_)
                g = lo
                if g == 0 or hi - lo == 1:
                    body(g)
                    g += 1
                end = hi - 1 if hi == st.groups else hi
                if end > g:
                    with eng.Fori(g, end) as i:
                        body(i)
                if end < hi and end >= g:
                    body(end)

        square_sum = work[:, 2, :]

        def add_projection(name, rhs, inputs=None):
            with phase("taken", "squared", "squares_summed") as (block, taken, squared, squares_summed):
                @block.gpsimd
                def _(pool):
                    for i in range(KD if name != ORDER[-1] else 0):
                        x, square = resid[:, i, :], work[:, i % 2, :] if i else square_sum
                        pool.wait_ge(taken, i + 1)
                        if i >= 3:
                            pool.wait_ge(squares_summed, i - 2)
                        nc.gpsimd.tensor_tensor(square, x, x, ALU.mult).then_inc(squared, 1)
                        if i:
                            pool.wait_ge(squared, i + 1)
                            if i >= 2:
                                pool.wait_ge(squares_summed, i - 1)
                            nc.gpsimd.tensor_tensor(square_sum, square_sum, square, ALU.add).then_inc(squares_summed, 1)

                @block.sync
                def _(sp):
                    load_stream(sp, name)

                @block.tensor
                def _(pe):
                    products(pe, name, rhs, taken, inputs)

                @block.scalar
                def _(act):
                    split_and_read(act, name, split_high, inputs=inputs)

                @block.vector
                def _(dve):
                    tiles = Stream(name).tiles

                    def read(g, m, done):
                        done()
                        x = tile_of(resid, g * tiles + m)
                        nc.vector.tensor_tensor(x, psum[:, m, :], x, ALU.add).then_inc(taken, 1)
                    split_and_read(dve, name, split_low, read, inputs=inputs)

        def split_tiles(n, src, parts):
            with phase("high_done", "low_done") as (block, high_done, low_done):
                @block.scalar
                def _(act):
                    for i in range(n):
                        nc.scalar.activation(parts(i)[0], src(i), ACT.Copy).then_inc(high_done, 1)

                @block.vector
                def _(dve):
                    for i in range(n):
                        dve.wait_ge(high_done, i + 1)
                        nc.vector.tensor_tensor(parts(i)[1], src(i), parts(i)[0].bitcast(F32),
                                                ALU.subtract).then_inc(low_done, 1)

        def norm(src, dst, n, gather, spread, gain, scale, guard, guard_op, parts=None, squares_ready=False):
            with phase("squared", "summed", "guarded", "rooted", "inverted", "spread_done", "scaled", "high_done",
                       "low_done") as \
                    (block, squared, summed, guarded, rooted, inverted, spread_done, scaled, high_done, low_done):
                sums = 1 if squares_ready else n
                one = spread is None
                leave = one and parts is not None

                @block.scalar
                def _(act):
                    for i in range(0 if squares_ready else n):
                        if i >= 4:
                            act.wait_ge(summed, i - 3)
                        nc.scalar.activation(work[:, i % 4, :], src(i), ACT.Square).then_inc(squared, 1)
                    act.wait_ge(guarded, 1)
                    nc.scalar.activation(rows[:, 1, :], rows[:, 0, :], ACT.Sqrt).then_inc(rooted, 1)
                    for i in range(n if parts and not leave else 0):
                        act.wait_ge(scaled, i + 1)
                        nc.scalar.activation(parts(i)[0], rows[:, 2 + i % 2, :], ACT.Copy).then_inc(high_done, 1)

                @block.tensor
                def _(pe):
                    for i in range(sums):
                        if not squares_ready:
                            pe.wait_ge(squared, i + 1)
                        nc.tensor.matmul(psum[:, 4, :], gather(i), square_sum if squares_ready else work[:, i % 4, :],
                                         start=(i == 0), stop=(i == sums - 1)).then_inc(summed, 1)
                    pe.wait_ge(inverted, 1)
                    for i in range(0 if one else n):
                        if i >= 2:
                            pe.wait_ge(scaled, i - 1)
                        nc.tensor.matmul(psum[:, 5 + i % 2, :], spread(i), rows[:, 0, :],
                                         start=True, stop=True).then_inc(spread_done, 1)

                def low(dve, i):
                    dve.wait_ge(high_done, i + 1)
                    nc.vector.tensor_tensor(parts(i)[1], rows[:, 2 + i % 2, :],
                                            parts(i)[0].bitcast(F32), ALU.subtract).then_inc(low_done, 1)

                @block.vector
                def _(dve):
                    dve.wait_ge(summed, sums)
                    nc.vector.tensor_scalar(rows[:, 0, :], psum[:, 4, :], scale, guard,
                                            ALU.mult, guard_op).then_inc(guarded, 1)
                    dve.wait_ge(rooted, 1)
                    nc.vector.reciprocal(rows[:, 0, :], rows[:, 1, :]).then_inc(inverted, 1)
                    for i in range(0 if leave else n):
                        if one:
                            dve.wait_ge(inverted, 1)
                        else:
                            dve.wait_ge(spread_done, i + 1)
                        if parts and i >= 2:
                            low(dve, i - 2)
                            dve.wait_ge(low_done, i - 1)
                        nc.vector.scalar_tensor_tensor(out=rows[:, 2 + i % 2, :] if parts else dst(i), in0=src(i),
                                                       scalar=gain(i), in1=rows[:, 0, :] if one else psum[:, 5 + i % 2, :],
                                                       op0=ALU.mult, op1=ALU.mult).then_inc(scaled, 1)
                    if parts and not leave:
                        low(dve, n - 2)
                        low(dve, n - 1)
            if leave:
                return Inputs(n, src, parts, gain)

        def rms_norm(src, dst, n, gain, eps=1e-6, parts=None, squares_ready=False):
            return norm(src, dst, n, lambda i: con("ones"), None, gain, 1.0 / (n * P), eps, ALU.add, parts, squares_ready)

        def head_sums(i):
            return con("head_rows", P, 30 - 2 * i)

        def head_spread(i):
            return con("head_cols", P, i * P)

        def transposes(n, src, read, engines=("scalar", "vector")):
            with phase("turned", "read_act", "read_dve") as (block, turned, read_act, read_dve):
                who = [engines[j % len(engines)] for j in range(n)]
                sem = {"scalar": read_act, "vector": read_dve}
                upto_ = [sum(w == who[j] for w in who[:j + 1]) for j in range(n)]

                @block.tensor
                def _(pe):
                    for j in range(n):
                        if j >= 8:
                            pe.wait_ge(sem[who[j - 8]], upto_[j - 8])
                        for b in range(4):
                            tr = nc.tensor.transpose(psum[:, j % 8, b * P:(b + 1) * P], src(j, b), con("ident"))
                        tr.then_inc(turned, 1)

                def reader(eng, name):
                    for j in range(n):
                        if who[j] == name:
                            eng.wait_ge(turned, j + 1)
                            read(name, j, psum[:, j % 8, :]).then_inc(sem[name], 1)

                @block.scalar
                def _(act):
                    reader(act, "scalar")

                @block.vector
                def _(dve):
                    reader(dve, "vector")

        def copy_on(eng, dst, src):
            if eng == "vector":
                return nc.vector.tensor_copy(dst, src)
            return nc.scalar.activation(dst, src, ACT.Copy)

        def by_chunk(bank):
            return bank.rearrange("p (c f) -> p c f", c=NCH)

        def to_tokens(src_tile, n, dst):
            transposes(n, lambda j, b: src_tile(j)[:, b * P:(b + 1) * P],
                       lambda eng, j, bank: copy_on(eng, dst[:, :, j * P:(j + 1) * P], by_chunk(bank)))

        XH, XL, HH, HL = 0, 8, 16, 16 + KF

        def ffn_input(gain):
            return rms_norm(lambda i: resid[:, i, :], None, KD, gain, parts=two_parts(XH, XL), squares_ready=True)

        def split_hidden(pool, st, multiplied, hidden_high, hidden_low):
            def body(g):
                for pair in range(st.tiles // 2):
                    n = g * (st.tiles // 2) + pair
                    pool.wait_ge(multiplied, n + 1)
                    nc.gpsimd.tensor_copy(tile_of(rounded(HH, KF), n), rows[:, 2 + pair, :]).then_inc(hidden_high, 1)
                    pool.wait_ge(hidden_high, n + 1)
                    nc.gpsimd.tensor_tensor(tile_of(rounded(HL, KF), n), rows[:, 2 + pair, :],
                                            tile_of(rounded(HH, KF), n).bitcast(F32), ALU.subtract).then_inc(hidden_low, 1)
            loop(pool, st.groups, body)

        def conv_ffn(layer):
            inputs = ffn_input(lambda i: col("ffn_g", layer * KD + i))
            name = f"up{layer}"
            cw, cb = VECTOR_AT["conv_w"] + layer * 132, VECTOR_AT["conv_b"] + layer * 44

            def v1(a):
                return vec[:, a:a + 1] if isinstance(a, int) else vec[:, bass.ds(a, 1)]

            with phase("biased", "conv_mid", "conv_done", "gated", "multiplied", "hidden_high", "hidden_low") as \
                    (block, biased, conv_mid, conv_done, gated, multiplied, hidden_high, hidden_low):
                st = Stream(name)

                @block.sync
                def _(sp):
                    load_stream(sp, name)

                @block.tensor
                def _(pe):
                    products(pe, name, two_parts(XH, XL), conv_done, inputs)

                @block.gpsimd
                def _(pool):
                    split_hidden(pool, st, multiplied, hidden_high, hidden_low)

                @block.scalar
                def _(act):
                    def read(g, r, done):
                        done()
                        wait(act, multiplied, g * 2 + (r // 2 + 1 - 2))
                        nc.scalar.activation(work[:, r, :], psum[:, r, :], ACT.Identity,
                                             bias=v1(g * R + (cb + r)), scale=v1(g * R + (cw + 88 + r))).then_inc(biased, 1)
                        if r % 2:
                            act.wait_ge(conv_done, g * R + r)
                            nc.scalar.activation(rows[:, r // 2, :], work[:, r - 1, :], ACT.Silu).then_inc(gated, 1)
                    split_and_read(act, name, split_high, read, inputs=inputs)

                @block.vector
                def _(dve):
                    def read(g, r, done):
                        dve.wait_ge(biased, g * R + (r + 1))
                        nc.vector.scalar_tensor_tensor(out=work[:, r, 1:T], in0=psum[:, r, 0:T - 1],
                                                       scalar=v1(g * R + (cw + 44 + r)), in1=work[:, r, 1:T],
                                                       op0=ALU.mult, op1=ALU.add).then_inc(conv_mid, 1)
                        dve.wait_ge(conv_mid, g * R + (r + 1))
                        nc.vector.scalar_tensor_tensor(out=work[:, r, 2:T], in0=psum[:, r, 0:T - 2],
                                                       scalar=v1(g * R + (cw + r)), in1=work[:, r, 2:T],
                                                       op0=ALU.mult, op1=ALU.add).then_inc(conv_done, 1)
                        if r % 2:
                            pair = r // 2
                            dve.wait_ge(conv_done, g * R + (r + 1))
                            dve.wait_ge(gated, g * 2 + (pair + 1))
                            wait(dve, hidden_low, g * 2 + (pair + 1 - 2))
                            nc.vector.tensor_tensor(rows[:, 2 + pair, :], rows[:, pair, :], work[:, r, :],
                                                    ALU.mult).then_inc(multiplied, 1)
                    split_and_read(dve, name, split_low, read, inputs=inputs)
            add_projection(f"down{layer}", two_parts(HH, HL, KF))

        def swiglu(layer):
            inputs = ffn_input(lambda i: col("ffn2_g", layer * KD + i))
            name = f"up{layer + 2}"
            with phase("gated", "multiplied", "taken", "hidden_high", "hidden_low") as \
                    (block, gated, multiplied, taken, hidden_high, hidden_low):
                st = Stream(name)

                @block.sync
                def _(sp):
                    load_stream(sp, name)

                @block.tensor
                def _(pe):
                    products(pe, name, two_parts(XH, XL), taken, inputs)

                @block.gpsimd
                def _(pool):
                    split_hidden(pool, st, multiplied, hidden_high, hidden_low)

                @block.scalar
                def _(act):
                    def read(g, r, done):
                        done()
                        if r % 2 == 0:
                            wait(act, multiplied, g * 2 + (r // 2 + 1 - 2))
                            nc.scalar.activation(rows[:, r // 2, :], psum[:, r, :], ACT.Silu).then_inc(gated, 1)
                        else:
                            nc.scalar.activation(work[:, r // 2, :], psum[:, r, :], ACT.Copy).then_inc(taken, 2)
                    split_and_read(act, name, split_high, read, inputs=inputs)

                @block.vector
                def _(dve):
                    def read(g, r, done):
                        if r % 2:
                            pair = r // 2
                            dve.wait_ge(gated, g * 2 + (pair + 1))
                            dve.wait_ge(taken, g * R + (r + 1))
                            wait(dve, hidden_low, g * 2 + (pair + 1 - 2))
                            nc.vector.tensor_tensor(rows[:, 2 + pair, :], rows[:, pair, :],
                                                    work[:, pair, :], ALU.mult).then_inc(multiplied, 1)
                    split_and_read(dve, name, split_low, read, inputs=inputs)
            add_projection(f"down{layer + 2}", two_parts(HH, HL, KF))

        with phase("loaded") as (block, loaded):
            @block.sync
            def _(sp):
                sp.wait_ge(loaded, 48)
                for r in range(R):
                    load_unit(sp, Stream(ORDER[0]), 0, r)

            @block.scalar
            def _(act):
                act.dma_start(resid[:, :, :], dram["x"]).then_inc(loaded, 16)
                act.dma_start(const[:, :], dram["const"]).then_inc(loaded, 16)
                act.dma_start(vec[:, :], dram["vec"]).then_inc(loaded, 16)

        def sgu():
            xn, uv, vt, mt, wc = 0, 8, 24, 32, 40
            xl = vt
            inputs = rms_norm(lambda i: resid[:, i, :], None, KD, lambda i: col("mix_g", i), parts=two_parts(xn, xl))
            wcv = span(wc, 4).rearrange("p (g t) -> p g t", g=NH)
            with phase("taken", "ws_loaded", "masked") as (block, taken, ws_loaded, masked):
                @block.sync
                def _(sp):
                    sp.dma_start(span(wc, 4), dram["sgu_ws"]).then_inc(ws_loaded, 16)
                    load_stream(sp, "sgu_in")

                @block.tensor
                def _(pe):
                    products(pe, "sgu_in", two_parts(xn, xl), taken, inputs)

                @block.vector
                def _(dve):
                    split_and_read(dve, "sgu_in", split_low, inputs=inputs)
                    dve.wait_ge(ws_loaded, 16)
                    nc.vector.tensor_tensor(wcv, wcv, con("le").unsqueeze(1).to_broadcast([P, NH, P]),
                                            ALU.mult).then_inc(masked, 1)

                @block.scalar
                def _(act):
                    def read(g, m, done):
                        done()
                        nc.scalar.activation(tile_of(arena, g * R + (m + uv)), psum[:, m, :], ACT.Gelu,
                                             bias=col("sgu_b", g * R + m)).then_inc(taken, 1)
                    split_and_read(act, "sgu_in", split_high, read, inputs=inputs)
            rms_norm(lambda i: arena[:, uv + 8 + i, :], lambda i: arena[:, uv + 8 + i, :], KD, lambda i: col("sgu_gv", i))
            vtv = span(vt, 8).rearrange("p (c f) -> p c f", c=NCH)
            mtv = span(mt, 8).rearrange("p (c f) -> p c f", c=NCH)
            to_tokens(lambda j: arena[:, uv + 8 + j, :], KD, vtv)
            with phase("mixed", "read") as (block, mixed, read):
                @block.tensor
                def _(pe):
                    for g in range(NH):
                        if g >= 8:
                            pe.wait_ge(read, g - 7)
                        nc.tensor.matmul(psum[:, g % 8, 0:256].rearrange("p (c f) -> p c f", c=NCH), wcv[:, g, :],
                                         vtv[:, :, g * HD:(g + 1) * HD], start=True, stop=True).then_inc(mixed, 1)

                @block.vector
                def _(dve):
                    for g in range(NH):
                        dve.wait_ge(mixed, g + 1)
                        nc.vector.tensor_scalar(mtv[:, :, g * HD:(g + 1) * HD],
                                                psum[:, g % 8, 0:256].rearrange("p (c f) -> p c f", c=NCH),
                                                col("sgu_bs", g), None, ALU.add).then_inc(read, 1)
            transposes(KD, lambda j, b: mtv[:, b, j * P:(j + 1) * P],
                       lambda eng, j, bank: nc.vector.tensor_tensor(arena[:, uv + j, :], bank, arena[:, uv + j, :], ALU.mult),
                       engines=("vector",))
            parts = two_parts(xn, uv)
            add_projection("sgu_out", parts, Inputs(KD, lambda i: arena[:, uv + i, :], parts))

        def rwkv():
            XN, XX, MX, RR, KK, VV, WW, AA = (8 * i for i in range(8))

            def whole_of(s):
                return span(s, 8)

            rms_norm(lambda i: resid[:, i, :], lambda i: arena[:, XN + i, :], KD, lambda i: col("mix_g", 8 + i),
                     squares_ready=True)
            lw1 = span(RR, 5)[:, 0:8 * 288].rearrange("p (k n) -> p k n", k=KD)
            w2 = span(XN, 2)
            a2 = span(XN + 2, 2)
            with phase("loaded", "shifted") as (block, loaded, shifted):
                @block.sync
                def _(sp):
                    sp.dma_start(span(RR, 5)[:, 0:8 * 288], dram["lora1"]).then_inc(loaded, 16)
                    sp.wait_ge(loaded, 16)

                @block.vector
                def _(dve):
                    a, b = arena[:, XN:XN + 8, :], arena[:, XX:XX + 8, :]
                    nc.vector.tensor_tensor(b[:, :, 1:T], a[:, :, 0:T - 1], a[:, :, 1:T], ALU.subtract).then_inc(shifted, 1)
                    nc.vector.tensor_scalar(b[:, :, 0:1], a[:, :, 0:1], -1.0, None, ALU.mult).then_inc(shifted, 1)
                    dve.wait_ge(shifted, 2)

            def mix(which, i, to):
                return nc.vector.scalar_tensor_tensor(out=tile_of(arena, i + to), in0=tile_of(arena, i + XX),
                                                      scalar=col("mu", i + which * KD), in1=tile_of(arena, i + XN),
                                                      op0=ALU.mult, op1=ALU.add)

            def part(pool, high, low, mixed, mixed_high, mixed_low):
                for i in range(KD):
                    f = arena[:, low + i, :]
                    pool.wait_ge(mixed, i + 1)
                    nc.gpsimd.tensor_copy(rounded(high)[:, i, :], f).then_inc(mixed_high, 1)
                    pool.wait_ge(mixed_high, i + 1)
                    nc.gpsimd.tensor_tensor(rounded(low)[:, i, :], f, rounded(high)[:, i, :].bitcast(F32),
                                            ALU.subtract).then_inc(mixed_low, 1)

            LOW_RANK = ((1, [(0, 64, 0, ACT.Tanh)]), (4, [(64, 64, 1, ACT.Copy)]),
                        (5, [(128, 128, 2, ACT.Sigmoid), (256, 32, 3, ACT.Sigmoid)]))
            with phase("mixed", "mix_used", "kept", "cleared", "first_mixed", "mixed_high", "mixed_low") as \
                    (block, mixed, mix_used, kept, cleared, first_mixed, mixed_high, mixed_low):
                @block.vector
                def _(dve):
                    for n, (which, _) in enumerate(LOW_RANK):
                        for i in range(KD):
                            if n:
                                dve.wait_ge(mix_used, (n - 1) * KD + i + 1)
                            mix(which, i, MX).then_inc(mixed, 1)
                            if n == 0:
                                mix(0, i, AA).then_inc(first_mixed, 1)

                @block.tensor
                def _(pe):
                    for n, (which, parts) in enumerate(LOW_RANK):
                        for k in range(KD):
                            pe.wait_ge(mixed, n * KD + k + 1)
                            for at, m, row, _ in parts:
                                mm = nc.tensor.matmul(psum[0:m, row, :], lw1[:, k, at:at + m], arena[:, MX + k, :],
                                                      start=(k == 0), stop=(k == KD - 1))
                            mm.then_inc(mix_used, 1)

                @block.scalar
                def _(act):
                    for n, (which, parts) in enumerate(LOW_RANK):
                        act.wait_ge(mix_used, (n + 1) * KD)
                        for at, m, row, func in parts:
                            nc.scalar.activation(rows[0:m, row, :], psum[0:m, row, :], func).then_inc(kept, 1)

                @block.gpsimd
                def _(pool):
                    nc.gpsimd.memset(rows[HD:P, 0:2, :], 0.0).then_inc(cleared, 1)
                    pool.wait_ge(cleared, 1)
                    part(pool, VV, AA, first_mixed, mixed_high, mixed_low)

            for name, dst, high, low, ahead in (("rwkv_r", RR, VV, AA, (2, WW, MX)), ("rwkv_k", KK, WW, MX, (3, XN, AA)),
                                                ("rwkv_v", VV, XN, AA, None)):
                with phase("mixed", "mixed_high", "mixed_low", "taken") as (block, mixed, mixed_high, mixed_low, taken):
                    @block.sync
                    def _(sp):
                        load_stream(sp, name)

                    @block.vector
                    def _(dve):
                        def mix_ahead(g, m, done):
                            which, _, to = ahead
                            mix(which, g * R + m, to).then_inc(mixed, 1)
                        split_and_read(dve, name, split_low, mix_ahead if ahead else None)

                    @block.tensor
                    def _(pe):
                        products(pe, name, two_parts(high, low), taken)

                    @block.scalar
                    def _(act):
                        def read(g, m, done):
                            done()
                            nc.scalar.activation(tile_of(arena, g * R + (m + dst)), psum[:, m, :], ACT.Copy).then_inc(taken, 1)
                        split_and_read(act, name, split_high, read)

                    @block.gpsimd
                    def _(pool):
                        if ahead:
                            _, high_next, low_next = ahead
                            part(pool, high_next, low_next, mixed, mixed_high, mixed_low)

            with phase("loaded_w", "loaded_a", "cleared", "summed", "kept") as (block, loaded_w, loaded_a, cleared, summed, kept):
                @block.vector
                def _(dve):
                    for w in (w2, a2):
                        nc.vector.memset(w[HD:P, :], 0.0).then_inc(cleared, 1)

                @block.sync
                def _(sp):
                    sp.dma_start(w2[0:HD, :], dram["lora_w2"]).then_inc(loaded_w, 16)
                    sp.dma_start(a2[0:HD, :], dram["lora_a2"]).then_inc(loaded_a, 16)

                jobs = [(w2, 0, WW, "w0", m) for m in range(KD)] + [(a2, 1, AA, "a0", m) for m in range(KD)]

                @block.tensor
                def _(pe):
                    for n, (w, row, dst, bias, m) in enumerate(jobs):
                        if m == 0:
                            pe.wait_ge(loaded_a if n else loaded_w, 16)
                            pe.wait_ge(cleared, 2 if n else 1)
                        if n >= 4:
                            pe.wait_ge(kept, n - 3)
                        nc.tensor.matmul(psum[:, n % 4, :], w[:, m * P:(m + 1) * P], rows[:, row, :],
                                         start=True, stop=True).then_inc(summed, 1)

                @block.scalar
                def _(act):
                    for n, (w, row, dst, bias, m) in enumerate(jobs):
                        act.wait_ge(summed, n + 1)
                        nc.scalar.activation(arena[:, dst + m, :], psum[:, n % 4, :], ACT.Sigmoid,
                                             bias=col(bias, m)).then_inc(kept, 1)

            with phase("scaled") as (block, scaled):
                @block.vector
                def _(dve):
                    for i in range(KD):
                        nc.vector.tensor_scalar(arena[:, XN + i, :], arena[:, KK + i, :], col("k_k", i), None,
                                                ALU.mult).then_inc(scaled, 1)
            norm(lambda i: arena[:, XN + i, :], lambda i: arena[:, XN + i, :], KD, head_sums, head_spread,
                 lambda i: 1.0, 1.0, 1e-24, ALU.max)

            mid = small[:, 0:32].rearrange("p (i c) -> p i c", c=NCH)
            end = small[:, 32:64].rearrange("p (i c) -> p i c", c=NCH)
            scl = small[:, 64:96].rearrange("p (i c) -> p i c", c=NCH)
            bonus = small[:, 128:192].rearrange("p (c h) -> p c h", c=NCH)
            chunks = "p (j t) -> p j t"

            with phase("tmp_done", "k_done", "rk_done", "bonus_scaled", "summed", "scanned", "mid_done", "centred", "less") as \
                    (block, tmp_done, k_done, rk_done, bonus_scaled, summed, scanned, mid_done, centred, less):
                @block.vector
                def _(dve):
                    for i in range(KD):
                        if i >= 4:
                            dve.wait_ge(k_done, i - 3)
                        nc.vector.tensor_scalar(work[:, i % 4, :], arena[:, AA + i, :], -1.0, col("k_a", i),
                                                ALU.add, ALU.mult).then_inc(tmp_done, 1)
                        for c in range(NCH):
                            s = slice(c * CH, (c + 1) * CH)
                            nc.vector.tensor_tensor_scan(arena[:, XX + i, s], con("ones"), arena[:, WW + i, s], 0.0,
                                                         ALU.mult, ALU.add).then_inc(scanned, 1)
                        dve.wait_ge(tmp_done, i + 1)
                        nc.vector.scalar_tensor_tensor(out=arena[:, KK + i, :], in0=work[:, i % 4, :], scalar=1.0,
                                                       in1=arena[:, KK + i, :], op0=ALU.add, op1=ALU.mult).then_inc(k_done, 1)
                    dve.wait_ge(scanned, KD * NCH)
                    sums = whole_of(XX).rearrange(chunks, t=CH)
                    nc.vector.tensor_copy(mid, sums[:, :, 63:64].rearrange("p (i c) o -> p i (c o)", c=NCH)).then_inc(mid_done, 1)
                    dve.wait_ge(mid_done, 1)
                    nc.vector.tensor_tensor(sums, sums, small[:, 0:32].unsqueeze(2).to_broadcast([P, 32, CH]),
                                            ALU.subtract).then_inc(centred, 1)
                    dve.wait_ge(centred, 1)
                    nc.vector.tensor_tensor(whole_of(WW), whole_of(XX), whole_of(WW), ALU.subtract).then_inc(less, 1)
                    dve.wait_ge(summed, 1)
                    nc.vector.tensor_copy(small[:, 128:192], psum[:, 0, 0:64]).then_inc(less, 1)

                @block.gpsimd
                def _(pool):
                    for i in range(KD):
                        m = arena[:, MX + i, :]
                        pool.wait_ge(k_done, i + 1)
                        nc.gpsimd.tensor_tensor(m, arena[:, RR + i, :], arena[:, KK + i, :], ALU.mult).then_inc(rk_done, 1)

                @block.scalar
                def _(act):
                    for i in range(KD):
                        act.wait_ge(rk_done, i + 1)
                        nc.scalar.activation(arena[:, MX + i, :], arena[:, MX + i, :], ACT.Copy, scale=col("r_k", i)).then_inc(bonus_scaled, 1)

                @block.tensor
                def _(pe):
                    pe.wait_ge(bonus_scaled, KD)
                    for c in range(NCH):
                        for i in range(KD):
                            mm = nc.tensor.matmul(psum[:, 0, c * NH + 2 * i:c * NH + 2 * i + 2],
                                                  arena[:, MX + i, c * CH:(c + 1) * CH], con("halves", 2),
                                                  start=True, stop=True)
                    mm.then_inc(summed, 1)

            with phase("b_done", "e1", "e2", "e3", "mids", "hats", "ends", "bonus_kept") as \
                    (block, b_done, e1, e2, e3, mids, hats, ends, bonus_kept):
                @block.scalar
                def _(act):
                    nc.scalar.activation(whole_of(MX), whole_of(XX), ACT.Exp, scale=-EXP_HALF).then_inc(e1, 1)
                    act.wait_ge(e1, 1)
                    nc.scalar.activation(whole_of(XX), whole_of(XX), ACT.Exp, scale=EXP_HALF).then_inc(e2, 1)
                    nc.scalar.activation(whole_of(WW), whole_of(WW), ACT.Exp, scale=-EXP_HALF).then_inc(e3, 1)
                    nc.scalar.activation(small[:, 96:128], small[:, 0:32], ACT.Exp, scale=-EXP_HALF).then_inc(mids, 1)

                @block.gpsimd
                def _(pool):
                    nc.gpsimd.tensor_tensor(whole_of(AA), whole_of(XN), whole_of(AA), ALU.mult).then_inc(b_done, 1)

                @block.vector
                def _(dve):
                    dve.wait_ge(e1, 1)
                    nc.vector.tensor_tensor(whole_of(RR), whole_of(RR), whole_of(MX), ALU.mult).then_inc(hats, 1)
                    nc.vector.tensor_copy(end, whole_of(MX).rearrange(chunks, t=CH)[:, :, 127:128]
                                          .rearrange("p (i c) o -> p i (c o)", c=NCH)).then_inc(ends, 1)
                    dve.wait_ge(e2, 1)
                    nc.vector.tensor_tensor(whole_of(KK), whole_of(KK), whole_of(XX), ALU.mult).then_inc(hats, 1)
                    dve.wait_ge(e3, 1)
                    nc.vector.scalar_tensor_tensor(out=whole_of(WW), in0=whole_of(WW), scalar=-1.0, in1=whole_of(XN),
                                                   op0=ALU.mult, op1=ALU.mult).then_inc(hats, 1)
                    dve.wait_ge(b_done, 1)
                    nc.vector.tensor_tensor(whole_of(AA), whole_of(AA), whole_of(XX), ALU.mult).then_inc(hats, 1)
                    dve.wait_ge(mids, 1)
                    dve.wait_ge(ends, 1)
                    nc.vector.tensor_tensor(scl[:, :, 0:3], end[:, :, 0:3],
                                            small[:, 96:128].rearrange("p (i c) -> p i c", c=NCH)[:, :, 1:4],
                                            ALU.mult).then_inc(ends, 1)

            vt = whole_of(MX).rearrange("p (c f) -> p c f", c=NCH)
            to_tokens(lambda j: arena[:, VV + j, :], KD, vt)
            yt = whole_of(VV).rearrange("p (c f) -> p c f", c=NCH)
            bufs = []
            for s in (XN, XX):
                w = whole_of(s)
                bufs.append(dict(
                    m=w[:, 0:2048].rearrange("p (k h t) -> p k h t", k=4, h=4),
                    x=w[:, 2048:3072].rearrange("p (k h t) -> p k h t", k=2, h=4),
                    xf=w[:, 2048:3072], lb=w[:, 3072:3584].rearrange("p (h t) -> p h t", h=4),
                    t1=w[:, 3584:4096].rearrange("p (h t) -> p h t", h=4), t1f=w[:, 3584:4096]))
            wf = flat(work[:, :, :])
            bk, z, sa = wf[:, 0:512], wf[:, 512:768], wf[:, 768:1024]
            padded = flat(spare[:, 0:2, :]).rearrange("p (w i e t) -> p w i e t", w=2, i=2, e=2)
            state = flat(spare[:, 2:4, :]).rearrange("p (i f) -> p i f", i=KD)
            AB, RB, AK, RK = range(4)
            KINDS = (AB, 4, RB, AK, RK)
            LEVELS, UNITS, LAST = 6, 4 * NCH, 4 * (NCH - 1)

            def per_head(ap):
                return ap.unsqueeze(1).to_broadcast([P, 4, P])

            def place(u):
                return u // 4, slice(u // 4 * CH, (u // 4 + 1) * CH), 2 * (u % 4)

            with phase("cleared", "padded_done", "scored", "masked", "first_inv", "ones_added", "lb_ready", "t1_done", "t1_kept",
                       "p_done", "pt_done", "x_added", "xt_added", "bk_turned", "bk_kept", "z_done", "z_kept", "sa_done",
                       "sa_kept", "y_done", "y_kept", "s_done", "s_added", "s_kept") as \
                    (block, cleared, padded_done, scored, masked, first_inv, ones_added, lb_ready, t1_done, t1_kept,
                     p_done, pt_done, x_added, xt_added, bk_turned, bk_kept, z_done, z_kept, sa_done,
                     sa_kept, y_done, y_kept, s_done, s_added, s_kept):
                @block.tensor
                def _(pe):
                    def score(u, n):
                        c, cs, i0 = place(u)
                        kind, job = KINDS[n], 5 * u + n
                        if n == 0:
                            pe.wait_ge(padded_done, 4 * (u + 1))
                        if job >= 2:
                            pe.wait_ge(masked, job - 1)
                        for j in range(4):
                            mine = padded[:, 1 if kind in (AK, RK) else 0, j // 2, j % 2, :]
                            other = arena[:, (RR if kind in (RB, RK) else WW) + i0 + j // 2, cs]
                            lhs, rhs = (other, mine) if kind == 4 else (mine, other)
                            mm = nc.tensor.matmul(psum[:, 3 + job % 2, j * P:(j + 1) * P], lhs, rhs, start=True, stop=True)
                        mm.then_inc(scored, 1)

                    def corrections_in(u):
                        c, cs, i0 = place(u)
                        if 0 < u <= LAST:
                            pe.wait_ge(s_kept, 2 * u)
                        if c < NCH - 1:
                            for w, slot in enumerate((AA, KK)):
                                for i in range(2):
                                    tr = nc.tensor.transpose(psum[:, 5, (2 * w + i) * P:(2 * w + i + 1) * P],
                                                             arena[:, slot + i0 + i, cs], con("ident"))
                            tr.then_inc(bk_turned, 1)
                        pe.wait_ge(masked, 5 * u + 5)
                        if c:
                            pe.wait_ge(s_kept, 2 * (u - 3))
                        for j in range(4):
                            if c and j % 2 == 0:
                                nc.tensor.matmul(psum[:, 6, j * HD:(j + 2) * HD], arena[:, WW + i0 + j // 2, cs],
                                                 state[:, i0 + j // 2, :], start=True, stop=False)
                            mm = nc.tensor.matmul(psum[:, 6, j * HD:(j + 1) * HD], bufs[u % 2]["m"][:, AK, j, :],
                                                  values(u, j), start=(c == 0), stop=(c == 0 or j % 2 == 1))
                        mm.then_inc(z_done, 1)

                    def values(u, j, n=1):
                        f = (4 * (u % 4) + j) * HD
                        return vt[:, u // 4, f:f + n * HD]

                    def corrections(u):
                        pe.wait_ge(z_kept, u + 1)
                        pe.wait_ge(xt_added, LEVELS * (u + 1))
                        for j in range(4):
                            mm = nc.tensor.matmul(psum[:, 6, 4 * HD + j * HD:4 * HD + (j + 1) * HD],
                                                  bufs[u % 2]["x"][:, 1, j, :], z[:, j * HD:(j + 1) * HD], start=True, stop=True)
                        mm.then_inc(sa_done, 1)

                    def output(u):
                        c, cs, i0 = place(u)
                        pe.wait_ge(sa_kept, u + 1)
                        if u:
                            pe.wait_ge(y_kept, u)
                        for j in range(4):
                            if c and j % 2 == 0:
                                nc.tensor.matmul(psum[:, 7, j * HD:(j + 2) * HD], arena[:, RR + i0 + j // 2, cs],
                                                 state[:, i0 + j // 2, :], start=True, stop=False)
                            o = psum[:, 7, j * HD:(j + 1) * HD]
                            nc.tensor.matmul(o, bufs[u % 2]["m"][:, RB, j, :], sa[:, j * HD:(j + 1) * HD], start=(c == 0), stop=False)
                            mm = nc.tensor.matmul(o, bufs[u % 2]["m"][:, RK, j, :], values(u, j), start=False,
                                                  stop=(c == 0 or j % 2 == 1))
                        mm.then_inc(y_done, 1)

                    def change(u):
                        if u >= LAST:
                            return
                        pe.wait_ge(bk_kept, u + 1)
                        for i in range(2):
                            o = psum[:, 5, i * P:(i + 1) * P]
                            nc.tensor.matmul(o, bk[:, i * P:(i + 1) * P], sa[:, i * P:(i + 1) * P], start=True, stop=False)
                            mm = nc.tensor.matmul(o, bk[:, (2 + i) * P:(3 + i) * P], values(u, 2 * i, 2), start=False, stop=True)
                        mm.then_inc(s_done, 1)

                    def fill(u, l, late):
                        if u and l < 3:
                            step = {(0, 0): corrections_in, (1, 0): corrections, (2, 0): output, (2, 1): change}.get((l, late))
                            if step:
                                step(u - 1)
                        if u + 1 < UNITS and 3 <= l and not (l == 5 and late):
                            score(u + 1, 2 * (l - 3) + late)
                    for n in range(5):
                        score(0, n)
                    for u in range(UNITS):
                        x = bufs[u % 2]["x"]
                        for l in range(LEVELS):
                            pe.wait_ge(lb_ready, LEVELS * u + l + 1)
                            if l == 0:
                                pe.wait_ge(ones_added, u + 1)
                            else:
                                pe.wait_ge(x_added, 5 * u + l)
                            for j in range(4):
                                mm = nc.tensor.matmul(psum[:, 0, j * P:(j + 1) * P], bufs[u % 2]["lb"][:, j, :],
                                                      x[:, 0, j, :], start=True, stop=True)
                            mm.then_inc(t1_done, 1)
                            fill(u, l, 0)
                            pe.wait_ge(t1_kept, LEVELS * u + l + 1)
                            if u or l:
                                pe.wait_ge(xt_added, LEVELS * u + l)
                            for which in ((1, 2) if l < 5 else (2,)):
                                for j in range(4):
                                    t1, xt = bufs[u % 2]["t1"][:, j, :], x[:, 1, j, :]
                                    lhs, rhs = (xt, t1) if which == 1 else (t1, xt)
                                    mm = nc.tensor.matmul(psum[:, which, j * P:(j + 1) * P], lhs, rhs, start=True, stop=True)
                                mm.then_inc(p_done if which == 1 else pt_done, 1)
                            fill(u, l, 1)
                    for step in (corrections_in, corrections, output):
                        step(UNITS - 1)

                @block.scalar
                def _(act):
                    def pad(u, e):
                        c, cs, i0 = place(u)
                        if u:
                            act.wait_ge(scored, 5 * u)
                        ps = slice(e * HD, (e + 1) * HD)
                        for w, slot in enumerate((AA, KK)):
                            nc.scalar.activation(padded[ps, w, :, e, :], arena[ps, slot + i0:slot + i0 + 2, cs],
                                                 ACT.Copy).then_inc(padded_done, 1)
                    act.wait_ge(cleared, 1)
                    pad(0, 0)
                    pad(0, 1)
                    for u in range(UNITS):
                        for l in range(LEVELS):
                            act.wait_ge(t1_done, LEVELS * u + l + 1)
                            nc.scalar.activation(bufs[u % 2]["t1f"], psum[:, 0, :], ACT.Copy).then_inc(t1_kept, 1)
                            if l == 0 and 0 < u <= LAST:
                                act.wait_ge(bk_turned, u)
                                nc.scalar.activation(bk, psum[:, 5, :], ACT.Copy).then_inc(bk_kept, 1)
                            if l in (1, 2) and u + 1 < UNITS:
                                pad(u + 1, l - 1)

                @block.vector
                def _(dve):
                    def mask(u, n):
                        kind, job = KINDS[n], 5 * u + n
                        if n == 0 and u >= 2:
                            dve.wait_ge(y_done, u - 1)
                        dve.wait_ge(scored, job + 1)
                        by = con("pair_low") if kind == 4 else con("lt") if kind in (AB, AK) else con("le")
                        to = bufs[u % 2]["x"][:, 0] if kind == 4 else bufs[u % 2]["m"][:, kind]
                        nc.vector.tensor_tensor(to, psum[:, 3 + job % 2, :].rearrange("p (h t) -> p h t", h=4), per_head(by),
                                                ALU.mult).then_inc(masked, 1)

                    def keep_z(u):
                        dve.wait_ge(z_done, u + 1)
                        nc.vector.tensor_copy(z, psum[:, 6, 0:4 * HD]).then_inc(z_kept, 1)

                    def keep_sa(u):
                        dve.wait_ge(sa_done, u + 1)
                        nc.vector.tensor_copy(sa, psum[:, 6, 4 * HD:8 * HD]).then_inc(sa_kept, 1)

                    def keep_y(u):
                        dve.wait_ge(y_done, u + 1)
                        q = u % 4
                        nc.vector.tensor_copy(yt[:, u // 4, q * 4 * HD:(q + 1) * 4 * HD], psum[:, 7, 0:4 * HD]).then_inc(y_kept, 1)

                    def keep_state(u):
                        if u >= LAST:
                            return
                        c, cs, i0 = place(u)
                        dve.wait_ge(s_done, u + 1)
                        dve.wait_ge(y_done, u + 1)
                        for e in range(2):
                            ps, f = slice(e * HD, (e + 1) * HD), slice(e * HD, (e + 1) * HD)
                            s0 = state[ps, i0:i0 + 2, f]
                            new = psum[ps, 5, 0:2 * P].rearrange("p (i f) -> p i f", i=2)[:, :, f]
                            sc = scl[ps, i0:i0 + 2, c:c + 1].to_broadcast([HD, 2, HD])
                            if c:
                                nc.vector.tensor_tensor(s0, new, s0, ALU.add).then_inc(s_added, 1)
                                dve.wait_ge(s_added, 2 * (u - 4) + e + 1)
                                nc.vector.tensor_tensor(s0, s0, sc, ALU.mult).then_inc(s_kept, 1)
                            else:
                                nc.vector.tensor_tensor(s0, new, sc, ALU.mult).then_inc(s_kept, 1)

                    def fill(u, l, late):
                        if u and l < 3:
                            step = {(0, 0): keep_z, (1, 0): keep_sa, (2, 0): keep_y, (2, 1): keep_state}.get((l, late))
                            if step:
                                step(u - 1)
                        if u + 1 < UNITS and 3 <= l and not (l == 5 and late):
                            mask(u + 1, 2 * (l - 3) + late)
                    for n in range(5):
                        mask(0, n)
                    for u in range(UNITS):
                        x = bufs[u % 2]["xf"]
                        for l in range(LEVELS):
                            fill(u, l, 0)
                            if l < 5:
                                dve.wait_ge(p_done, 5 * u + l + 1)
                                nc.vector.tensor_tensor(x[:, 0:T], psum[:, 1, :], x[:, 0:T], ALU.add).then_inc(x_added, 1)
                            dve.wait_ge(pt_done, LEVELS * u + l + 1)
                            nc.vector.tensor_tensor(x[:, T:2 * T], psum[:, 2, :], x[:, T:2 * T], ALU.add).then_inc(xt_added, 1)
                            fill(u, l, 1)
                    for step in (keep_z, keep_sa, keep_y):
                        step(UNITS - 1)

                @block.gpsimd
                def _(pool):
                    def first_blocks(u):
                        b = bufs[u % 2]
                        pool.wait_ge(masked, 5 * u + 1)
                        nc.gpsimd.tensor_tensor(b["x"][:, 1], b["m"][:, AB], per_head(con("levels")), ALU.mult).then_inc(first_inv, 1)
                        pool.wait_ge(first_inv, u + 1)
                        pool.wait_ge(masked, 5 * u + 2)
                        x8 = b["xf"].rearrange("p (h t) -> p h t", h=8)
                        nc.gpsimd.tensor_tensor(x8, x8, con("ident").unsqueeze(1).to_broadcast([P, 8, P]),
                                                ALU.add).then_inc(ones_added, 1)
                    nc.gpsimd.memset(flat(spare[:, :, :]), 0.0).then_inc(cleared, 1)
                    first_blocks(0)
                    for u in range(UNITS):
                        b = bufs[u % 2]
                        for l in range(LEVELS):
                            if l:
                                pool.wait_ge(t1_done, LEVELS * u + l)
                            nc.gpsimd.tensor_tensor(b["lb"], b["m"][:, AB], per_head(con("levels", P, (l + 1) * P)),
                                                    ALU.mult).then_inc(lb_ready, 1)
                        if u + 1 < UNITS:
                            first_blocks(u + 1)

            yw = whole_of(VV).rearrange("p (j f) -> p j f", f=HD)
            sq = whole_of(XN).rearrange("p (j f) -> p j f", f=HD)
            g2 = span(XX, 4)
            with phase("g2_loaded", "mean_sum", "mean_done", "less_mean", "squared", "var_sum", "var_done", "rooted",
                       "inverted", "done") as \
                    (block, g2_loaded, mean_sum, mean_done, less_mean, squared, var_sum, var_done, rooted, inverted, done):
                m1, m2, m3 = small[:, 0:64], small[:, 64:128], roots[:, :]

                @block.sync
                def _(sp):
                    sp.dma_start(g2[:, 0:D], dram["lora_g2"][0:P, :]).then_inc(g2_loaded, 16)
                    sp.dma_start(g2[0:32, D:2 * D], dram["lora_g2"][P:160, :]).then_inc(g2_loaded, 16)
                    sp.wait_ge(g2_loaded, 32)

                @block.vector
                def _(dve):
                    nc.vector.reduce_sum(m1, yw, axis=AX).then_inc(mean_sum, 1)
                    dve.wait_ge(mean_sum, 1)
                    nc.vector.tensor_scalar(m2, m1, 1.0 / HD, None, ALU.mult).then_inc(mean_done, 1)
                    dve.wait_ge(mean_done, 1)
                    nc.vector.tensor_tensor(yw, yw, m2.unsqueeze(2).to_broadcast([P, 64, HD]), ALU.subtract).then_inc(less_mean, 1)
                    dve.wait_ge(squared, 1)
                    nc.vector.reduce_sum(m1, sq, axis=AX).then_inc(var_sum, 1)
                    dve.wait_ge(var_sum, 1)
                    nc.vector.tensor_scalar(m2, m1, 1.0 / HD, 64e-5, ALU.mult, ALU.add).then_inc(var_done, 1)
                    dve.wait_ge(rooted, 1)
                    nc.vector.reciprocal(m1, m3).then_inc(inverted, 1)
                    dve.wait_ge(inverted, 1)
                    nc.vector.tensor_tensor(yw, yw, m1.unsqueeze(2).to_broadcast([P, 64, HD]), ALU.mult).then_inc(done, 1)

                @block.gpsimd
                def _(pool):
                    vw = whole_of(MX).rearrange("p (j f) -> p j f", f=HD)
                    nc.gpsimd.tensor_tensor(vw, vw, small[:, 128:192].unsqueeze(2).to_broadcast([P, 64, HD]), ALU.mult).then_inc(done, 1)

                @block.scalar
                def _(act):
                    act.wait_ge(less_mean, 1)
                    nc.scalar.activation(whole_of(XN), whole_of(VV), ACT.Square).then_inc(squared, 1)
                    act.wait_ge(var_done, 1)
                    nc.scalar.activation(m3, m2, ACT.Sqrt).then_inc(rooted, 1)

            def take(eng, j, bank):
                i = j // 2
                if j % 2 == 0:
                    return nc.scalar.activation(arena[:, RR + i, :], bank, ACT.Identity, bias=col("ln_b", i), scale=col("ln_w", i))
                return nc.vector.tensor_copy(arena[:, KK + i, :], bank)
            transposes(2 * KD, lambda j, b: (yt, vt)[j % 2][:, b, (j // 2) * P:(j // 2 + 1) * P], take)
            with phase("summed", "gated", "added") as (block, summed, gated, added):
                @block.tensor
                def _(pe):
                    for m in range(KD):
                        if m >= 4:
                            pe.wait_ge(gated, m - 3)
                        nc.tensor.matmul(psum[:, m % 4, :], g2[:, m * P:(m + 1) * P], rows[:, 2, :], start=True, stop=False)
                        nc.tensor.matmul(psum[:, m % 4, :], g2[0:32, D + m * P:D + (m + 1) * P], rows[0:32, 3, :],
                                         start=False, stop=True).then_inc(summed, 1)

                @block.vector
                def _(dve):
                    for m in range(KD):
                        y = arena[:, RR + m, :]
                        nc.vector.tensor_tensor(y, y, arena[:, KK + m, :], ALU.add).then_inc(added, 1)
                        dve.wait_ge(added, m + 1)
                        dve.wait_ge(summed, m + 1)
                        nc.vector.tensor_tensor(y, psum[:, m % 4, :], y, ALU.mult).then_inc(gated, 1)
            parts = two_parts(WW, RR)
            add_projection("rwkv_o", parts, Inputs(KD, lambda i: arena[:, RR + i, :], parts))

        def attention(units, sb, pr, pt, bias, before):
            n = len(units)
            scale = HD ** -0.5
            mx, nm, sm, rc = (small[:, 8 * a:8 * a + 8] for a in range(4))
            with phase("scored", "biased", "maxed", "negated", "expd", "turned", "pt_kept", "pv_done", "inverted",
                       "out_done", "bias_ready", "bias_loaded") as \
                    (block, scored, biased, maxed, negated, expd, turned, pt_kept, pv_done, inverted, out_done,
                     bias_ready, bias_loaded):
                if bias:
                    before(block, bias_ready, bias_loaded, biased)

                @block.tensor
                def _(pe):
                    for i in range(n + 3):
                        if i < n:
                            if i >= 4:
                                pe.wait_ge(biased if bias else expd, i - 3)
                            nc.tensor.matmul(psum[:, i % 4, :], units[i][0], units[i][1], start=True, stop=True).then_inc(scored, 1)
                        if 2 <= i < n + 2:
                            u = i - 2
                            pe.wait_ge(expd, u + 1)
                            if u >= 2:
                                pe.wait_ge(pt_kept, u - 1)
                            for b in range(4):
                                tr = nc.tensor.transpose(psum[:, 4 + u % 2, b * P:(b + 1) * P],
                                                         pr[u % 3][:, b * P:(b + 1) * P], con("ident"))
                            tr.then_inc(turned, 1)
                        if i >= 3:
                            u = i - 3
                            pe.wait_ge(pt_kept, u + 1)
                            if u >= 2:
                                pe.wait_ge(out_done, u - 1)
                            for b in range(4):
                                mm = nc.tensor.matmul(psum[:, 6 + u % 2, 0:HD], pt[u % 2][:, b * P:(b + 1) * P],
                                                      units[u][2](b), start=(b == 0), stop=(b == 3))
                            mm.then_inc(pv_done, 1)

                @block.scalar
                def _(act):
                    for i in range(n + 1):
                        if i < n:
                            act.wait_ge(negated, i + 1)
                            if i >= 3:
                                act.wait_ge(turned, i - 2)
                            if i >= 8:
                                act.wait_ge(inverted, i - 7)
                            src = sb[i % 2] if bias else psum[:, i % 4, :]
                            nc.scalar.activation(pr[i % 3], src, ACT.Exp, bias=nm[:, i % 8:i % 8 + 1],
                                                 scale=1.0 if bias else scale,
                                                 accum_out=sm[:, i % 8:i % 8 + 1]).then_inc(expd, 1)
                        if i >= 1:
                            u = i - 1
                            act.wait_ge(turned, u + 1)
                            if u >= 2:
                                act.wait_ge(pv_done, u - 1)
                            nc.scalar.activation(pt[u % 2], psum[:, 4 + u % 2, :], ACT.Copy).then_inc(pt_kept, 1)

                @block.vector
                def _(dve):
                    def maximum(i):
                        dve.wait_ge(scored, i + 1)
                        if i >= 8:
                            dve.wait_ge(negated, i - 7)
                        c8 = i % 8
                        if bias:
                            dve.wait_ge(bias_ready, i // 4 + 1)
                            if i >= 2:
                                dve.wait_ge(expd, i - 1)
                            nc.vector.scalar_tensor_tensor(out=sb[i % 2], in0=psum[:, i % 4, :], scalar=scale,
                                                           in1=bias(i), op0=ALU.mult, op1=ALU.add).then_inc(biased, 1)
                            dve.wait_ge(biased, i + 1)
                            nc.vector.reduce_max(mx[:, c8:c8 + 1], sb[i % 2], axis=AX).then_inc(maxed, 1)
                        else:
                            nc.vector.reduce_max(mx[:, c8:c8 + 1], psum[:, i % 4, :], axis=AX).then_inc(maxed, 1)
                        dve.wait_ge(maxed, i + 1)
                        if i >= 8:
                            dve.wait_ge(expd, i - 7)
                        nc.vector.tensor_scalar(nm[:, c8:c8 + 1], mx[:, c8:c8 + 1], -1.0 if bias else -scale, None,
                                                ALU.mult).then_inc(negated, 1)

                    for i in range(n + 4):
                        if i < n:
                            maximum(i)
                        if i >= 4:
                            u = i - 4
                            dve.wait_ge(expd, u + 1)
                            if u >= 8:
                                dve.wait_ge(out_done, u - 7)
                            nc.vector.reciprocal(rc[:, u % 8:u % 8 + 1], sm[:, u % 8:u % 8 + 1]).then_inc(inverted, 1)
                            dve.wait_ge(inverted, u + 1)
                            dve.wait_ge(pv_done, u + 1)
                            nc.vector.tensor_scalar(units[u][3], psum[:, 6 + u % 2, 0:HD], rc[:, u % 8:u % 8 + 1], None,
                                                    ALU.mult).then_inc(out_done, 1)

        def key_halves(keys, first):
            with phase("zeroed", "copied") as (block, zeroed, copied):
                @block.gpsimd
                def _(pool):
                    for n, (e, t) in enumerate(keys):
                        nc.gpsimd.memset(arena[(1 - e) * HD:(2 - e) * HD, first + n, :], 0.0).then_inc(zeroed, 1)

                @block.vector
                def _(dve):
                    for n, (e, t) in enumerate(keys):
                        ps = slice(e * HD, (e + 1) * HD)
                        nc.vector.tensor_copy(arena[ps, first + n, :], arena[ps, t, :]).then_inc(copied, 1)

        def even_in():
            XN, Q, Z, XS = 0, 8, 20, 28
            name = "even_in"
            n0 = first_unit[name]
            XNL = 44
            inputs = rms_norm(lambda i: resid[:, i, :], None, KD, lambda i: col("even_g", i), parts=two_parts(XN, XNL))
            wdt = span(52, 1)[:, 0:8 * 32].rearrange("p (k n) -> p k n", k=KD)
            cw, cb = VECTOR_AT["ssd_cw"], VECTOR_AT["ssd_cb"]

            def v1(a):
                return vec[:, a:a + 1] if isinstance(a, int) else vec[:, bass.ds(a, 1)]

            with phase("taken", "biased", "tap0", "tap1", "tap3", "wdt_loaded", "dt_done", "dt_kept") as \
                    (block, taken, biased, tap0, tap1, tap3, wdt_loaded, dt_done, dt_kept):
                @block.sync
                def _(sp):
                    sp.dma_start(span(52, 1)[:, 0:8 * 32], dram["even_dt"]).then_inc(wdt_loaded, 16)
                    load_stream(sp, name)

                @block.tensor
                def _(pe):
                    products(pe, name, two_parts(XN, XNL), taken, inputs)
                    pe.wait_ge(wdt_loaded, 16)
                    for c in range(NCH):
                        for k in range(2 * KD):
                            x = two_parts(XN, XNL)(k % KD)[k // KD]
                            mm = nc.tensor.matmul(psum[:, 4, c * 32:(c + 1) * 32], x[:, c * CH:(c + 1) * CH].bitcast(F32),
                                                  wdt[:, k % KD, :], start=(k == 0), stop=(k == 2 * KD - 1))
                    mm.then_inc(dt_done, 1)

                @block.scalar
                def _(act):
                    def read_copy(g, r, done):
                        done()
                        nc.scalar.activation(tile_of(arena, g * R + (r + Q)), psum[:, r, :], ACT.Copy).then_inc(taken, 1)

                    def read_silu(g, r, done):
                        done()
                        nc.scalar.activation(tile_of(arena, g * R + (r + Q)), psum[:, r, :], ACT.Silu).then_inc(taken, 1)

                    def read_conv(g, r, done):
                        done()
                        nc.scalar.activation(tile_of(arena, g * R + (r + Q)), psum[:, r, :], ACT.Identity,
                                             bias=v1(g * R + (r + cb - 20)), scale=v1(g * R + (r + cw + 32 - 20))).then_inc(biased, 1)
                    split_and_read(act, name, split_high, groups=[(read_copy, 0, 3), (read_silu, 3, 5), (read_conv, 5, 9)], inputs=inputs)

                @block.vector
                def _(dve):
                    def read_conv(g, r, done):
                        o = tile_of(arena, g * R + (r + Q))

                        def tap(j, dst, src, sem):
                            return nc.vector.scalar_tensor_tensor(
                                out=o[:, dst], in0=psum[:, r, src], scalar=v1(g * R + (r + cw + 16 * j - 20)), in1=o[:, dst],
                                op0=ALU.mult, op1=ALU.add).then_inc(sem, 1)
                        dve.wait_ge(biased, g * R + (r + 1 - 20))
                        tap(0, slice(2, T), slice(0, T - 2), tap0)
                        dve.wait_ge(tap0, g * R + (r + 1 - 20))
                        tap(1, slice(1, T), slice(0, T - 1), tap1)
                        dve.wait_ge(tap1, g * R + (r + 1 - 20))
                        tap(3, slice(0, T - 1), slice(1, T), taken)
                    split_and_read(dve, name, split_low, groups=[(None, 0, 5), (read_conv, 5, 9)], inputs=inputs)
                    dve.wait_ge(dt_done, 1)
                    nc.vector.tensor_tensor(rows[:, 3, 0:128].rearrange("p (c h) -> p c h", c=NCH),
                                            psum[:, 4, 0:128].rearrange("p (c h) -> p c h", c=NCH),
                                            col("dt_bias", 0, 32).unsqueeze(1).to_broadcast([P, NCH, 32]),
                                            ALU.add).then_inc(dt_kept, 1)
            U, DT, AC, TM = (rows[:, 3, 128 * a:128 * (a + 1)] for a in range(4))
            with phase("silu_done", "abs_done", "exp_done", "ln_done", "dt_ready", "rate_ready", "decay_ready") as \
                    (block, silu_done, abs_done, exp_done, ln_done, dt_ready, ea_done, a_ready):
                @block.scalar
                def _(act):
                    nc.scalar.activation(TM, U, ACT.Abs).then_inc(abs_done, 1)
                    act.wait_ge(abs_done, 1)
                    nc.scalar.activation(DT, TM, ACT.Exp, scale=-1.0).then_inc(exp_done, 1)
                    act.wait_ge(exp_done, 1)
                    nc.scalar.activation(TM, DT, ACT.Ln, bias=con("ones", 1)).then_inc(ln_done, 1)
                    nc.scalar.activation(small[:, 0:32], col("A_log", 0, 32), ACT.Exp).then_inc(ea_done, 1)
                    x = span(XS, 16)
                    nc.scalar.activation(x, x, ACT.Silu).then_inc(silu_done, 1)

                @block.vector
                def _(dve):
                    dve.wait_ge(ln_done, 1)
                    nc.vector.scalar_tensor_tensor(out=DT, in0=U, scalar=0.0, in1=TM, op0=ALU.max, op1=ALU.add).then_inc(dt_ready, 1)
                    dve.wait_ge(dt_ready, 1)
                    dve.wait_ge(ea_done, 1)
                    v = "p (c h) -> p c h"
                    nc.vector.scalar_tensor_tensor(out=U.rearrange(v, c=NCH), in0=DT.rearrange(v, c=NCH), scalar=-1.0,
                                                   in1=small[:, 0:32].unsqueeze(1).to_broadcast([P, NCH, 32]),
                                                   op0=ALU.mult, op1=ALU.mult).then_inc(a_ready, 1)
            INTO, OVER, OUTOF = rows[:, 1, 0:128], U, TM
            TWICE = rows[:, 1, 128:384].rearrange("p (c n d) -> p c n d", c=NCH, n=2)
            SUM_PARTS, PICK = high_r[:, 1, T:2 * T], high_r[:, 1, 0:32]
            with phase("summed", "totalled", "kept", "doubled", "turned", "picked", "zeroed", "high_done", "low_done", "rest",
                       "into_done", "over_done", "outof_done") as \
                    (block, summed, totalled, kept, doubled, turned, picked, zeroed, high_done, low_done, rest,
                     into_done, over_done, outof_done):
                @block.tensor
                def _(pe):
                    for c in range(NCH):
                        for back in range(2):
                            d = slice(c * 32 + back * 16, c * 32 + back * 16 + 16)
                            mm = nc.tensor.matmul(psum[:, 0, d], con("ge") if back else con("le"), U[:, d], start=True, stop=True)
                    mm.then_inc(summed, 1)
                    nc.tensor.matmul(psum[:, 2, 0:128], con("ones"), U, start=True, stop=True).then_inc(totalled, 1)
                    pe.wait_ge(doubled, 2)
                    for c in range(NCH):
                        tr = nc.tensor.transpose(psum[0:64, 1, c * P:(c + 1) * P],
                                                 rows[:, 1, 128 + c * 64:192 + c * 64], con("ident"))
                    tr.then_inc(turned, 1)

                @block.vector
                def _(dve):
                    dve.wait_ge(summed, 1)
                    nc.vector.tensor_copy(AC, psum[:, 0, 0:128]).then_inc(kept, 1)
                    for n in range(2):
                        nc.vector.tensor_copy(TWICE[:, :, n, :], psum[:, 0, 0:128].rearrange("p (c d) -> p c d", c=NCH)).then_inc(doubled, 1)
                    nc.vector.tensor_tensor(PICK, con("ident", 32), con("ident", 32, 32), ALU.add).then_inc(picked, 1)
                    dve.wait_ge(totalled, 1)
                    dve.wait_ge(kept, 1)
                    nc.vector.tensor_tensor(TM, psum[:, 2, 0:128], AC, ALU.subtract).then_inc(rest, 1)
                    dve.wait_ge(high_done, 1)
                    nc.vector.tensor_tensor(SUM_PARTS[32:64], psum[32:64, 1, :], SUM_PARTS[32:64].bitcast(F32),
                                            ALU.subtract).then_inc(low_done, 1)

                @block.scalar
                def _(act):
                    nc.scalar.activation(SUM_PARTS[64:P], vec[64:P, 0:T], ACT.Copy, scale=0.0).then_inc(zeroed, 1)
                    act.wait_ge(turned, 1)
                    nc.scalar.activation(SUM_PARTS[0:64], psum[0:64, 1, :], ACT.Copy).then_inc(high_done, 1)
                    act.wait_ge(kept, 1)
                    nc.scalar.activation(INTO, AC, ACT.Exp).then_inc(into_done, 1)
                    act.wait_ge(rest, 1)
                    nc.scalar.activation(OVER, psum[:, 2, 0:128], ACT.Exp).then_inc(over_done, 1)
                    nc.scalar.activation(OUTOF, TM, ACT.Exp).then_inc(outof_done, 1)

        def ssd():
            XN, Z, XS, BT, CT, XT = 0, 20, 28, 36, 40, 44
            OVER, DT, AC, OUTOF = (rows[:, 3, 128 * a:128 * (a + 1)] for a in range(4))
            INTO = rows[:, 1, 0:128]
            SUM_PARTS, PICK = high_r[:, 1, T:2 * T], high_r[:, 1, 0:32]
            xt = span(XT, 8).rearrange("p (c f) -> p c f", c=NCH)
            yt = span(XN, 8).rearrange("p (c f) -> p c f", c=NCH)
            to_tokens(lambda j: arena[:, XS + j, :], KD, xt)

            def dtx(u):
                return span(52, 4)[:, (u % 8) * 256:(u % 8 + 1) * 256].rearrange("p (c f) -> p c f", c=NCH)

            def masked(grp, back):
                return arena[:, 56 + 2 * (grp % 2) + back, :]
            b_tokens, GW = arena[:, 60, :], 4 * HD
            state_after = [arena[:, 61 + k, :] for k in range(3)]

            def tiles_of(coef, d):
                return coef.rearrange("p (c d) -> p c d", c=NCH)[:, :, d:d + 1]

            def heads_of(coef, tile, grp, lo, hi):
                c = coef[:, tile * 32:(tile + 1) * 32].rearrange("p (d h) -> p d h", d=2)
                return c[:, lo:hi, 4 * grp:4 * grp + 4].unsqueeze(3).to_broadcast([P, hi - lo, 4, HD])

            def by_head(x, lo=0, hi=2):
                return x[:, lo * GW:hi * GW].rearrange("p (d h f) -> p d h f", d=hi - lo, h=4)

            def directions(j):
                return (0 if j else 1), (2 if j < 3 else 1)
            UNITS = 32
            with phase("spread_done", "argued", "argued_back", "expd", "weighted", "dtx_done", "source_done", "inside_done", "y_kept",
                       "bc_done", "bc_kept", "b_turned", "b_kept", "state_done", "first_kept", "decayed", "state_kept",
                       "brought", "brought_scaled", "half_added", "added") as \
                    (block, spread_done, argued, argued_back, expd, weighted, dtx_done, source_done, inside_done, y_kept,
                     bc_done, bc_kept, b_turned, b_kept, state_done, first_kept, decayed, state_kept,
                     brought, brought_scaled, half_added, added):
                @block.tensor
                def _(pe):
                    def spread(u):
                        if u >= 2:
                            pe.wait_ge(argued_back if u % 2 else argued, u // 2 * 4)
                        d = u // 2 + 16 * (u % 2)
                        nc.tensor.matmul(psum[:, u % 2, :], PICK[:, d:d + 1].to_broadcast([P, P]), SUM_PARTS,
                                         start=True, stop=True).then_inc(spread_done, 1)

                    def products_bc(grp):
                        if grp:
                            pe.wait_ge(state_kept, 2 * grp)
                        for i in range(NCH):
                            s = slice(i * P, (i + 1) * P)
                            mm = nc.tensor.matmul(psum[:, 4, s], arena[:, BT + grp, s], arena[:, CT + grp, s], start=True, stop=True)
                        mm.then_inc(bc_done, 1)
                        for i in range(NCH):
                            s = slice(i * P, (i + 1) * P)
                            tr = nc.tensor.transpose(psum[:, 5, s], arena[:, BT + grp, s], con("ident"))
                        tr.then_inc(b_turned, 1)

                    def inside(u):
                        h, back = u // 2, u % 2
                        pe.wait_ge(dtx_done, u + 1)
                        pe.wait_ge(weighted, u + 1)
                        if h >= 2 and not back:
                            pe.wait_ge(y_kept, h - 1)
                        for i in range(NCH):
                            mm = nc.tensor.matmul(psum[:, 2 + h % 2, i * HD:(i + 1) * HD], work[:, u % 4, i * P:(i + 1) * P],
                                                  dtx(u)[:, i, :], start=(back == 0 and i == 0), stop=(back == 1 and i == NCH - 1))
                        mm.then_inc(inside_done, 1)

                    def states(grp):
                        pe.wait_ge(source_done, 8 * (grp + 1))
                        pe.wait_ge(b_kept, grp + 1)
                        pe.wait_ge(bc_kept, 2 * (grp + 1))
                        for k in range(3):
                            if k == 2:
                                pe.wait_ge(first_kept, grp + 1)
                            for back, x in ((0, xt), (1, yt)):
                                i = 3 - k if back else k
                                mm = nc.tensor.matmul(psum[:, 4 + k % 2, back * GW:(back + 1) * GW], b_tokens[:, i * P:(i + 1) * P],
                                                      x[:, i, grp * GW:(grp + 1) * GW], start=True, stop=True)
                            mm.then_inc(state_done, 1)

                    def bring(n):
                        grp, j = n // 4, n % 4
                        pe.wait_ge(state_kept, 2 * (grp + 1))
                        if n >= 2:
                            pe.wait_ge(brought_scaled, n - 1)
                        for back in range(*directions(j)):
                            mm = nc.tensor.matmul(psum[:, 6 + n % 2, back * GW:(back + 1) * GW], arena[:, CT + grp, j * P:(j + 1) * P],
                                                  state_after[2 - j if back else j - 1][:, back * GW:(back + 1) * GW],
                                                  start=True, stop=True)
                        mm.then_inc(brought, 1)
                    spread(0)
                    spread(1)
                    products_bc(0)
                    spread(2)
                    for u in range(UNITS):
                        for ahead in (u + 3, u + 4):
                            if u % 2 == 0 and ahead < UNITS:
                                spread(ahead)
                        if u % 8 == 3:
                            states(u // 8)
                        inside(u)
                        if u % 8 == 5 and u + 8 < UNITS:
                            products_bc(u // 8 + 1)
                        if u >= 8 and u % 8 in (0, 1):
                            for n in range(2):
                                bring(4 * (u // 8 - 1) + 2 * (u % 8) + n)
                    for n in range(4):
                        bring(12 + n)

                @block.vector
                def _(dve):
                    def mask(grp):
                        dve.wait_ge(bc_done, grp + 1)
                        for back in range(2):
                            nc.vector.tensor_tensor(by_chunk(masked(grp, back)), by_chunk(psum[:, 4, :]),
                                                    con("ge" if back else "le").unsqueeze(1).to_broadcast([P, NCH, P]),
                                                    ALU.mult).then_inc(bc_kept, 1)

                    def argue(u):
                        dve.wait_ge(spread_done, u + 1)
                        if u >= 4:
                            dve.wait_ge(inside_done, u - 3)
                        for i in range(NCH):
                            s = slice(i * P, (i + 1) * P)
                            d = i * 32 + u // 2
                            nc.vector.tensor_scalar(work[:, u % 4, s], psum[:, 0, s], AC[:, d:d + 1], 0.0,
                                                    ALU.subtract, ALU.min).then_inc(argued, 1)

                    def weigh(u):
                        dve.wait_ge(expd, u + 1)
                        if u % 8 == 0:
                            dve.wait_ge(bc_kept, 2 * (u // 8) + 2)
                        nc.vector.tensor_tensor(work[:, u % 4, :], work[:, u % 4, :], masked(u // 8, u % 2),
                                                ALU.mult).then_inc(weighted, 1)

                    def carry(grp):
                        for k in (1, 2):
                            new, old = state_after[k], state_after[k - 1]
                            if k == 1:
                                dve.wait_ge(first_kept, grp + 1)
                                if grp:
                                    dve.wait_ge(brought, 4 * grp)
                            else:
                                dve.wait_ge(state_kept, 2 * grp + 1)
                            for back in range(2):
                                nc.vector.tensor_tensor(by_head(new, back, back + 1), by_head(old, back, back + 1),
                                                        heads_of(OVER, 3 - k if back else k, grp, back, back + 1),
                                                        ALU.mult).then_inc(decayed, 1)
                            dve.wait_ge(decayed, 4 * grp + 2 * k)
                            dve.wait_ge(state_done, 3 * grp + k + 1)
                            nc.vector.tensor_tensor(new, psum[:, 4 + k % 2, :], new, ALU.add).then_inc(state_kept, 1)

                    def scale(n):
                        grp, j = n // 4, n % 4
                        lo, hi = directions(j)
                        dve.wait_ge(brought, n + 1)
                        if n >= 2:
                            dve.wait_ge(added, n - 1)
                        nc.vector.tensor_tensor(by_head(spare[:, n % 2, :], lo, hi), by_head(psum[:, 6 + n % 2, :], lo, hi),
                                                heads_of(INTO, j, grp, lo, hi), ALU.mult).then_inc(brought_scaled, 1)
                    argue(0)
                    mask(0)
                    for u in range(UNITS):
                        if u + 2 < UNITS and u % 2 == 0:
                            argue(u + 2)
                        weigh(u)
                        if u % 8 == 3:
                            carry(u // 8)
                        if u % 8 == 6 and u + 8 < UNITS:
                            mask(u // 8 + 1)
                        if u >= 8 and u % 8 in (1, 2):
                            for n in range(2):
                                scale(4 * (u // 8 - 1) + 2 * (u % 8 - 1) + n)
                    for n in range(4):
                        scale(12 + n)

                @block.scalar
                def _(act):
                    def keep_b(grp):
                        act.wait_ge(b_turned, grp + 1)
                        if grp:
                            act.wait_ge(state_done, 3 * grp)
                        nc.scalar.activation(b_tokens, psum[:, 5, :], ACT.Copy).then_inc(b_kept, 1)

                    def keep(h):
                        act.wait_ge(inside_done, 2 * h + 2)
                        act.wait_ge(state_done, 3 * (h // 4 + 1))
                        nc.scalar.activation(yt[:, :, h * HD:(h + 1) * HD], psum[:, 2 + h % 2, 0:4 * HD]
                                             .rearrange("p (c f) -> p c f", c=NCH), ACT.Copy).then_inc(y_kept, 1)
                    def argue(u):
                        act.wait_ge(spread_done, u + 1)
                        if u >= 4:
                            act.wait_ge(inside_done, u - 3)
                        for i in range(NCH):
                            s = slice(i * P, (i + 1) * P)
                            d = i * 32 + 16 + u // 2
                            nc.scalar.activation(work[:, u % 4, s], psum[:, 1, s], ACT.Relu, bias=AC[:, d:d + 1],
                                                 scale=-1.0).then_inc(argued_back, 1)
                    argue(1)
                    keep_b(0)
                    for u in range(UNITS):
                        act.wait_ge(argued_back if u % 2 else argued, 4 * (u // 2 + 1))
                        nc.scalar.activation(work[:, u % 4, :], work[:, u % 4, :], ACT.Exp,
                                             scale=-1.0 if u % 2 else 1.0).then_inc(expd, 1)
                        if u % 2 and u + 2 < UNITS:
                            argue(u + 2)
                        if u % 8 == 3:
                            act.wait_ge(state_done, 3 * (u // 8) + 1)
                            if u > 8:
                                act.wait_ge(brought, 4 * (u // 8))
                            nc.scalar.activation(state_after[0], psum[:, 4, :], ACT.Copy).then_inc(first_kept, 1)
                        if u % 8 == 7 and u + 8 < UNITS:
                            keep_b(u // 8 + 1)
                        if u % 2 and u >= 3:
                            keep(u // 2 - 1)
                    keep(15)

                @block.gpsimd
                def _(pool):
                    def source(u, x):
                        return x[:, :, (u // 2) * HD:(u // 2 + 1) * HD]

                    def add(n):
                        grp, j = n // 4, n % 4
                        pool.wait_ge(brought_scaled, n + 1)
                        pool.wait_ge(y_kept, 4 * (grp + 1))
                        y = yt[:, j, grp * GW:(grp + 1) * GW]
                        lo, hi = directions(j)
                        for back in range(lo, hi):
                            if back and not lo:
                                pool.wait_ge(half_added, sum(directions(m % 4) == (0, 2) for m in range(n + 1)))
                            nc.gpsimd.tensor_tensor(y, y, spare[:, n % 2, back * GW:(back + 1) * GW],
                                                    ALU.add).then_inc(half_added if back == 0 and hi == 2 else added, 1)
                    for h in range(UNITS // 2):
                        for u in (2 * h, 2 * h + 1):
                            if u >= 8:
                                pool.wait_ge(inside_done, u - 7)
                            if u >= 8 and u % 8 == 0:
                                pool.wait_ge(state_done, 3 * (u // 8))
                            nc.gpsimd.tensor_tensor(dtx(u), source(u, xt), tiles_of(DT, h + 16 * (u % 2)).to_broadcast([P, NCH, HD]),
                                                    ALU.mult).then_inc(dtx_done, 1)
                        for u in (2 * h, 2 * h + 1):
                            pool.wait_ge(dtx_done, 2 * h + 2)
                            nc.gpsimd.tensor_tensor(source(u, yt if u % 2 else xt), dtx(u),
                                                    tiles_of(OUTOF, h + 16 * (u % 2)).to_broadcast([P, NCH, HD]),
                                                    ALU.mult).then_inc(source_done, 1)
                        if h % 4 == 3 and h > 4:
                            for n in range(4):
                                add(4 * (h // 4 - 1) + n)
                    for n in range(4):
                        add(12 + n)
            def take(eng, j, bank):
                x = arena[:, XS + j, :]
                return nc.vector.scalar_tensor_tensor(out=x, in0=x, scalar=col("ssd_D", j), in1=bank, op0=ALU.mult, op1=ALU.add)
            transposes(KD, lambda j, b: yt[:, b, j * P:(j + 1) * P], take, engines=("vector",))
            with phase("gated") as (block, gated):
                @block.vector
                def _(dve):
                    nc.vector.tensor_tensor(span(XS, 8), span(XS, 8), span(Z, 8), ALU.mult).then_inc(gated, 1)
            norm(lambda i: arena[:, XS + i, :], None, KD,
                 lambda i: con("group_rows", P, 3 - i // 2), lambda i: con("ident", 1, i // 2).to_broadcast([P, P]),
                 lambda i: col("ssd_g", i), 1.0 / 256, 1e-6, ALU.add, parts=two_parts(XN, XS))

        def neighbourhood():
            Q, K, V, KP, VT, OT = 8, 12, 16, 20, 48, 44
            norm(lambda i: arena[:, Q + i, :], lambda i: arena[:, Q + i, :], 8, head_sums, head_spread,
                 lambda i: col("na_qk", i), 1.0 / HD, 1e-6, ALU.add)
            key_halves([(h % 2, K + h // 2) for h in range(8)], KP)
            vt = span(VT, 4).rearrange("p (c f) -> p c f", c=NCH)
            to_tokens(lambda j: arena[:, V + j, :], 4, vt)
            ot = span(OT, 4).rearrange("p (c f) -> p c f", c=NCH)
            win = [span(52, 2)[:, 0:14 * 64], span(54, 2)[:, 0:14 * 64]]
            units = []
            for h in range(8):
                for qt in range(4):
                    units.append((arena[:, Q + h // 2, qt * P:(qt + 1) * P], arena[:, KP + h, :],
                                  lambda b, h=h: vt[:, b, h * HD:(h + 1) * HD], ot[:, qt, h * HD:(h + 1) * HD]))

            def bias(u):
                lo = (6 - 2 * (u % 4)) * 64
                return win[(u // 4) % 2][:, lo:lo + T]

            def before(block, bias_ready, bias_loaded, biased):
                @block.sync
                def _(sp):
                    for h in range(8):
                        if h >= 2:
                            sp.wait_ge(biased, 4 * (h - 1))
                        if h >= 1:
                            sp.wait_ge(bias_loaded, 32 * h)
                        w = win[h % 2].rearrange("p (d k) -> p d k", k=64)
                        for rr in range(2):
                            sp.dma_start(w[rr * 64:(rr + 1) * 64, :, :],
                                         dram["na_bias"][h, 1 - rr:15 - rr, :, :].rearrange("d c k -> c d k"))\
                                .then_inc(bias_loaded, 16)

                @block.gpsimd
                def _(pool):
                    for h in range(8):
                        pool.wait_ge(bias_loaded, 32 * (h + 1))
                        w = win[h % 2].rearrange("p (d k) -> p d k", k=64)
                        nc.gpsimd.tensor_tensor(w, w, con("window", 64).unsqueeze(1).to_broadcast([P, 14, 64]),
                                                ALU.add).then_inc(bias_ready, 1)
            attention(units, [arena[:, 56, :], arena[:, 57, :]], [arena[:, 58 + i, :] for i in range(3)],
                      [arena[:, 61, :], arena[:, 62, :]], bias, before)
            transposes(4, lambda j, b: ot[:, b, j * P:(j + 1) * P],
                       lambda eng, j, bank: copy_on(eng, arena[:, Q + j, :], bank))
            split_tiles(4, lambda i: arena[:, Q + i, :], two_parts(K, Q, 4))

        def gqa():
            XN, Q, K, V, COS, SIN, VT, OT = 0, 8, 16, 18, 20, 21, 22, 24
            inputs = rms_norm(lambda i: resid[:, i, :], None, KD, lambda i: col("odd_g", i), parts=two_parts(XN, OT),
                              squares_ready=True)
            with phase("taken", "rope_loaded") as (block, taken, rope_loaded):
                @block.sync
                def _(sp):
                    sp.dma_start(span(COS, 2), dram["rope"]).then_inc(rope_loaded, 16)
                    load_stream(sp, "qkv")
                    sp.wait_ge(rope_loaded, 16)

                @block.tensor
                def _(pe):
                    products(pe, "qkv", two_parts(XN, OT), taken, inputs)

                @block.scalar
                def _(act):
                    def read(g, m, done):
                        done()
                        nc.scalar.activation(tile_of(arena, g * R + (m + Q)), psum[:, m, :], ACT.Copy).then_inc(taken, 1)
                    split_and_read(act, "qkv", split_high, read, inputs=inputs)

                @block.vector
                def _(dve):
                    split_and_read(dve, "qkv", split_low, inputs=inputs)
            norm(lambda i: arena[:, Q + i, :], lambda i: arena[:, Q + i, :], 10, head_sums, head_spread,
                 lambda i: col("gqa_qk", i), 1.0 / HD, 1e-6, ALU.add)
            with phase("rotated", "sin_done", "cos_done", "roped") as (block, rotated, sin_done, cos_done, roped):
                @block.tensor
                def _(pe):
                    for i in range(10):
                        if i >= 4:
                            pe.wait_ge(sin_done, i - 3)
                        nc.tensor.matmul(psum[:, i % 4, :], con("rot"), arena[:, Q + i, :], start=True, stop=True).then_inc(rotated, 1)

                @block.vector
                def _(dve):
                    for i in range(10):
                        dve.wait_ge(rotated, i + 1)
                        if i >= 4:
                            dve.wait_ge(roped, i - 3)
                        x = arena[:, Q + i, :]
                        nc.vector.tensor_tensor(work[:, i % 4, :], psum[:, i % 4, :], arena[:, SIN, :], ALU.mult).then_inc(sin_done, 1)
                        nc.vector.tensor_tensor(x, x, arena[:, COS, :], ALU.mult).then_inc(cos_done, 1)
                        dve.wait_ge(sin_done, i + 1)
                        dve.wait_ge(cos_done, i + 1)
                        nc.vector.tensor_tensor(x, x, work[:, i % 4, :], ALU.add).then_inc(roped, 1)
            key_halves([(kv % 2, K + kv // 2) for kv in range(4)], 40)
            vt = span(VT, 2).rearrange("p (c f) -> p c f", c=NCH)
            to_tokens(lambda j: arena[:, V + j, :], 2, vt)
            ot = span(OT, 8).rearrange("p (c f) -> p c f", c=NCH)
            units = []
            for n in range(NH):
                j, e = n // 2, n % 2
                h = (j if j < 4 else j + 4) + 4 * e
                kv = h // 4
                for qt in range(4):
                    units.append((arena[:, Q + j, qt * P:(qt + 1) * P], arena[:, 40 + kv, :],
                                  lambda b, kv=kv: vt[:, b, kv * HD:(kv + 1) * HD], ot[:, qt, h * HD:(h + 1) * HD]))
            attention(units, None, [arena[:, 32 + i, :] for i in range(3)], [arena[:, 35, :], arena[:, 36, :]], None, None)
            transposes(KD, lambda j, b: ot[:, b, j * P:(j + 1) * P],
                       lambda eng, j, bank: copy_on(eng, arena[:, Q + j, :], bank))
            parts = two_parts(XN, Q)
            add_projection("odd_out", parts, Inputs(KD, lambda i: arena[:, Q + i, :], parts))

        def final_norm():
            rms_norm(lambda i: resid[:, i, :], lambda i: resid[:, i, :], KD, lambda i: col("final_g", i), squares_ready=True)

        def even():
            even_in()
            ssd()
            neighbourhood()
            add_projection("even_out", lambda k: two_parts(12, 8, 4)(k) if k < 4 else two_parts(0, 28)(k - 4))

        sgu()
        conv_ffn(0)
        rwkv()
        conv_ffn(1)
        final_norm()
        even()
        swiglu(0)
        gqa()
        swiglu(1)
        with phase("stored") as (block, stored):
            @block.sync
            def _(sp):
                sp.dma_start(out, resid[:, :, :]).then_inc(stored, 16)
                sp.wait_ge(stored, 16)


def constants():
    i = np.arange(P)
    p, f = i[:, None], i[None, :]
    levels = []
    for b in (1, 2, 4, 8, 16, 32, 64):
        levels.append(((f // b) % 2 == 1) & (p // b == f // b - 1))
    rot = np.zeros((P, P), np.float32)
    even = np.arange(0, P, 2)
    rot[even + 1, even] = -1.0
    rot[even, even + 1] = 1.0
    c = np.arange(HD)
    start = np.clip(c - 8, 0, HD - 16)
    inside = (c[None, :] >= start[:, None]) & (c[None, :] < start[:, None] + 16)
    window = np.where(np.concatenate([inside, inside]), 0.0, -1e30)
    head_rows = np.zeros((P, 160), np.float32)
    head_rows[i, 30 + i // HD] = 1.0
    head_cols = np.zeros((P, 10, P), np.float32)
    for t in range(10):
        for e in range(2):
            head_cols[2 * t + e, t, e * HD:(e + 1) * HD] = 1.0
    halves = np.zeros((P, 2), np.float32)
    halves[i, i // HD] = 1.0
    group_rows = np.zeros((P, 132), np.float32)
    group_rows[:, 3] = 1.0
    parts = dict(ident=np.eye(P), le=p <= f, lt=p < f, ge=p >= f, levels=np.concatenate(levels, 1),
                 pair_low=levels[0].T, ones=np.ones((P, P)), rot=rot, window=window, head_rows=head_rows,
                 head_cols=head_cols.reshape(P, -1), halves=halves, group_rows=group_rows)
    return np.concatenate([np.asarray(parts[n], np.float32) for n, _ in CONST_PARTS], 1)


def rope_tables():
    t = np.arange(T)
    freqs = (10000.0 ** (-np.arange(0, 32, 2, dtype=np.float32) / np.float32(32))).astype(np.float32)
    ang = np.concatenate([(t // 64).astype(np.float32)[:, None] * freqs, (t % 64).astype(np.float32)[:, None] * freqs], 1)
    def table(x):
        x = np.repeat(x.T, 2, axis=0).astype(np.float32)
        return np.concatenate([x, x], 0)
    return np.concatenate([table(np.cos(ang)), table(np.sin(ang))], 1)


def layouts(a):
    def blocks(w, order=None):
        k, m = w.shape
        w = w.reshape(k // P, P, m // P, P).transpose(2, 1, 0, 3)
        if order is not None:
            w = w[order]
        return np.ascontiguousarray(w.reshape(m // P, P, k))

    def cols(v):
        return v.reshape(-1, P).T

    def turns(n):
        return np.stack([np.arange(n), np.arange(n) + n], 1).reshape(-1)

    d = {}
    d["x"] = np.ascontiguousarray(a["x"][0].T.reshape(KD, P, T).transpose(1, 0, 2))
    d["const"] = constants()
    d["rope"] = rope_tables()
    pair = turns(KF)
    d["sgu_in"] = blocks(a["sgu_w_in"][0])
    d["sgu_out"] = blocks(a["sgu_w_out"][0])
    d["sgu_ws"] = np.ascontiguousarray(a["sgu_w_s"][0].transpose(2, 0, 1).reshape(P, -1))
    for l in range(2):
        d[f"up{l}"] = blocks(a["ffn_w_up"][l], order=pair)
        d[f"down{l}"] = blocks(a["ffn_w_down"][l])
        d[f"up{l + 2}"] = blocks(a["ffn_w13_2"][l], order=pair)
        d[f"down{l + 2}"] = blocks(a["ffn_w2_2"][l])
    for n in "rkvo":
        d[f"rwkv_{n}"] = blocks(a[f"rwkv_w_{n}"][0])
    lora1 = np.concatenate([a["rwkv_w1"][0], a["rwkv_a1"][0], a["rwkv_g1"][0]], 1)
    d["lora1"] = np.ascontiguousarray(lora1.reshape(KD, P, 288).transpose(1, 0, 2).reshape(P, -1))
    d["lora_w2"] = a["rwkv_w2"][0]
    d["lora_a2"] = a["rwkv_a2"][0]
    d["lora_g2"] = a["rwkv_g2"][0]
    even = a["even_w_in_2"][0]
    d["even_in"] = blocks(np.ascontiguousarray(even[:, :4608]))
    d["even_dt"] = np.ascontiguousarray(even[:, 4608:].reshape(KD, P, 32).transpose(1, 0, 2).reshape(P, -1))
    d["even_out"] = blocks(a["even_w_out_2"][0])
    heads = [(j if j < 4 else j + 4) + 4 * e for j in range(8) for e in range(2)]
    qcols = np.concatenate([np.arange(h * HD, (h + 1) * HD) for h in heads] + [np.arange(1024, 1536)])
    d["qkv"] = blocks(a["odd_w_qkv_2"][0][:, qcols])
    d["odd_out"] = blocks(a["odd_w_out_2"][0])
    rpb = np.pad(a["na_rel_bias_2"][0], ((0, 0), (0, 0), (48, 48)))
    c = np.arange(HD)
    d["na_bias"] = np.ascontiguousarray(rpb[:, :, 63 + c[None, :] - c[:, None]])
    spread = lambda v: np.broadcast_to(v, (P, v.size))
    twice = lambda v: np.concatenate([v, v])[:, None]
    vectors = dict(
        mix_g=cols(a["norm_mix_g"]), ffn_g=cols(a["norm_ffn_g"]), final_g=cols(a["norm_final_g"]),
        sgu_b=cols(a["sgu_b_in"]), sgu_gv=cols(a["sgu_g_v"]), sgu_bs=a["sgu_b_s"][0].T, mu=cols(a["rwkv_mu"]),
        w0=cols(a["rwkv_w0"]), a0=cols(a["rwkv_a0"]), k_k=cols(a["rwkv_k_k"]), k_a=cols(a["rwkv_k_a"]),
        r_k=cols(a["rwkv_r_k"]), ln_w=cols(a["rwkv_ln_w"]), ln_b=cols(a["rwkv_ln_b"]),
        conv_w=np.concatenate([cols(a["ffn_conv_w"][l, j])[:, pair] for l in range(2) for j in range(3)], 1),
        conv_b=np.concatenate([cols(a["ffn_conv_b"][l])[:, pair] for l in range(2)], 1),
        even_g=cols(a["even_mix_norm_2"]), ssd_cw=cols(a["ssd_conv_w_2"]), ssd_cb=cols(a["ssd_conv_b_2"]),
        ssd_D=cols(np.repeat(a["ssd_D_2"][0], HD)), ssd_g=cols(a["ssd_out_norm_2"]),
        dt_bias=spread(a["ssd_dt_bias_2"].reshape(-1)), A_log=spread(a["ssd_A_log_2"].reshape(-1)),
        na_qk=np.concatenate([twice(a["na_q_norm_2"][0])] * 4 + [twice(a["na_k_norm_2"][0])] * 4, 1),
        odd_g=cols(a["odd_mix_norm_2"]),
        gqa_qk=np.concatenate([twice(a["gqa_q_norm_2"][0])] * 8 + [twice(a["gqa_k_norm_2"][0])] * 2, 1),
        ffn2_g=cols(a["ffn_norm_2"]))
    d["vec"] = np.ascontiguousarray(np.concatenate([vectors[n] for n, _ in VECTOR_PARTS], 1))
    return d


def kernel(**inputs):
    import concourse.bacc as bacc
    from concourse.bass_utils import run_bass_kernel_spmd

    arrays = layouts({k: np.asarray(v) for k, v in inputs.items()})
    nc = bacc.Bacc("TRN2", target_bir_lowering=False, num_devices=1)
    dram = {k: nc.dram_tensor(f"in_{k}", v.shape, F32, kind="ExternalInput").ap() for k, v in arrays.items()}
    out = nc.dram_tensor("out", (P, KD, T), F32, kind="ExternalOutput").ap()
    build(nc, dram, out)
    result = run_bass_kernel_spmd(nc, [{f"in_{k}": v for k, v in arrays.items()}], core_ids=[0])
    y = result.results[0]["out"]
    return np.ascontiguousarray(y.transpose(1, 0, 2).reshape(D, T).T)[None]
```
